# Optimizing a Trainium2 kernel written in Bass

```python
import jax, jax.numpy as jnp
from jax import lax
import numpy as np
import math

D_MODEL = 1024
BATCH = 1
SEQ = 256
DEPTH = 2

N_META = 16
ATT_BLOCK = 128
ATT_HEADS = 16
ATT_HEAD_DIM = 64
DN_HEADS = 8
DN_HEAD_DIM = 128
DN_CONV = 4
DN_CHUNK = 64
FFN_DIM = 2816
FFN_CONV = 3
N_ATTN_LAYERS = (DEPTH + 1) // 2
N_DN_LAYERS = DEPTH // 2
ATT_HD = ATT_HEADS * ATT_HEAD_DIM
DN_HD = DN_HEADS * DN_HEAD_DIM
ATT_IN = 4 * ATT_HD + ATT_HEADS
DN_IN = 4 * DN_HD + 2 * DN_HEADS
EPS = 1e-6
NEG = -1e30


def rmsnorm(x, g):
    xf = x.astype(jnp.float32)
    y = xf * lax.rsqrt(jnp.mean(xf * xf, axis=-1, keepdims=True) + EPS)
    return (y * g.astype(jnp.float32)).astype(x.dtype)

def l2norm(x):
    xf = x.astype(jnp.float32)
    return xf * lax.rsqrt(jnp.sum(xf * xf, axis=-1, keepdims=True) + EPS)

def causal_dwconv(x, w):
    K, C = w.shape
    return lax.conv_general_dilated(
        x, w[:, None, :].astype(x.dtype), window_strides=(1,), padding=[(K - 1, 0)],
        dimension_numbers=('NWC', 'WIO', 'NWC'), feature_group_count=C)

def forgetting_attention(h, w_in, b_forget, q_gain, k_gain, w_out):
    B, L, _ = h.shape
    pad = (-L) % ATT_BLOCK
    hp = jnp.pad(h, ((0, 0), (pad, 0), (0, 0)))
    Lp = L + pad
    proj = hp @ w_in
    q, k, v, og, fl = jnp.split(proj, [ATT_HD, 2 * ATT_HD, 3 * ATT_HD, 4 * ATT_HD], axis=-1)
    q = rmsnorm(q.reshape(B, Lp, ATT_HEADS, ATT_HEAD_DIM), q_gain).transpose(0, 2, 1, 3)
    k = rmsnorm(k.reshape(B, Lp, ATT_HEADS, ATT_HEAD_DIM), k_gain).transpose(0, 2, 1, 3)
    v = v.reshape(B, Lp, ATT_HEADS, ATT_HEAD_DIM).transpose(0, 2, 1, 3)
    logf = jax.nn.log_sigmoid(fl.astype(jnp.float32) + b_forget.astype(jnp.float32))
    c = jnp.cumsum(logf, axis=1).transpose(0, 2, 1)
    pos = jnp.arange(Lp)
    n_blk = Lp // ATT_BLOCK
    qb = q.reshape(B, ATT_HEADS, n_blk, ATT_BLOCK, ATT_HEAD_DIM).transpose(2, 0, 1, 3, 4)
    cb = c.reshape(B, ATT_HEADS, n_blk, ATT_BLOCK).transpose(2, 0, 1, 3)
    pb = pos.reshape(n_blk, ATT_BLOCK)
    scale = ATT_HEAD_DIM ** -0.5

    def one_block(args):
        q_i, c_i, p_i = args
        s = jnp.einsum('bhqd,bhkd->bhqk', q_i, k).astype(jnp.float32) * scale
        s = s + c_i[..., :, None] - c[:, :, None, :]
        mask = (pos[None, :] <= p_i[:, None]) & (pos[None, :] >= pad)
        p = jax.nn.softmax(jnp.where(mask, s, NEG), axis=-1)
        return jnp.einsum('bhqk,bhkd->bhqd', p.astype(v.dtype), v)

    o = lax.map(one_block, (qb, cb, pb))
    o = o.transpose(1, 0, 3, 2, 4).reshape(B, Lp, ATT_HD)
    o = o * jax.nn.sigmoid(og)
    return (o @ w_out)[:, pad:]

def gated_deltanet(h, w_in, conv_w, a_log, dt_bias, o_gain, w_out):
    B, L, _ = h.shape
    H, Dh, C = DN_HEADS, DN_HEAD_DIM, DN_CHUNK
    pad = (-L) % C
    hp = jnp.pad(h, ((0, 0), (pad, 0), (0, 0)))
    Lp = L + pad
    N = Lp // C
    proj = hp @ w_in
    qkv, og, b_logit, a_logit = jnp.split(proj, [3 * DN_HD, 4 * DN_HD, 4 * DN_HD + H], axis=-1)
    qkv = jax.nn.silu(causal_dwconv(qkv, conv_w))
    q, k, v = jnp.split(qkv, [DN_HD, 2 * DN_HD], axis=-1)
    q = l2norm(q.reshape(B, Lp, H, Dh)) * (Dh ** -0.5)
    k = l2norm(k.reshape(B, Lp, H, Dh))
    v = v.reshape(B, Lp, H, Dh).astype(jnp.float32)
    beta = jax.nn.sigmoid(b_logit.astype(jnp.float32))
    g = -jnp.exp(a_log.astype(jnp.float32)) * jax.nn.softplus(
        a_logit.astype(jnp.float32) + dt_bias.astype(jnp.float32))

    def chunk(t):
        return t.reshape(B, N, C, H, Dh).transpose(0, 3, 1, 2, 4)
    qc, kc, vc = chunk(q), chunk(k), chunk(v)
    bc = beta.reshape(B, N, C, H).transpose(0, 3, 1, 2)
    gc = jnp.cumsum(g.reshape(B, N, C, H).transpose(0, 3, 1, 2), axis=-1)
    idx = jnp.arange(C)
    strict = idx[:, None] > idx[None, :]
    incl = idx[:, None] >= idx[None, :]
    dec = jnp.exp(jnp.where(incl, gc[..., :, None] - gc[..., None, :], -jnp.inf))
    kk = jnp.einsum('bhnid,bhnjd->bhnij', kc, kc)
    A = jnp.where(strict, kk * dec * bc[..., :, None], 0.0)
    lhs = A + jnp.eye(C, dtype=jnp.float32)
    rhs = jnp.concatenate([kc * (bc * jnp.exp(gc))[..., None], vc * bc[..., None]], axis=-1)
    sol = lax.linalg.triangular_solve(lhs, rhs, left_side=True, lower=True, unit_diagonal=True)
    W, U0 = sol[..., :Dh], sol[..., Dh:]
    qk = jnp.einsum('bhnid,bhnjd->bhnij', qc, kc) * dec
    q_dec = qc * jnp.exp(gc)[..., None]
    k_dec = kc * jnp.exp(gc[..., -1:] - gc)[..., None]
    g_last = jnp.exp(gc[..., -1])

    def to_n(t):
        return jnp.moveaxis(t, 2, 0)

    def step(S, xs):
        W_n, U0_n, qk_n, qd_n, kd_n, gl_n = xs
        U = U0_n - jnp.einsum('bhcd,bhvd->bhcv', W_n, S)
        O = jnp.einsum('bhcd,bhvd->bhcv', qd_n, S) + jnp.einsum('bhij,bhjv->bhiv', qk_n, U)
        S = gl_n[..., None, None] * S + jnp.einsum('bhcv,bhcd->bhvd', U, kd_n)
        return S, O

    S0 = jnp.zeros((B, H, Dh, Dh), jnp.float32)
    _, O = lax.scan(step, S0, (to_n(W), to_n(U0), to_n(qk), to_n(q_dec), to_n(k_dec), to_n(g_last)))
    O = O.transpose(1, 0, 3, 2, 4).reshape(B, Lp, H, Dh)
    O = rmsnorm(O, o_gain) * jax.nn.silu(og.reshape(B, Lp, H, Dh).astype(jnp.float32))
    return (O.reshape(B, Lp, DN_HD).astype(h.dtype) @ w_out)[:, pad:]

def conv_ffn(h, w_up, conv_w, w_down):
    u = causal_dwconv(h @ w_up, conv_w)
    gate, up = jnp.split(u, [FFN_DIM], axis=-1)
    return (jax.nn.gelu(gate, approximate=True) * up) @ w_down

def first_inputs(seed: int = 0) -> dict:
    key = jax.random.key(seed)
    ks = jax.random.split(key, 24)
    D = D_MODEL
    nrm = lambda k, shape, s: jax.random.normal(k, shape, jnp.float32) * s
    gain = lambda k, shape: 1.0 + 0.1 * jax.random.normal(k, shape, jnp.float32)
    dt = jnp.exp(jax.random.uniform(ks[12], (N_DN_LAYERS, DN_HEADS), jnp.float32,
                                    np.log(1e-3), np.log(1e-1)))
    return {
        "x": nrm(ks[0], (BATCH, SEQ, D), 1.0),
        "meta_tokens": nrm(ks[1], (N_META, D), 1.0),
        "norm_mix_pre": gain(ks[2], (DEPTH, D)),
        "norm_mix_post": gain(ks[3], (DEPTH, D)),
        "norm_ffn_pre": gain(ks[4], (DEPTH, D)),
        "norm_ffn_post": gain(ks[5], (DEPTH, D)),
        "attn_w_in": nrm(ks[6], (N_ATTN_LAYERS, D, ATT_IN), D ** -0.5),
        "attn_b_forget": jax.random.uniform(ks[7], (N_ATTN_LAYERS, ATT_HEADS), jnp.float32, 2.0, 6.0),
        "attn_q_norm": gain(ks[8], (N_ATTN_LAYERS, ATT_HEAD_DIM)),
        "attn_k_norm": gain(ks[9], (N_ATTN_LAYERS, ATT_HEAD_DIM)),
        "attn_w_out": nrm(ks[10], (N_ATTN_LAYERS, ATT_HD, D), ATT_HD ** -0.5),
        "dn_w_in": nrm(ks[11], (N_DN_LAYERS, D, DN_IN), D ** -0.5),
        "dn_conv": nrm(ks[13], (N_DN_LAYERS, DN_CONV, 3 * DN_HD), DN_CONV ** -0.5),
        "dn_a_log": jnp.log(jax.random.uniform(ks[14], (N_DN_LAYERS, DN_HEADS), jnp.float32, 1.0, 16.0)),
        "dn_dt_bias": dt + jnp.log(-jnp.expm1(-dt)),
        "dn_o_norm": gain(ks[15], (N_DN_LAYERS, DN_HEAD_DIM)),
        "dn_w_out": nrm(ks[16], (N_DN_LAYERS, DN_HD, D), DN_HD ** -0.5),
        "ffn_w_up": nrm(ks[17], (DEPTH, D, 2 * FFN_DIM), D ** -0.5),
        "ffn_conv": nrm(ks[18], (DEPTH, FFN_CONV, 2 * FFN_DIM), FFN_CONV ** -0.5),
        "ffn_w_down": nrm(ks[19], (DEPTH, FFN_DIM, D), FFN_DIM ** -0.5),
    }

def first_block(x, meta_tokens, norm_mix_pre, norm_mix_post, norm_ffn_pre, norm_ffn_post,
              attn_w_in, attn_b_forget, attn_q_norm, attn_k_norm, attn_w_out,
              dn_w_in, dn_conv, dn_a_log, dn_dt_bias, dn_o_norm, dn_w_out,
              ffn_w_up, ffn_conv, ffn_w_down):
    B = x.shape[0]
    meta = jnp.broadcast_to(meta_tokens[None].astype(x.dtype), (B, N_META, x.shape[-1]))
    h = jnp.concatenate([meta, x], axis=1)
    for i in range(DEPTH):
        j = i // 2
        a = rmsnorm(h, norm_mix_pre[i])
        if i % 2 == 0:
            m = forgetting_attention(a, attn_w_in[j], attn_b_forget[j], attn_q_norm[j],
                                     attn_k_norm[j], attn_w_out[j])
        else:
            m = gated_deltanet(a, dn_w_in[j], dn_conv[j], dn_a_log[j], dn_dt_bias[j],
                               dn_o_norm[j], dn_w_out[j])
        h = h + rmsnorm(m, norm_mix_post[i])
        f = conv_ffn(rmsnorm(h, norm_ffn_pre[i]), ffn_w_up[i], ffn_conv[i], ffn_w_down[i])
        h = h + rmsnorm(f, norm_ffn_post[i])
    return h[:, N_META:]


N_A = DEPTH // 2
N_B = DEPTH - N_A

H_A = 16
NOPE_A = 64
ROPE_A = 32
V_A = 64
Q_LORA = 768
KV_LORA = 256
WIDTH_A = H_A * V_A
QBLOCK = 128

H_B = 16
HD_B = 64
WIDTH_B = H_B * HD_B
MOBA_BLOCK = 256
MOBA_TOPK = 3
QCHUNK = 8

THETA = 10000.0
LN_EPS = 1e-5
RMS_EPS = 1e-6
ALPHA = (2 * DEPTH) ** 0.25
BETA = (8 * DEPTH) ** (-0.25)


def rope_tables(seq, dim):
    inv = THETA ** (-jnp.arange(0, dim, 2, dtype=jnp.float32) / dim)
    ang = jnp.arange(seq, dtype=jnp.float32)[:, None] * inv[None, :]
    ang = jnp.concatenate([ang, ang], axis=-1)
    return jnp.cos(ang), jnp.sin(ang)

def apply_rope(x, cos, sin):
    x1, x2 = jnp.split(x, 2, axis=-1)
    rot = jnp.concatenate([-x2, x1], axis=-1)
    return (x * cos + rot * sin).astype(x.dtype)

def layer_norm(x, g, b):
    xf = x.astype(jnp.float32)
    mu = jnp.mean(xf, axis=-1, keepdims=True)
    var = jnp.mean(jnp.square(xf - mu), axis=-1, keepdims=True)
    return ((xf - mu) * lax.rsqrt(var + LN_EPS) * g + b).astype(x.dtype)

def rms_norm(x, g):
    xf = x.astype(jnp.float32)
    return (xf * lax.rsqrt(jnp.mean(jnp.square(xf), axis=-1, keepdims=True) + RMS_EPS) * g).astype(x.dtype)

def mla_mixer(x, w_in, q_norm, kv_norm, w_uq, w_ukv, w_o, cos, sin):
    B, S, _ = x.shape
    h = x @ w_in
    c_q, c_kv, k_rope, gate = jnp.split(h, [Q_LORA, Q_LORA + KV_LORA, Q_LORA + KV_LORA + ROPE_A], axis=-1)
    q = (rms_norm(c_q, q_norm) @ w_uq).reshape(B, S, H_A, NOPE_A + ROPE_A)
    q_nope = q[..., :NOPE_A]
    q_rope = apply_rope(q[..., NOPE_A:], cos[None, :, None, :], sin[None, :, None, :])
    kv = (rms_norm(c_kv, kv_norm) @ w_ukv).reshape(B, S, H_A, NOPE_A + V_A)
    k_nope, v = kv[..., :NOPE_A], kv[..., NOPE_A:]
    k_rope = apply_rope(k_rope, cos[None], sin[None])
    scale = (NOPE_A + ROPE_A) ** -0.5
    outs = []
    for i in range(S // QBLOCK):
        q0, kend = i * QBLOCK, (i + 1) * QBLOCK
        s = (jnp.einsum('bqhd,bkhd->bhqk', q_nope[:, q0:kend], k_nope[:, :kend])
             + jnp.einsum('bqhr,bkr->bhqk', q_rope[:, q0:kend], k_rope[:, :kend])).astype(jnp.float32) * scale
        q_pos = q0 + jnp.arange(QBLOCK)
        mask = jnp.arange(kend)[None, :] <= q_pos[:, None]
        p = jax.nn.softmax(jnp.where(mask, s, -jnp.inf), axis=-1).astype(v.dtype)
        outs.append(jnp.einsum('bhqk,bkhd->bqhd', p, v[:, :kend]))
    o = jnp.concatenate(outs, axis=1).reshape(B, S, WIDTH_A)
    return (o * jax.nn.silu(gate)) @ w_o

def moba_shared_kv(x, w_kv, cos, sin):
    B, S, _ = x.shape
    kv = x @ w_kv
    k = kv[..., :WIDTH_B].reshape(B, S, H_B, HD_B)
    v = kv[..., WIDTH_B:].reshape(B, S, H_B, HD_B)
    k = apply_rope(k, cos[None, :, None, :], sin[None, :, None, :])
    nb = -(-S // MOBA_BLOCK)
    pad = nb * MOBA_BLOCK - S
    k = jnp.pad(k, ((0, 0), (0, pad), (0, 0), (0, 0)))
    v = jnp.pad(v, ((0, 0), (0, pad), (0, 0), (0, 0)))
    k_blocks = k.reshape(B, nb, MOBA_BLOCK, H_B, HD_B).transpose(0, 3, 1, 2, 4)
    v_blocks = v.reshape(B, nb, MOBA_BLOCK, H_B, HD_B).transpose(0, 3, 1, 2, 4)
    cnt = jnp.clip(S - jnp.arange(nb) * MOBA_BLOCK, 1, MOBA_BLOCK).astype(jnp.float32)
    k_mean = (jnp.sum(k_blocks.astype(jnp.float32), axis=3) / cnt[:, None]).astype(k.dtype)
    return k_blocks, v_blocks, k_mean

def moba_mixer(x, k_blocks, v_blocks, k_mean, w_in, w_o, cos, sin):
    B, S, _ = x.shape
    nb = k_blocks.shape[2]
    h = x @ w_in
    q, gate = h[..., :WIDTH_B], h[..., WIDTH_B:]
    q = apply_rope(q.reshape(B, S, H_B, HD_B), cos[None, :, None, :], sin[None, :, None, :])
    q = q.transpose(0, 2, 1, 3)
    gs = jnp.einsum('bhsd,bhnd->bhsn', q, k_mean).astype(jnp.float32)
    q_blk = jnp.arange(S) // MOBA_BLOCK
    past = jnp.arange(nb)[None, :] < q_blk[:, None]
    gs = jnp.where(past, gs, -jnp.inf)
    topk = min(MOBA_TOPK, nb)
    _, idx = lax.top_k(gs, topk)
    valid = idx < q_blk[:, None]
    n_chunks = S // QCHUNK
    q_c = q.reshape(B, H_B, n_chunks, QCHUNK, HD_B).transpose(2, 0, 1, 3, 4)
    idx_c = idx.reshape(B, H_B, n_chunks, QCHUNK, topk).transpose(2, 0, 1, 3, 4)
    valid_c = valid.reshape(B, H_B, n_chunks, QCHUNK, topk).transpose(2, 0, 1, 3, 4)
    starts = jnp.arange(n_chunks, dtype=jnp.int32) * QCHUNK
    b_ix = jnp.arange(B)[:, None, None, None]
    h_ix = jnp.arange(H_B)[None, :, None, None]
    scale = HD_B ** -0.5

    def attend(args):
        qq, ii, vv, start = args
        k_sel = k_blocks[b_ix, h_ix, ii]
        v_sel = v_blocks[b_ix, h_ix, ii]
        qb = start // MOBA_BLOCK
        k_own = lax.dynamic_index_in_dim(k_blocks, qb, axis=2, keepdims=False)
        v_own = lax.dynamic_index_in_dim(v_blocks, qb, axis=2, keepdims=False)
        s_sel = jnp.einsum('bhcd,bhctkd->bhctk', qq, k_sel).astype(jnp.float32) * scale
        s_sel = jnp.where(vv[..., None], s_sel, -jnp.inf).reshape(B, H_B, QCHUNK, topk * MOBA_BLOCK)
        s_own = jnp.einsum('bhcd,bhkd->bhck', qq, k_own).astype(jnp.float32) * scale
        k_pos = qb * MOBA_BLOCK + jnp.arange(MOBA_BLOCK)
        q_pos = start + jnp.arange(QCHUNK)
        s_own = jnp.where(k_pos[None, :] <= q_pos[:, None], s_own, -jnp.inf)
        p = jax.nn.softmax(jnp.concatenate([s_sel, s_own], axis=-1), axis=-1).astype(qq.dtype)
        p_sel = p[..., :topk * MOBA_BLOCK].reshape(B, H_B, QCHUNK, topk, MOBA_BLOCK)
        p_own = p[..., topk * MOBA_BLOCK:]
        return (jnp.einsum('bhctk,bhctkd->bhcd', p_sel, v_sel)
                + jnp.einsum('bhck,bhkd->bhcd', p_own, v_own))

    o = lax.map(attend, (q_c, idx_c, valid_c, starts))
    o = o.transpose(1, 0, 3, 2, 4).reshape(B, S, WIDTH_B)
    return (o * jax.nn.silu(gate)) @ w_o

def second_inputs(seed: int = 0) -> dict:
    key = jax.random.key(seed)
    ks = jax.random.split(key, 14)

    def nrm(k, shape, fan_in, scale=1.0):
        return jax.random.normal(k, shape, jnp.float32) * (scale * fan_in ** -0.5)

    x = jax.random.normal(ks[0], (BATCH, SEQ, D_MODEL), jnp.float32)
    mla_w_in = nrm(ks[1], (N_A, D_MODEL, Q_LORA + KV_LORA + ROPE_A + WIDTH_A), D_MODEL)
    mla_q_norm = 1.0 + 0.02 * jax.random.normal(ks[2], (N_A, Q_LORA), jnp.float32)
    mla_kv_norm = 1.0 + 0.02 * jax.random.normal(ks[3], (N_A, KV_LORA), jnp.float32)
    mla_w_uq = nrm(ks[4], (N_A, Q_LORA, H_A * (NOPE_A + ROPE_A)), Q_LORA)
    mla_w_ukv = nrm(ks[5], (N_A, KV_LORA, H_A * (NOPE_A + V_A)), KV_LORA)
    mla_w_o = nrm(ks[6], (N_A, WIDTH_A, D_MODEL), WIDTH_A, BETA)
    moba_w_kv = nrm(ks[7], (D_MODEL, 2 * WIDTH_B), D_MODEL)
    moba_w_in = nrm(ks[8], (N_B, D_MODEL, 2 * WIDTH_B), D_MODEL)
    moba_w_o = nrm(ks[9], (N_B, WIDTH_B, D_MODEL), WIDTH_B, BETA)
    ln_g = 1.0 + 0.02 * jax.random.normal(ks[10], (DEPTH, D_MODEL), jnp.float32)
    ln_b = 0.02 * jax.random.normal(ks[11], (DEPTH, D_MODEL), jnp.float32)
    return {"x": x, "mla_w_in": mla_w_in, "mla_q_norm": mla_q_norm, "mla_kv_norm": mla_kv_norm,
            "mla_w_uq": mla_w_uq, "mla_w_ukv": mla_w_ukv, "mla_w_o": mla_w_o,
            "moba_w_kv": moba_w_kv, "moba_w_in": moba_w_in, "moba_w_o": moba_w_o,
            "ln_g": ln_g, "ln_b": ln_b}

def second_block(x, mla_w_in, mla_q_norm, mla_kv_norm, mla_w_uq, mla_w_ukv, mla_w_o,
              moba_w_kv, moba_w_in, moba_w_o, ln_g, ln_b):
    S = x.shape[1]
    cos_a, sin_a = rope_tables(S, ROPE_A)
    cos_b, sin_b = rope_tables(S, HD_B)
    shared = None
    for layer in range(DEPTH):
        if layer < N_A:
            y = mla_mixer(x, mla_w_in[layer], mla_q_norm[layer], mla_kv_norm[layer],
                          mla_w_uq[layer], mla_w_ukv[layer], mla_w_o[layer], cos_a, sin_a)
        else:
            if shared is None:
                shared = moba_shared_kv(x, moba_w_kv, cos_b, sin_b)
            j = layer - N_A
            y = moba_mixer(x, shared[0], shared[1], shared[2], moba_w_in[j], moba_w_o[j], cos_b, sin_b)
        x = layer_norm(ALPHA * x + y, ln_g[layer], ln_b[layer])
    return x


def setup_inputs(seed=0):
    out = dict(first_inputs(seed))
    for name, value in second_inputs(seed + 1).items():
        if name != "x":
            out[name + "_2"] = value
    return out


def reference(
    x, meta_tokens, norm_mix_pre, norm_mix_post, norm_ffn_pre, norm_ffn_post, attn_w_in,
    attn_b_forget, attn_q_norm, attn_k_norm, attn_w_out, dn_w_in, dn_conv, dn_a_log, dn_dt_bias,
    dn_o_norm, dn_w_out, ffn_w_up, ffn_conv, ffn_w_down, mla_w_in_2, mla_q_norm_2,
    mla_kv_norm_2, mla_w_uq_2, mla_w_ukv_2, mla_w_o_2, moba_w_kv_2, moba_w_in_2, moba_w_o_2,
    ln_g_2, ln_b_2,
):
    x = first_block(
        x, meta_tokens, norm_mix_pre, norm_mix_post, norm_ffn_pre, norm_ffn_post, attn_w_in,
        attn_b_forget, attn_q_norm, attn_k_norm, attn_w_out, dn_w_in, dn_conv, dn_a_log,
        dn_dt_bias, dn_o_norm, dn_w_out, ffn_w_up, ffn_conv, ffn_w_down,
    )
    return second_block(
        x, mla_w_in_2, mla_q_norm_2, mla_kv_norm_2, mla_w_uq_2, mla_w_ukv_2, mla_w_o_2,
        moba_w_kv_2, moba_w_in_2, moba_w_o_2, ln_g_2, ln_b_2,
    )


_drawn_inputs = setup_inputs


def setup_inputs(seed=0):
    import zlib

    import numpy as np

    out = dict(_drawn_inputs(seed))
    spreads = {}
    factors = {'mla_q_norm_2': 8.0, 'mla_kv_norm_2': 8.0}
    for name, (base, spread) in spreads.items():
        noise = np.random.default_rng([zlib.crc32(name.encode()), seed]).standard_normal(out[name].shape)
        drawn = base * np.exp(spread * noise) if base else spread * noise
        out[name] = __import__('jax').numpy.asarray(drawn.astype(out[name].dtype))
    for name, factor in factors.items():
        out[name] = (out[name] * factor).astype(out[name].dtype)
    return out
```

```python
from contextlib import ExitStack

import numpy as np

import concourse.bass as bass
from concourse import mybir

F32 = mybir.dt.float32
ALU = mybir.AluOpType
ACT = mybir.ActivationFunctionType
AX = mybir.AxisListType.X

P = 128
D = 1024
KT = D // P
META = 16
SEQ = 256
T = META + SEQ
CONV_PAST = 2
FFN = 2816
FT = FFN // P
PAIRS = 8
DNH = 8
C = 96
NC = 3
TP = C * NC
PAD = TP - T
LEVELS = 7
SLOT = 32 * P
NEG = -1e30
ALPHA = 4 ** 0.25
RMS_EPS = 1e-6
LN_EPS = 1e-5
QL, KVL = 6, 2

BLK_A = [(0, META), (META, META + P), (META + P, T)]
BLK_B = [(META, META + P), (META + P, T)]


def tables():
    t = {}
    t["ident"] = np.eye(P)
    t["ones"] = np.ones((P, P))
    t["head_ones"] = np.kron(np.eye(2), np.ones((64, 64)))

    def rot(dim, copies):
        m = np.zeros((dim, dim))
        for d in range(dim // 2):
            m[d + dim // 2, d] = -1.0
            m[d, d + dim // 2] = 1.0
        return np.kron(np.eye(copies), m)

    t["rot64"] = rot(64, 2)
    t["rot32"] = rot(32, 2)

    def angles(dim):
        inv = (np.float32(10000.0) ** (-np.arange(0, dim, 2, dtype=np.float32) / np.float32(dim))).astype(np.float32)
        a = np.arange(SEQ, dtype=np.float32)[:, None] * inv[None, :]
        a = np.concatenate([a, a], -1).T
        return np.concatenate([a, a], 0)

    t["cos64"], t["sin64"] = np.cos(angles(64)), np.sin(angles(64))
    t["cos32"], t["sin32"] = np.cos(angles(32)), np.sin(angles(32))

    def causal(blocks):
        parts = []
        for q0, q1 in blocks:
            q = np.arange(q0, q0 + P)[:, None]
            k = np.arange(blocks[0][0], q1)[None, :]
            parts.append(np.where(k <= q, 0.0, NEG))
        return np.concatenate(parts, 1)

    t["mask_a"] = causal(BLK_A)
    t["mask_b"] = causal(BLK_B)
    j, i = np.arange(C)[:, None], np.arange(C)[None, :]
    t["later"] = np.where(i >= j, 0.0, NEG)
    t["strict"] = (i > j) * 1.0
    lev = [((i // (2 * b) == j // (2 * b)) & (j % (2 * b) < b) & (i % (2 * b) >= b)) * 1.0
           for b in (1 << n for n in range(LEVELS))]
    t["levels"] = np.concatenate(lev, 1)
    t["ident_c"] = np.eye(C)
    sel = np.zeros((P, P))
    sel[32:40] = 1.0
    t["sum_gc"] = sel
    sel = np.zeros((P, C))
    sel[0:8] = 1.0
    t["sum_beta"] = sel
    own = np.zeros((P, DNH))
    own[np.arange(8), np.arange(8)] = 1.0
    own[32 + np.arange(8), np.arange(8)] = 1.0
    t["own_head"] = own
    t["own_head_a"] = np.eye(16)
    t["rms_eps"] = np.full((P, 1), RMS_EPS)
    t["ln_eps"] = np.full((P, 1), LN_EPS)
    return t


def table_columns():
    at, where = 0, {}
    for name, a in tables().items():
        where[name] = (a.shape[0], at, a.shape[1])
        at += a.shape[1]
    return where, at


PARAMS = [("mix_pre", 2 * KT), ("mix_post", 2 * KT), ("ffn_pre", 2 * KT), ("ffn_post", 2 * KT),
          ("q_gain", 1), ("k_gain", 1), ("b_forget", 1), ("a_log", 1), ("dt_bias", 1), ("o_gain", 1),
          ("q_lat", QL), ("kv_lat", KVL), ("ln_g", 2 * KT), ("ln_b", 2 * KT),
          ("dn_conv", DNH * 3 * 4), ("ffn_conv", 2 * FT * 2 * 3),
          ("w_forget", KT * 16), ("w_beta_a", KT * 64), ("w_k_rope", KT * 64)]


def param_columns():
    at, where = 0, {}
    for name, n in PARAMS:
        where[name] = (at, n)
        at += n
    return where, at


UNIT_W = {"attn": 32 * P, "out": 32 * P, "up": 32 * P, "down": FT * P, "mla": 21 * P}
STREAM = [("w_attn", "attn", PAIRS), ("w_attn_out", "out", 2), ("w_up0", "up", FT // 2), ("w_down0", "down", KT),
          ("w_dn", "attn", DNH), ("w_dn_out", "out", 2), ("w_up1", "up", FT // 2), ("w_down1", "down", KT),
          ("w_latent", "out", 2), ("w_mla", "mla", PAIRS), ("w_mla_out", "out", 2),
          ("w_moba", "attn", PAIRS), ("w_moba_out", "out", 2)]


class Steps:

    def __init__(self, eng, sem):
        self.eng, self.sem, self.base, self.n = eng, sem, 0, 0

    def __call__(self, ins):
        ins.then_inc(self.sem, 1)
        self.n += 1
        return self.n

    def settle(self, upto=None):
        self.eng.wait_ge(self.sem, self.base + (self.n if upto is None else upto))

    def loop(self, start, stop, per, body):
        before = self.base + self.n
        with self.eng.Fori(start, stop) as i:
            self.base, self.n = (i - start) * per + before, 0
            body(i)
            assert self.n == per, (self.n, per)
        self.base, self.n = 0, before + (stop - start) * per


def wait(eng, sem, value):
    if not isinstance(value, int) or value > 0:
        eng.wait_ge(sem, value)


def build(nc, x, table, params, w, out):
    tcol, tw = table_columns()
    pcol, pw = param_columns()
    unit0, at = {}, 0
    for name, kind, n in STREAM:
        unit0[name] = at
        at += n
    ctx = ExitStack()
    with ctx:
        def sb(name, shape, rows=P):
            return ctx.enter_context(nc.sbuf_tensor(name, [rows, *shape], F32))

        def sem(name):
            return ctx.enter_context(nc.semaphore(name))

        bank = [ctx.enter_context(nc.psum_tensor(f"bank{i}", [P, 512], F32)) for i in range(8)]
        tab = sb("tab", [tw])
        par = sb("par", [pw])
        slot = [sb(f"slot{i}", [SLOT]) for i in range(2)]
        h = sb("h", [KT, T])
        a = sb("a", [KT, T])
        m = sb("m", [KT, T])
        o_room = sb("o_room", [DNH * NC * P])
        o_t = o_room[:, 0:KT * T].rearrange("p (k t) -> p k t", k=KT)
        sq = sb("sq", [2, T])
        root = sb("root", [T])
        rstd = sb("rstd", [T])
        root2 = sb("root2", [T])
        rstd2 = sb("rstd2", [T])

        def tb(name):
            rows, at, n = tcol[name]
            return tab[0:rows, at:at + n]

        def pr(name):
            at, n = pcol[name]
            return par[:, at:at + n]

        ident, ones, head_ones = tb("ident"), tb("ones"), tb("head_ones")
        eps = {"rms": tb("rms_eps"), "ln": tb("ln_eps")}

        s_in = sem("s_in")
        loaded = [sem(f"slot{i}_loaded") for i in range(2)]
        act_step, dve_step, pool_step = sem("act_step"), sem("dve_step"), sem("pool_step")
        sq_ready, sq_used = sem("sq_ready"), sem("sq_used")
        sum_done, root_done = sem("sum_done"), sem("root_done")
        h_ready, a_ready, m_ready = sem("h_ready"), sem("a_ready"), sem("m_ready")
        z_ready, out_done = sem("z_ready"), sem("out_done")
        stored = sem("stored")

        WORK = 5300
        work = sb("work", [WORK])
        used = [0]

        def carve(shape, rows=P):
            n = int(np.prod(shape))
            at = used[0]
            used[0] += n
            assert used[0] <= WORK
            part = work[0:rows, at:at + n]
            if len(shape) == 1:
                return part
            names = "abc"[:len(shape)]
            return part.rearrange(f"p ({' '.join(names)}) -> p {' '.join(names)}", **dict(zip(names, shape)))

        q_raw, k_raw = sb("q_raw", [T]), sb("k_raw", [T])
        q_sq, k_sq = sb("q_sq", [T]), sb("k_sq", [T])
        q_n, k_n = carve([T]), carve([T])
        q_rp, k_rp = carve([T], 64), carve([T], 64)
        rp_raw = carve([T], 64)
        t_sin = sb("t_sin", [T])
        v_s = carve([3, P])
        th, gate = sb("th", [T]), carve([T])
        s_m = carve([2, 432])
        p_e = carve([2, 432])
        mx, rs, ri = sb("mx", [2, 3]), sb("rs", [2, 3]), sb("ri", [2, 3])
        pt = carve([2, 384])
        pt0 = carve([2, T], META)
        used[0] = 0
        dn_keys = sb("dn_keys", [2 * DNH * TP])
        rows_a = dn_keys[0:16, 0:16 * T].rearrange("p (a t) -> p a t", a=16)
        rows_d = sb("rows_d", [DNH, TP])
        sp_a = sb("sp_a", [T], 64)
        sp_b = sb("sp_b", [T], 64)
        sp_c = sb("sp_c", [T], 64)

        q_proj, k_proj, v_proj, g_proj = sem("q_proj"), sem("k_proj"), sem("v_proj"), sem("g_proj")
        q_copied, k_copied = sem("q_copied"), sem("k_copied")
        q_side, k_side = sem("q_side"), sem("k_side")
        qk_root = sem("qk_root")
        q_ready, k_ready, v_ready, gate_ready, th_ready = (sem(n) for n in (
            "q_ready", "k_ready", "v_ready", "gate_ready", "th_ready"))
        s_done, s_taken, max_ready, exp_done, p_ready = (sem(n) for n in (
            "s_done", "s_taken", "max_ready", "exp_done", "p_ready"))
        pt_done, pt_taken, o_done, o_taken = (sem(n) for n in ("pt_done", "pt_taken", "o_done", "o_taken"))
        small_done, rows_ready, kr_seen, kr_rot, kr_ready = (sem(n) for n in (
            "small_done", "rows_ready", "kr_seen", "kr_rot", "kr_ready"))
        z_known, ln_done = sem("z_known"), sem("ln_done")

        region = sb("region", [FT * T + 6 * T])
        hid = region[:, 0:FT * T].rearrange("p (j t) -> p j t", j=FT)
        pieces = region[:, FT * T:].rearrange("p (n t) -> p n t", n=6)
        g_y, u_y, g_e = pieces[:, 0:2], pieces[:, 2:4], pieces[:, 4:6]
        up_done, tap_ready, conv_done, gelu_done, hid_ready = (sem(n) for n in (
            "up_done", "tap_ready", "conv_done", "gelu_done", "hid_ready"))

        HD = DNH * TP
        a_tr = region[0:C, 0:HD].rearrange("p (h t) -> p h t", h=DNH)
        d_in = region[0:C, HD:2 * HD].rearrange("p (h t) -> p h t", h=DNH)
        d_tr = region[0:C, 2 * HD:3 * HD].rearrange("p (h t) -> p h t", h=DNH)
        kn_all = dn_keys[:, 0:HD].rearrange("p (h t) -> p h t", h=DNH)
        qd_all = dn_keys[:, HD:2 * HD].rearrange("p (h t) -> p h t", h=DNH)
        qk_all = sb("qk_all", [DNH, TP], C)
        kd_all, vb_all = o_room[0:C].rearrange("p (h c v) -> p h c v", h=DNH, c=NC), carve([DNH, NC, P], C)
        o_gate = m
        q_st, k_st, v_st = sb("q_st", [TP]), sb("k_st", [TP]), sb("v_st", [TP])
        q_y, k_y, v_y = q_raw, k_raw, th
        e_row = sb("e_row", [TP])
        t_dec, dec = sb("t_dec", [TP], C), sb("dec", [TP], C)
        at_1, at_2 = region[0:C, 3 * HD:3 * HD + TP], region[0:C, 3 * HD + TP:3 * HD + 2 * TP]
        bg = sb("bg", [TP])
        bg_t = sb("bg_t", [NC, 64], C)
        eg_t, nbz = sb("eg_t", [NC, DNH], C), sb("nbz", [NC, DNH], C)
        g_last = sb("g_last", [DNH, NC])
        neg_a = sb("neg_a", [1], 64)
        l_st = carve([2, TP], C)
        x_st = carve([2, TP], C)
        s_t = sb("s_t", [DNH, P])
        r_st, u_st = carve([2, P], C), carve([2, P], C)
        o_raw = kn_all
        dn = {n: sem("dn_" + n) for n in (
            "proj", "tap", "conv", "sq", "ssq", "root", "st", "v_st", "gate", "row", "vt", "vt_out", "kk", "kt",
            "kt_out", "beta", "dec_t", "dec", "erow", "a1", "a2", "at", "qk", "qd", "kcopy", "prep", "bg", "bgt",
            "init", "l", "x", "x_out", "dd", "d", "ks", "r", "u", "u_out", "o", "o_out", "s_up", "s_new",
            "osq", "osum", "oroot", "zero", "negexp", "bgt_out", "eg", "ot")}

        block = ctx.enter_context(nc.Block())

        def unit_used(name, kind, u):
            if name == "w_dn":
                return dn["proj"], 4 * (u + 1)
            if kind in ("attn", "mla"):
                f = {"w_attn": 0, "w_mla": 1, "w_moba": 2}[name]
                return g_proj, 8 * f + u + 1
            if kind == "up":
                f = {"w_up0": 0, "w_up1": 1}[name]
                return up_done, 2 * FT * f + 4 * (u + 1)
            o = out_stage[name]
            return out_done, 8 * o + (u + 1 if kind == "down" else 4 * (u + 1))

        out_names = [n for n, kind, _ in STREAM if kind in ("out", "down")]
        out_stage = {n: i for i, n in enumerate(out_names)}

        def weights_here(eng, name, c, i=0):
            n = unit0[name] + c
            eng.wait_ge(loaded[n % 2], 16 * (n // 2 + 1) + 16 * i)
            return slot[n % 2]

        H_FINAL = 6 * KT

        @block.sync
        def _(sp):
            sp.dma_start(h[:], x).then_inc(s_in, 16)
            sp.dma_start(par[:], params).then_inc(s_in, 16)
            sp.dma_start(tab[:], table).then_inc(s_in, 16)
            before = []
            for name, kind, n in STREAM:
                width = UNIT_W[kind]

                def load(c, i=0):
                    s = (unit0[name] + c) % 2
                    sp.dma_start(slot[s][:, 0:width], w[name][c + 2 * i]).then_inc(loaded[s], 16)

                for u in range(2):
                    if before:
                        s_, v_ = unit_used(*before[u])
                        sp.wait_ge(s_, v_)
                    load(u)
                if n > 2:
                    with sp.Fori(0, (n - 2) // 2) as i:
                        for r in range(2):
                            s_, v0 = unit_used(name, kind, r)
                            _, v2 = unit_used(name, kind, r + 2)
                            sp.wait_ge(s_, i * (v2 - v0) + v0)
                            load(2 + r, i)
                    if n % 2:
                        s_, v_ = unit_used(name, kind, n - 3)
                        sp.wait_ge(s_, v_)
                        load(n - 1)
                before = [(name, kind, n - 2), (name, kind, n - 1)]
            sp.wait_ge(h_ready, H_FINAL)
            sp.dma_start(out, h[:, :, META:T]).then_inc(stored, 16)
            sp.wait_ge(stored, 16)

        REDUCE = ([(f"pre{i}", KT) if k % 2 == 0 else (f"post{i}", KT) for i in range(4) for k in (0, 1)]
                  + [("lat_q", QL), ("lat_kv", KVL), ("var1", KT), ("var2", KT)])
        sq0, red_no, tot = {}, {}, 0
        for n_, (name, tiles) in enumerate(REDUCE):
            sq0[name], red_no[name] = tot, n_
            tot += tiles
        sum_order = [n for n, _ in REDUCE[:10]] + ["mean1", "var1", "mean2", "var2"]
        sum_no = {n: i + 1 for i, n in enumerate(sum_order)}
        root_no = {n: i + 1 for i, (n, _) in enumerate(REDUCE)}
        H_AFTER = {"post0": 8, "post1": 16, "post2": 24, "post3": 32, "ln1": 40, "ln2": 48}

        def square(act, src, name, j, cols):
            n = sq0[name] + j
            wait(act, sq_used, n - 1)
            par2 = (sq0[name] + (j if isinstance(j, int) else 0)) % 2
            nc.scalar.activation(sq[:, par2, cols[0]:cols[1]], src, ACT.Square).then_inc(sq_ready, 1)

        def sum_tile(pe, name, j, tiles, cols, static_j=None, where=7):
            n = sq0[name] + j
            pe.wait_ge(sq_ready, n + 1)
            sj = j if static_j is None else static_j
            first = static_j is None and j == 0
            last = static_j is None and j == tiles - 1
            mm = nc.tensor.matmul(bank[where][:, cols[0]:cols[1]], ones, sq[:, (sq0[name] + sj) % 2, cols[0]:cols[1]],
                                  start=first, stop=last)
            mm.then_inc(sq_used, 1)

        def rms_root(act, name, count, cols, dst, where=7, e="rms"):
            act.wait_ge(sq_used, sq0[name] + dict(REDUCE)[name])
            nc.scalar.activation(dst[:, cols[0]:cols[1]], bank[where][:, cols[0]:cols[1]], ACT.Sqrt,
                                 bias=eps[e], scale=1.0 / count).then_inc(root_done, 1)

        def invert_root(dve, st, name, cols, src, dst):
            dve.wait_ge(root_done, root_no[name])
            st(nc.vector.reciprocal(dst[:, cols[0]:cols[1]], src[:, cols[0]:cols[1]]))
            st.settle()

        def pre_norm_act(act, name, cols, h_base):
            for j in range(KT):
                if h_base is None:
                    if j == 0:
                        act.wait_ge(s_in, 48)
                else:
                    act.wait_ge(h_ready, h_base + j + 1)
                square(act, h[:, j, cols[0]:cols[1]], name, j, cols)
            rms_root(act, name, D, cols, root)

        def sums_pe(pe, name, tiles, cols, where=7):
            for j in range(tiles):
                sum_tile(pe, name, j, tiles, cols, where=where)

        def pre_norm_dve(dve, st, name, gain, cols):
            invert_root(dve, st, name, cols, root, rstd)
            for j in range(KT):
                nc.vector.scalar_tensor_tensor(a[:, j, cols[0]:cols[1]], h[:, j, cols[0]:cols[1]], gain[:, j:j + 1],
                                               rstd[:, cols[0]:cols[1]], ALU.mult, ALU.mult).then_inc(a_ready, 1)

        def post_norm_dve(dve, st, name, gain, cols):
            invert_root(dve, st, name, cols, root, rstd)
            c0, c1 = cols
            marks = []
            for j in range(KT + 2):
                if j < KT:
                    marks.append(st(nc.vector.scalar_tensor_tensor(
                        m[:, j, c0:c1], m[:, j, c0:c1], gain[:, j:j + 1], rstd[:, c0:c1], ALU.mult, ALU.mult)))
                if j >= 2:
                    st.settle(marks[j - 2])
                    nc.vector.tensor_tensor(h[:, j - 2, c0:c1], h[:, j - 2, c0:c1], m[:, j - 2, c0:c1],
                                            ALU.add).then_inc(h_ready, 1)

        def out_pe(pe, wname, norm, src, src_tiles, cols, first_wait, mean=False):
            o = 8 * out_stage[wname]
            down = src_tiles == FT
            b_out = 4 if down else 0
            c0, c1 = cols

            def tile(j, jr, ws, at, c=None):
                if jr >= 2 or not isinstance(j, int):
                    pe.wait_ge(z_ready if mean else sq_ready, (ZB[wname] if mean else sq0[norm]) + j - 1)
                for k in range(src_tiles):
                    if j is jr and jr == 0:
                        first_wait(pe, k)
                    mm = nc.tensor.matmul(bank[b_out + jr % 2][:, c0:c1], ws[:, (at * src_tiles + k) * P:(at * src_tiles + k + 1) * P],
                                          src[:, k, c0:c1], start=k == 0, stop=k == src_tiles - 1)
                mm.then_inc(out_done, 1)

            def add(j, static=None):
                if mean:
                    pe.wait_ge(z_ready, ZB[wname] + j + 1)
                    mm = nc.tensor.matmul(bank[7][:, c0:c1], ones, m[:, j, c0:c1], start=j == 0, stop=j == KT - 1)
                    if j == KT - 1:
                        mm.then_inc(sum_done, 1)
                else:
                    sum_tile(pe, norm, j, KT, cols, static_j=static)

            if down:
                tile(0, 0, weights_here(pe, wname, 0), 0)
                tile(1, 1, weights_here(pe, wname, 1), 0)
                add(0)
                with pe.Fori(1, KT // 2) as i:
                    for r in range(2):
                        ws = weights_here(pe, wname, r, i)
                        tile(i * 2 + r, r, ws, 0)
                        add(i * 2 + (r - 1), static=(r - 1) % 2)
                add(KT - 1)
            else:
                for u in range(2):
                    ws = weights_here(pe, wname, u)
                    for q in range(4):
                        j = 4 * u + q
                        tile(j, j, ws, q)
                        if j:
                            add(j - 1)
                add(KT - 1)

        ZB = {"w_mla_out": 0, "w_moba_out": 8}

        def out_act(act, wname, norm, cols):
            b_out = 4 if "down" in wname else 0
            o = 8 * out_stage[wname]
            c0, c1 = cols

            def tile(j, r):
                act.wait_ge(out_done, j + (o + 1))
                nc.scalar.activation(m[:, j, c0:c1], bank[b_out + r][:, c0:c1], ACT.Copy).then_inc(m_ready, 1)
                n = j + sq0[norm]
                wait(act, sq_used, n - 1)
                nc.scalar.activation(sq[:, (sq0[norm] + r) % 2, c0:c1], bank[b_out + r][:, c0:c1], ACT.Square).then_inc(sq_ready, 1)

            tile(0, 0)
            tile(1, 1)
            with act.Fori(1, KT // 2) as i:
                for r in range(2):
                    tile(i * 2 + r, r)
            rms_root(act, norm, D, cols, root)

        def ln_dve(dve, st, wname, n_ln):
            o = 8 * out_stage[wname]
            c0, c1 = META, T
            for j in range(KT):
                dve.wait_ge(out_done, o + j + 1)
                nc.vector.scalar_tensor_tensor(m[:, j, c0:c1], h[:, j, c0:c1], ALPHA, bank[j % 2][:, c0:c1],
                                               ALU.mult, ALU.add).then_inc(z_ready, 1)
            dve.wait_ge(sum_done, n_ln)
            st(nc.vector.tensor_scalar(root2[:, c0:c1], bank[7][:, c0:c1], 1.0 / D, None, ALU.mult))
            st.settle()
            dve.wait_ge(z_ready, ZB[wname] + KT)
            for j in range(KT):
                nc.vector.tensor_tensor(m[:, j, c0:c1], m[:, j, c0:c1], root2[:, c0:c1],
                                        ALU.subtract).then_inc(m_ready, 1)
            invert_root(dve, st, f"var{n_ln}", (c0, c1), root, rstd)
            dve.wait_ge(m_ready, MB_LN[n_ln] + KT)
            g0 = (n_ln - 1) * KT
            for j in range(KT):
                st(nc.vector.scalar_tensor_tensor(m[:, j, c0:c1], m[:, j, c0:c1], pr("ln_g")[:, g0 + j:g0 + j + 1],
                                                  rstd[:, c0:c1], ALU.mult, ALU.mult))
            st.settle()
            for j in range(KT):
                nc.vector.tensor_scalar(h[:, j, c0:c1], m[:, j, c0:c1], pr("ln_b")[:, g0 + j:g0 + j + 1], None,
                                        ALU.add).then_inc(h_ready, 1)

        MB_LN = {1: 4 * KT, 2: 5 * KT}

        def ln_act(act, n_ln):
            c0, c1 = META, T
            for j in range(KT):
                act.wait_ge(m_ready, MB_LN[n_ln] + j + 1)
                square(act, m[:, j, c0:c1], f"var{n_ln}", j, (c0, c1))
            rms_root(act, f"var{n_ln}", D, (c0, c1), root, e="ln")

        SCALE = {0: 0.125, 1: 96 ** -0.5, 2: 0.125}

        def blocks(f):
            return BLK_A if f == 0 else BLK_B

        def span(f):
            return (0, T) if f == 0 else (META, T)

        def s_cols(f):
            at, res = 0, []
            for q0, q1 in blocks(f):
                n = q1 - blocks(f)[0][0]
                res.append((at, at + n))
                at += n
            return res

        def pe_project(pe, f, p, c, i, aw):
            name = ("w_attn", "w_mla", "w_moba")[f]
            g = p + 8 * f
            c0, c1 = span(f)
            ws = weights_here(pe, name, c, i)
            x_in = a if f == 0 else h
            if f != 1:
                at = {"q": 0, "k": KT * P, "v": 2 * KT * P, "g": 3 * KT * P}
                src = {s: (x_in, 0, KT) for s in "qkvg"}
            else:
                at = {"q": 0, "r": QL * P, "k": QL * P + QL * 64, "v": QL * P + QL * 64 + KVL * P,
                      "g": QL * P + QL * 64 + 2 * KVL * P}
                src = {"q": (a, 0, QL), "r": (a, 0, QL), "k": (a, QL, KVL), "v": (a, QL, KVL), "g": (h, 0, KT)}

            def feature(s, dst, width=P):
                t_, t0, n = src[s]
                for k in range(n):
                    if s == "q" and isinstance(p, int) and p == 0:
                        aw(pe, k)
                    mm = nc.tensor.matmul(dst, ws[:, at[s] + k * width:at[s] + (k + 1) * width], t_[:, t0 + k, c0:c1],
                                          start=k == 0, stop=k == n - 1)
                return mm

            def q_and_k():
                wait(pe, q_ready, g)
                mm = feature("q", bank[0][:, 0:c1 - c0])
                if f == 1:
                    mm = feature("r", bank[0][0:64, 256:512], 64)
                mm.then_inc(q_proj, 1)
                wait(pe, k_ready, g)
                feature("k", bank[1][:, 0:c1 - c0]).then_inc(k_proj, 1)

            def sides():
                n = c1 - c0
                if f != 1:
                    pe.wait_ge(q_copied, g + 1)
                k_seen = g + 1 if f == 0 else p + 9
                if f == 0:
                    nc.tensor.matmul(bank[0][:, 0:n], head_ones, q_sq[:, 0:n], start=True, stop=True).then_inc(q_side, 1)
                    pe.wait_ge(k_copied, k_seen)
                    nc.tensor.matmul(bank[1][:, 0:n], head_ones, k_sq[:, 0:n], start=True, stop=True).then_inc(k_side, 1)
                elif f == 1:
                    nc.tensor.matmul(bank[0][0:64, 256:512], tb("rot32"), rp_raw[:, 0:n], start=True, stop=True).then_inc(q_side, 1)
                else:
                    nc.tensor.matmul(bank[0][:, 0:n], tb("rot64"), q_raw[:, 0:n], start=True, stop=True).then_inc(q_side, 1)
                    pe.wait_ge(k_copied, k_seen)
                    nc.tensor.matmul(bank[1][:, 0:n], tb("rot64"), k_raw[:, 0:n], start=True, stop=True).then_inc(k_side, 1)

            def values():
                if f == 1:
                    pe.wait_ge(q_copied, g + 1)
                wait(pe, v_ready, g)
                t_, t0, n = src["v"]
                for b, (b0, b1) in enumerate(blocks(f)):
                    for k in range(n):
                        mm = nc.tensor.matmul(bank[2][0:b1 - b0, b * P:(b + 1) * P], t_[:, t0 + k, b0:b1],
                                              ws[:, at["v"] + k * P:at["v"] + (k + 1) * P], start=k == 0, stop=k == n - 1)
                mm.then_inc(v_proj, 1)

            def gates():
                wait(pe, gate_ready, g)
                feature("g", bank[3][:, 0:c1 - c0]).then_inc(g_proj, 1)

            return q_and_k, sides, values, gates

        def pe_scores(pe, f, p):
            g = p + 8 * f
            c0, c1 = span(f)
            pe.wait_ge(q_ready, g + 1)
            pe.wait_ge(k_ready, g + 1)
            wait(pe, o_taken, g)
            wait(pe, pt_taken, 2 * g)
            for hh in range(2):
                dst = bank[5 - hh]
                r = slice(64 * hh, 64 * hh + 64)
                for (q0, q1), (s0, s1) in zip(blocks(f), s_cols(f)):
                    n = s1 - s0
                    mm = nc.tensor.matmul(dst[:, s0:s1], q_n[r, q0 - c0:q0 - c0 + P], k_n[r, 0:n],
                                          start=True, stop=f == 2)
                    if f == 0:
                        mm = nc.tensor.matmul(dst[:, s0:s1], ones[0:16, :], rows_a[:, p * 2 + hh, 0:n],
                                              start=False, stop=True)
                    if f == 1:
                        r2 = slice(32 * hh, 32 * hh + 32)
                        mm = nc.tensor.matmul(dst[0:q1 - q0, s0:s1], q_rp[r2, q0 - c0:q1 - c0], k_rp[r2, 0:n],
                                              start=False, stop=True)
                mm.then_inc(s_done, 1)

        def pe_transposes(pe, f, p):
            g = p + 8 * f
            sc = s_cols(f)
            for hh in range(2):
                pe.wait_ge(p_ready, 2 * g + hh + 1)
                dst = (bank[6], bank[4])[hh]
                if f == 0:
                    lay = [(1, META, META + P, 0), (2, META, META + P, P), (2, META + P, T, 2 * P)]
                else:
                    lay = [(0, 0, P, 0), (1, 0, P, P), (1, P, 2 * P, 2 * P)]
                for b, k0, k1, at in lay:
                    mm = nc.tensor.transpose(dst[0:P, at:at + P], p_e[0:P, hh, sc[b][0] + k0:sc[b][0] + k1], ident)
                if f == 0:
                    for b in (1, 2):
                        mm = nc.tensor.transpose(bank[7][0:META, 256 * hh + (b - 1) * P:256 * hh + b * P],
                                                 p_e[0:P, hh, sc[b][0]:sc[b][0] + META], ident)
                    mm = nc.tensor.transpose(dst[0:META, 384:384 + META], p_e[0:META, hh, 0:META], ident[0:META, 0:META])
                mm.then_inc(pt_done, 1)

        def pe_outputs(pe, f, p):
            g = p + 8 * f
            pe.wait_ge(v_ready, g + 1)
            pe.wait_ge(pt_taken, 2 * g + 2)
            for hh in range(2):
                dst = bank[5][64 * hh:64 * hh + 64]
                vr = slice(64 * hh, 64 * hh + 64)
                if f == 0:
                    nc.tensor.matmul(dst[:, 0:T], v_s[0:META, 0, vr], pt0[:, hh, :], start=True, stop=False)
                    nc.tensor.matmul(dst[:, META:T], v_s[:, 1, vr], pt[:, hh, 0:256], start=False, stop=False)
                    mm = nc.tensor.matmul(dst[:, META + P:T], v_s[:, 2, vr], pt[:, hh, 256:384], start=False, stop=True)
                else:
                    nc.tensor.matmul(dst[:, 0:256], v_s[:, 0, vr], pt[:, hh, 0:256], start=True, stop=False)
                    mm = nc.tensor.matmul(dst[:, 128:256], v_s[:, 1, vr], pt[:, hh, 256:384], start=False, stop=True)
            mm.then_inc(o_done, 1)

        def attention_pe(pe, f):
            def aw(pe_, k):
                if f == 0:
                    pe_.wait_ge(a_ready, k + 1)
                elif f == 1 and k == 0:
                    pe_.wait_ge(a_ready, A_LAT)
                elif f == 2 and k == 0:
                    pe_.wait_ge(h_ready, H_AFTER["ln1"])

            def step(p, c, i):
                parts = pe_project(pe, f, p, c, i, aw)
                parts[0]()
                if not (isinstance(p, int) and p == 0):
                    pe_scores(pe, f, p - 1)
                for part in (parts[1:3] if f != 1 else (parts[2], parts[1])):
                    part()
                if not (isinstance(p, int) and p == 0):
                    pe_transposes(pe, f, p - 1)
                parts[3]()
                if not (isinstance(p, int) and p == 0):
                    pe_outputs(pe, f, p - 1)

            step(0, 0, 0)
            if f == 0:
                for k in range(KT):
                    mm = nc.tensor.matmul(bank[7][0:16, 0:T], pr("w_forget")[:, 16 * k:16 * k + 16], a[:, k, :],
                                          start=k == 0, stop=k == KT - 1)
                mm.then_inc(small_done, 1)
                pe.wait_ge(rows_ready, 1)
            elif f == 1:
                pe.wait_ge(kr_ready, 1)
            step(1, 1, 0)
            with pe.Fori(1, PAIRS // 2) as i:
                for r in range(2):
                    step(i * 2 + r, r, i)
            pe_scores(pe, f, PAIRS - 1)
            pe_transposes(pe, f, PAIRS - 1)
            pe_outputs(pe, f, PAIRS - 1)

        def attention_act(act, st, f):
            c0, c1 = span(f)
            n = c1 - c0

            def copies(p):
                g = p + 8 * f
                if f == 1:
                    if not (isinstance(p, int) and p == 0):
                        act.wait_ge(s_done, 2 * g)
                    act.wait_ge(q_proj, g + 1)
                    st(nc.scalar.activation(q_n[:, 0:n], bank[0][:, 0:n], ACT.Copy))
                    nc.scalar.activation(rp_raw[:, 0:n], bank[0][0:64, 256:512], ACT.Copy).then_inc(q_copied, 1)
                    act.wait_ge(k_proj, g + 1)
                    nc.scalar.activation(k_n[:, 0:n], bank[1][:, 0:n], ACT.Copy).then_inc(k_ready, 1)
                    return
                act.wait_ge(q_proj, g + 1)
                if f == 0:
                    st(nc.scalar.activation(q_raw[:, 0:n], bank[0][:, 0:n], ACT.Copy))
                    nc.scalar.activation(q_sq[:, 0:n], bank[0][:, 0:n], ACT.Square).then_inc(q_copied, 1)
                else:
                    nc.scalar.activation(q_raw[:, 0:n], bank[0][:, 0:n], ACT.Copy).then_inc(q_copied, 1)
                act.wait_ge(k_proj, g + 1)
                if f == 0:
                    st(nc.scalar.activation(k_raw[:, 0:n], bank[1][:, 0:n], ACT.Copy))
                    nc.scalar.activation(k_sq[:, 0:n], bank[1][:, 0:n], ACT.Square).then_inc(k_copied, 1)
                else:
                    nc.scalar.activation(k_raw[:, 0:n], bank[1][:, 0:n], ACT.Copy).then_inc(k_copied, 1)

            def roots(p):
                if f == 0:
                    g = p
                    act.wait_ge(q_side, g + 1)
                    wait(act, q_ready, g)
                    nc.scalar.activation(q_sq[:, 0:n], bank[0][:, 0:n], ACT.Sqrt, bias=eps["rms"], scale=1.0 / 64).then_inc(qk_root, 1)
                    act.wait_ge(k_side, g + 1)
                    wait(act, k_ready, g)
                    nc.scalar.activation(k_sq[:, 0:n], bank[1][:, 0:n], ACT.Sqrt, bias=eps["rms"], scale=1.0 / 64).then_inc(qk_root, 1)

            def exps(p):
                g = p + 8 * f
                for hh in range(2):
                    act.wait_ge(max_ready, 2 * g + hh + 1)
                    bl = list(enumerate(zip(blocks(f), s_cols(f))))
                    for b, ((q0, q1), (s0, s1)) in bl:
                        r = slice(0, q1 - q0)
                        ins = nc.scalar.activation(p_e[r, hh, s0:s1], s_m[r, hh, s0:s1], ACT.Exp, bias=mx[r, hh, b:b + 1],
                                                   scale=SCALE[f], accum_out=rs[r, hh, b:b + 1])
                        if b == len(bl) - 1:
                            ins.then_inc(exp_done, 1)
                        else:
                            st(ins)

            def pt_copies(p):
                g = p + 8 * f
                for hh in range(2):
                    act.wait_ge(pt_done, 2 * g + hh + 1)
                    src = (bank[6], bank[4])[hh]
                    if f == 0:
                        nc.scalar.activation(pt0[:, hh, 0:META], src[0:META, 384:384 + META], ACT.Copy)
                        if hh:
                            nc.scalar.activation(pt0[:, :, META:T], bank[7][0:META, :].rearrange("p (h t) -> p h t", h=2),
                                                 ACT.Copy)
                    nc.scalar.activation(pt[:, hh, :], src[:, 0:384], ACT.Copy).then_inc(pt_taken, 1)

            def value_copy(p):
                g = p + 8 * f
                act.wait_ge(v_proj, g + 1)
                if not (isinstance(p, int) and p == 0):
                    act.wait_ge(o_done, g)
                if f == 0:
                    nc.scalar.activation(v_s[0:META, 0, :], bank[2][0:META, 0:P], ACT.Copy)
                    nc.scalar.activation(v_s[:, 1:3, :], bank[2][:, P:3 * P], ACT.Copy).then_inc(v_ready, 1)
                else:
                    nc.scalar.activation(v_s[:, 0:2, :], bank[2][:, 0:2 * P], ACT.Copy).then_inc(v_ready, 1)
                act.wait_ge(g_proj, g + 1)
                wait(act, gate_ready, g)
                nc.scalar.activation(th[:, 0:n], bank[3][:, 0:n], ACT.Tanh, scale=0.5).then_inc(th_ready, 1)

            copies(0)
            roots(0)
            value_copy(0)
            if f == 0:
                act.wait_ge(z_known, 1)
                st(nc.scalar.activation(sp_a[0:16], sp_c[0:16], ACT.Abs))
                st.settle()
                st(nc.scalar.activation(sp_b[0:16], sp_a[0:16], ACT.Exp, scale=-1.0))
                st.settle()
                nc.scalar.activation(sp_a[0:16], sp_b[0:16], ACT.Ln, bias=ones[0:16, 0:1]).then_inc(ln_done, 1)

            def step(p):
                copies(p)
                roots(p)
                exps(p - 1)
                pt_copies(p - 1)
                value_copy(p)

            nb = len(blocks(f)) - 1
            step(1)
            per = 2 * nb + (2 if f == 0 else 1 if f == 1 else 0)
            st.loop(2, PAIRS, per, step)
            exps(PAIRS - 1)
            pt_copies(PAIRS - 1)

        def attention_dve(dve, st, f):
            c0, c1 = span(f)
            n = c1 - c0
            sc = s_cols(f)
            mask = tb("mask_a") if f == 0 else tb("mask_b")

            def maxima(p):
                g = p + 8 * f
                for hh in range(2):
                    dve.wait_ge(s_done, 2 * g + hh + 1)
                    src = bank[5 - hh]
                    if f == 0:
                        r = slice(0, META)
                        st(nc.vector.tensor_tensor(s_m[r, hh, 0:META], src[r, 0:META], mask[r, 0:META], ALU.add))
                        lo = META
                    else:
                        lo = 0
                    hi = sc[-1][1]
                    nc.vector.tensor_tensor(s_m[:, hh, lo:hi], src[:, lo:hi], mask[:, lo:hi], ALU.add).then_inc(s_taken, 1)
                for hh in range(2):
                    dve.wait_ge(s_taken, 2 * g + hh + 1)
                    for b, ((q0, q1), (s0, s1)) in enumerate(zip(blocks(f), sc)):
                        r = slice(0, q1 - q0)
                        st(nc.vector.tensor_reduce(mx[r, hh, b:b + 1], s_m[r, hh, s0:s1], AX, ALU.max, negate=True))
                st.settle()
                for hh in range(2):
                    nc.vector.tensor_scalar(mx[:, hh, :], mx[:, hh, :], SCALE[f], None, ALU.mult).then_inc(max_ready, 1)

            def norm(p, which):
                g = p + 8 * f
                raw, t_, dst, side, ready, bk = {
                    "q": (q_raw, q_sq, q_n, q_side, q_ready, 0), "k": (k_raw, k_sq, k_n, k_side, k_ready, 1)}[which]
                if which == "q":
                    wait(dve, k_ready, g)
                elif f == 0:
                    dve.wait_ge(q_ready, g + 1)
                if f == 0:
                    dve.wait_ge(qk_root, 2 * g + (1 if which == "q" else 2))
                    st(nc.vector.reciprocal(t_sin[:, 0:n], t_[:, 0:n]))
                    st.settle()
                    gain = pr("q_gain" if which == "q" else "k_gain")
                    nc.vector.scalar_tensor_tensor(dst[:, 0:n], raw[:, 0:n], gain, t_sin[:, 0:n], ALU.mult,
                                                   ALU.mult).then_inc(ready, 1)
                    return
                if f == 1:
                    if which == "k":
                        return
                    raw, dst, src, rr = rp_raw, q_rp, bank[0][0:64, 256:512], slice(0, 64)
                    cos, sin = tb("cos32"), tb("sin32")
                else:
                    src, rr = bank[bk][:, 0:n], slice(0, P)
                    cos, sin = tb("cos64"), tb("sin64")
                dve.wait_ge(side, g + 1)
                st(nc.vector.tensor_tensor(t_sin[rr, 0:n], src, sin, ALU.mult))
                st(nc.vector.tensor_tensor(dst[rr, 0:n], raw[rr, 0:n], cos, ALU.mult))
                st.settle()
                nc.vector.tensor_tensor(dst[rr, 0:n], dst[rr, 0:n], t_sin[rr, 0:n], ALU.add).then_inc(ready, 1)

            def norm_k(p):
                if f == 2:
                    dve.wait_ge(q_ready, p + 17)
                    dve.wait_ge(k_side, p + 9)
                    st(nc.vector.tensor_tensor(t_sin[:, 0:n], bank[1][:, 0:n], tb("sin64"), ALU.mult))
                    st(nc.vector.tensor_tensor(k_n[:, 0:n], k_raw[:, 0:n], tb("cos64"), ALU.mult))
                    st.settle()
                    nc.vector.tensor_tensor(k_n[:, 0:n], k_n[:, 0:n], t_sin[:, 0:n], ALU.add).then_inc(k_ready, 1)
                else:
                    norm(p, "k")

            def probs(p):
                g = p + 8 * f
                for hh in range(2):
                    dve.wait_ge(exp_done, 2 * g + hh + 1)
                    st(nc.vector.reciprocal(ri[:, hh, :], rs[:, hh, :]))
                    st.settle()
                    for b, ((q0, q1), (s0, s1)) in enumerate(zip(blocks(f), sc)):
                        r = slice(0, q1 - q0)
                        ins = nc.vector.tensor_scalar(p_e[r, hh, s0:s1], p_e[r, hh, s0:s1], ri[r, hh, b:b + 1], None, ALU.mult)
                        if b == len(sc) - 1:
                            ins.then_inc(p_ready, 1)

            def outputs(p):
                g = p + 8 * f
                dve.wait_ge(o_done, g + 1)
                nc.vector.scalar_tensor_tensor(o_t[:, p, c0:c1], bank[5][:, 0:n], 0.5, gate[:, 0:n],
                                               ALU.mult, ALU.mult).then_inc(o_taken, 1)

            def gates(p):
                g = p + 8 * f
                dve.wait_ge(th_ready, g + 1)
                wait(dve, o_taken, g)
                if f == 0:
                    nc.vector.tensor_scalar(gate[:, 0:n], th[:, 0:n], 1.0, None, ALU.add).then_inc(gate_ready, 1)
                else:
                    nc.vector.scalar_tensor_tensor(gate[:, 0:n], th[:, 0:n], 1.0, bank[3][:, 0:n], ALU.add,
                                                   ALU.mult).then_inc(gate_ready, 1)

            norm(0, "q")
            norm_k(0)
            gates(0)
            if f == 0:
                z = sp_c[0:16]
                dve.wait_ge(small_done, 1)
                nc.vector.tensor_scalar(z, bank[7][0:16, 0:T], pr("b_forget")[0:16], None, ALU.add).then_inc(z_known, 1)
                dve.wait_ge(ln_done, 1)
                dve.wait_ge(z_known, 1)
                st(nc.vector.scalar_tensor_tensor(sp_b[0:16], z, 0.0, sp_a[0:16], ALU.min, ALU.subtract))
                st.settle()
                st(nc.vector.tensor_tensor_scan(z, one_row[0:16, 0:T], sp_b[0:16], 0.0, ALU.mult, ALU.add))
                st.settle()
                st(nc.vector.tensor_scalar(sp_b[0:16], z, -8.0, None, ALU.mult))
                st.settle()
                nc.vector.tensor_tensor(rows_a, sp_b[0:16].unsqueeze(1).to_broadcast([16, 16, T]),
                                        tb("own_head_a").unsqueeze(2).to_broadcast([16, 16, T]),
                                        ALU.mult).then_inc(rows_ready, 1)

            def step(p):
                maxima(p - 1)
                norm(p, "q")
                probs(p - 1)
                norm_k(p)
                outputs(p - 1)
                gates(p)

            per = (2 if f == 0 else 0) + 2 * len(sc) + 2 + {0: 2, 1: 2, 2: 4}[f]
            step(1)
            st.loop(2, PAIRS, per, step)
            maxima(PAIRS - 1)
            probs(PAIRS - 1)
            outputs(PAIRS - 1)

        one_row = sb("one_row", [T], 64)
        A_LAT = 4 * KT + 2 * 4

        def ffn_span(f):
            return (0, T) if f == 0 else (META - CONV_PAST, T)

        def ffn_pe(pe, f):
            c0, c1 = ffn_span(f)
            name = f"w_up{f}"
            ab = KT * (2 * f + 1)

            def unit(u, c, i):
                ws = weights_here(pe, name, c, i)
                for r in range(2):
                    g = u * 2 + (r + FT * f)
                    if not (isinstance(u, int) and u == 0 and f == 0):
                        pe.wait_ge(conv_done, g - 1)
                    for half in range(2):
                        for k in range(KT):
                            if isinstance(u, int) and u == 0 and r == 0 and half == 0:
                                pe.wait_ge(a_ready, ab + k + 1)
                            w0 = ((2 * r + half) * KT + k) * P
                            mm = nc.tensor.matmul(bank[2 * r + half][:, c0:c1], ws[:, w0:w0 + P], a[:, k, c0:c1],
                                                  start=k == 0, stop=k == KT - 1)
                        mm.then_inc(up_done, 1)

            unit(0, 0, 0)
            with pe.Fori(0, (FT // 2 - 1) // 2) as i:
                for r in range(2):
                    unit(i * 2 + (1 + r), 1 + r, i)

            def hid_wait(pe_, k):
                pe_.wait_ge(hid_ready, FT * f + k + 1)

            out_pe(pe, f"w_down{f}", f"post{2 * f + 1}", hid, FT, (0, T) if f == 0 else (META, T), hid_wait)

        def conv_w(f, j, half, tap):
            cw = pr("ffn_conv").rearrange("p (f j a t) -> p f j a t", f=2, j=FT, a=2)
            return cw[:, f, j, half, tap:tap + 1]

        def ffn_act(act, st, f):
            c0, c1 = ffn_span(f)
            o0 = 0 if f == 0 else META

            def step(j, r):
                g = j + FT * f
                for half, y in ((0, g_y), (1, u_y)):
                    act.wait_ge(up_done, 2 * g + half + 1)
                    if half == 0 and not (isinstance(j, int) and j < 2 and f == 0):
                        act.wait_ge(hid_ready, g - 1)
                    nc.scalar.activation(y[:, r, o0:T], bank[2 * r + half][:, o0:T], ACT.Copy,
                                         scale=conv_w(f, j, half, 2)).then_inc(tap_ready, 1)
                act.wait_ge(conv_done, g + 1)
                nc.scalar.activation(g_e[:, r, o0:T], g_y[:, r, o0:T], ACT.Gelu_apprx_tanh).then_inc(gelu_done, 1)

            step(0, 0)
            step(1, 1)
            with act.Fori(1, FT // 2) as i:
                for r in range(2):
                    step(i * 2 + r, r)
            out_act(act, f"w_down{f}", f"post{2 * f + 1}", (0, T) if f == 0 else (META, T))

        def ffn_dve(dve, st, f):
            o0 = 0 if f == 0 else META

            def step(j, r):
                g = j + FT * f
                dve.wait_ge(tap_ready, 2 * g + 2)
                for back in (1, 2):
                    lo = max(o0, back)
                    for half, y in ((0, g_y), (1, u_y)):
                        ins = nc.vector.scalar_tensor_tensor(y[:, r, lo:T], bank[2 * r + half][:, lo - back:T - back],
                                                             conv_w(f, j, half, 2 - back), y[:, r, lo:T], ALU.mult, ALU.add)
                        if back == 1:
                            st(ins)
                        elif half == 1:
                            ins.then_inc(conv_done, 1)
                    if back == 1:
                        st.settle()
                dve.wait_ge(gelu_done, g + 1)
                nc.vector.tensor_tensor(hid[:, j, o0:T], g_e[:, r, o0:T], u_y[:, r, o0:T], ALU.mult).then_inc(hid_ready, 1)

            step(0, 0)
            step(1, 1)

            def both(i):
                for r in range(2):
                    step(i * 2 + r, r)
            st.loop(1, FT // 2, 4, both)

        def dn_pe(pe):
            def feature(ws, which, b):
                for k in range(KT):
                    mm = nc.tensor.matmul(bank[b][:, 0:T], ws[:, (which * KT + k) * P:(which * KT + k + 1) * P], a[:, k, :],
                                          start=k == 0, stop=k == KT - 1)
                mm.then_inc(dn["proj"], 1)

            def prepare(d):
                pe.wait_ge(dn["st"], 2 * d + 2)
                pe.wait_ge(dn["v_st"], d + 1)
                wait(pe, dn["kt_out"], 3 * d)
                wait(pe, dn["at"], d)
                wait(pe, dn["qk"], d)
                nc.tensor.matmul(bank[4][:, 0:TP], tb("sum_gc"), rows_d[:, d, :], start=True, stop=True).then_inc(dn["row"], 1)
                for c in range(NC):
                    mm = nc.tensor.transpose(bank[5][0:C, c * P:(c + 1) * P], v_st[:, c * C:(c + 1) * C], ident)
                mm.then_inc(dn["vt"], 1)
                for b, src in ((6, k_st), (7, q_st)):
                    for c in range(NC):
                        cc = slice(c * C, (c + 1) * C)
                        mm = nc.tensor.matmul(bank[b][0:C, cc], k_st[:, cc], src[:, cc], start=True, stop=True)
                mm.then_inc(dn["kk"], 1)
                pe.wait_ge(dn["erow"], d + 1)
                pe.wait_ge(dn["dec_t"], 3 * d + 3)
                for c in range(NC):
                    mm = nc.tensor.transpose(bank[4][0:C, c * P:(c + 1) * P], k_st[:, c * C:(c + 1) * C], ident)
                mm.then_inc(dn["kt"], 1)
                pe.wait_ge(dn["vt_out"], 3 * d + 3)
                nc.tensor.matmul(bank[5][0:C, 0:TP], tb("sum_beta"), rows_d[:, d, :], start=True, stop=True).then_inc(dn["beta"], 1)

            def step(d, c, i):
                ws = weights_here(pe, "w_dn", c, i)
                first = isinstance(d, int) and d == 0
                for which, b in ((0, 0), (1, 1), (2, 2)):
                    if which < 2:
                        wait(pe, dn["root"], 2 * d + which - 1 if not first else 0)
                    else:
                        wait(pe, dn["conv"], 3 * d if not first else 0)
                    feature(ws, which, b)
                pe.wait_ge(dn["conv"], 3 * d + 1)
                pe.wait_ge(dn["sq"], 2 * d + 1)
                nc.tensor.matmul(bank[0][:, 0:T], ones, q_sq[:, 0:T], start=True, stop=True).then_inc(dn["ssq"], 1)
                pe.wait_ge(dn["conv"], 3 * d + 2)
                pe.wait_ge(dn["sq"], 2 * d + 2)
                nc.tensor.matmul(bank[1][:, 0:T], ones, k_sq[:, 0:T], start=True, stop=True).then_inc(dn["ssq"], 1)
                if not first:
                    prepare(d - 1)
                    pe.wait_ge(dn["gate"], d)
                feature(ws, 3, 3)

            for k in range(KT):
                pe.wait_ge(a_ready, 2 * KT + k + 1)
                mm = nc.tensor.matmul(bank[4][0:64, 0:T], pr("w_beta_a")[:, 64 * k:64 * k + 64], a[:, k, :],
                                      start=k == 0, stop=k == KT - 1)
            mm.then_inc(small_done, 1)
            step(0, 0, 0)
            pe.wait_ge(dn["bg"], 2)
            for c in range(NC):
                mm = nc.tensor.transpose(bank[5][0:C, c * 64:(c + 1) * 64], bg[0:64, c * C:(c + 1) * C], ident[0:64, 0:64])
            mm.then_inc(dn["bgt"], 1)
            pe.wait_ge(rows_ready, 2)
            pe.wait_ge(dn["bgt_out"], 1)
            step(1, 1, 0)
            with pe.Fori(1, DNH // 2) as i:
                for r in range(2):
                    step(i * 2 + r, r, i)
            prepare(DNH - 1)

            pe.wait_ge(dn["init"], 1)
            pe.wait_ge(dn["gate"], DNH)
            pe.wait_ge(dn["kt_out"], NC * DNH)

            def level(lv):
                def x_of(hd):
                    g = lv * DNH + hd
                    pe.wait_ge(dn["l"], g + 1)
                    if not (isinstance(lv, int) and lv == 0):
                        pe.wait_ge(dn["d"], g - DNH + 1)
                    wait(pe, dn["x_out"], g - 1)
                    for c in range(NC):
                        cc = slice(c * C, (c + 1) * C)
                        mm = nc.tensor.matmul(bank[hd % 2][0:C, cc], l_st[:, hd % 2, cc], d_in[:, hd, cc], start=True, stop=True)
                    mm.then_inc(dn["x"], 1)

                def update(hd):
                    g = lv * DNH + hd
                    pe.wait_ge(dn["x_out"], g + 1)
                    wait(pe, dn["d"], g - 1)
                    for c in range(NC):
                        cc = slice(c * C, (c + 1) * C)
                        nc.tensor.matmul(bank[2 + hd % 2][0:C, cc], d_tr[:, hd, cc], x_st[:, hd % 2, cc], start=True, stop=True)
                        mm = nc.tensor.matmul(bank[4 + hd % 2][0:C, cc], x_st[:, hd % 2, cc], d_tr[:, hd, cc], start=True, stop=True)
                    mm.then_inc(dn["dd"], 1)

                x_of(0)
                for hd in range(1, DNH):
                    x_of(hd)
                    update(hd - 1)
                update(DNH - 1)

            level(0)
            with pe.Fori(1, LEVELS) as lv:
                level(lv)

            for c in range(NC):
                cc = slice(c * C, (c + 1) * C)

                def first_half(hd):
                    g = c * DNH + hd
                    if c:
                        pe.wait_ge(dn["s_new"], g - DNH + 1)
                        wait(pe, dn["r"], g - 1 - DNH)
                        nc.tensor.matmul(bank[hd % 2][0:C, 0:P], kn_all[:, hd, cc], s_t[:, hd, :], start=True,
                                         stop=True).then_inc(dn["ks"], 1)

                def second_half(hd):
                    g = c * DNH + hd
                    if c:
                        pe.wait_ge(dn["r"], g + 1 - DNH)
                        rhs = r_st[:, hd % 2, :]
                    else:
                        rhs = vb_all[:, hd, 0, :]
                        if hd == 0:
                            pe.wait_ge(dn["d"], LEVELS * DNH)
                    wait(pe, dn["u_out"], g - 1)
                    nc.tensor.matmul(bank[2 + hd % 2][0:C, 0:P], d_tr[:, hd, cc], rhs, start=True, stop=True).then_inc(dn["u"], 1)

                def third(hd):
                    g = c * DNH + hd
                    pe.wait_ge(dn["u_out"], g + 1)
                    wait(pe, dn["o_out"], g - 1)
                    if c:
                        nc.tensor.matmul(bank[4 + hd % 2][:, 0:C], s_t[:, hd, :], qd_all[:, hd, cc], start=True, stop=False)
                    nc.tensor.matmul(bank[4 + hd % 2][:, 0:C], u_st[:, hd % 2, :], qk_all[:, hd, cc], start=c == 0,
                                     stop=True).then_inc(dn["o"], 1)
                    if c < NC - 1:
                        wait(pe, dn["s_new"], g - 1)
                        nc.tensor.matmul(bank[6 + hd % 2][:, 0:P], kd_all[:, hd, c, :], u_st[:, hd % 2, :], start=True,
                                         stop=True).then_inc(dn["s_up"], 1)

                for hd in range(DNH + 2):
                    if hd < DNH:
                        first_half(hd)
                    if 0 <= hd - 1 < DNH:
                        second_half(hd - 1)
                    if hd >= 2:
                        third(hd - 2)

            for hd in range(DNH):
                pe.wait_ge(dn["osq"], hd + 1)
                wait(pe, dn["oroot"], hd - 1)
                nc.tensor.matmul(bank[6 + hd % 2][:, 0:T], ones, sq[:, hd % 2, :], start=True, stop=True).then_inc(dn["osum"], 1)

            def o_wait(pe_, k):
                pe_.wait_ge(dn["ot"], k + 1)
            out_pe(pe, "w_dn_out", "post2", o_t, KT, (META - CONV_PAST, T), o_wait)

        def dn_conv_w(d, which, tap):
            cw = pr("dn_conv").rearrange("p (h a t) -> p h a t", h=DNH, a=3)
            return cw[:, d, which, tap:tap + 1]

        def dn_act(act, st):
            bb = slice(32, 40)
            act.wait_ge(small_done, 2)
            act.wait_ge(dn["zero"], 1)
            nc.scalar.activation(bg[0:8, PAD:TP], bank[4][0:8, 0:T], ACT.Sigmoid).then_inc(dn["bg"], 1)
            act.wait_ge(z_known, 2)
            st(nc.scalar.activation(sp_a[bb], sp_c[bb], ACT.Abs))
            st.settle()
            st(nc.scalar.activation(sp_b[bb], sp_a[bb], ACT.Exp, scale=-1.0))
            nc.scalar.activation(neg_a[bb], pr("a_log")[bb], ACT.Exp).then_inc(dn["negexp"], 1)
            st.settle()
            nc.scalar.activation(sp_a[bb], sp_b[bb], ACT.Ln, bias=ones[bb, 0:1]).then_inc(ln_done, 1)

            def tap(d, which, y):
                act.wait_ge(dn["proj"], 4 * d + which + 1)
                nc.scalar.activation(y[:, 0:T], bank[which][:, 0:T], ACT.Copy, scale=dn_conv_w(d, which, 3)).then_inc(dn["tap"], 1)

            def silu_sq(d, which, y, s):
                act.wait_ge(dn["conv"], 3 * d + which + 1)
                st(nc.scalar.activation(y[:, 0:T], y[:, 0:T], ACT.Silu))
                st.settle()
                nc.scalar.activation(s[:, 0:T], y[:, 0:T], ACT.Square).then_inc(dn["sq"], 1)

            def main(d):
                first = isinstance(d, int) and d == 0
                wait(act, dn["st"], 2 * d if not first else 0)
                tap(d, 0, q_y)
                tap(d, 1, k_y)
                silu_sq(d, 0, q_y, q_sq)
                silu_sq(d, 1, k_y, k_sq)
                wait(act, dn["v_st"], d)
                tap(d, 2, v_y)

            def value(d):
                act.wait_ge(dn["conv"], 3 * d + 3)
                if not (isinstance(d, int) and d == 0):
                    act.wait_ge(dn["vt"], d)
                nc.scalar.activation(v_st[:, PAD:TP], v_y[:, 0:T], ACT.Silu).then_inc(dn["v_st"], 1)

            def roots(d):
                for which, s in ((0, q_sq), (1, k_sq)):
                    act.wait_ge(dn["ssq"], 2 * d + which + 1)
                    nc.scalar.activation(s[:, 0:T], bank[which][:, 0:T], ACT.Sqrt, bias=eps["rms"]).then_inc(dn["root"], 1)

            def out_gate(d):
                act.wait_ge(dn["proj"], 4 * d + 4)
                nc.scalar.activation(o_gate[:, d, :], bank[3][:, 0:T], ACT.Silu).then_inc(dn["gate"], 1)

            def prep(d):
                act.wait_ge(dn["row"], d + 1)
                wait(act, dn["qd"], d)
                st.settle()
                nc.scalar.activation(e_row[:], bank[4][:, 0:TP], ACT.Exp).then_inc(dn["erow"], 1)
                act.wait_ge(dn["vt"], d + 1)
                for c in range(NC):
                    nc.scalar.activation(vb_all[:, d, c, :], bank[5][0:C, c * P:(c + 1) * P], ACT.Copy,
                                         scale=bg_t[:, c, bass.ds(d, 1)]).then_inc(dn["vt_out"], 1)
                act.wait_ge(dn["dec_t"], 3 * d + 3)
                nc.scalar.activation(dec[:], t_dec[:], ACT.Exp).then_inc(dn["dec"], 1)
                act.wait_ge(dn["kt"], d + 1)
                act.wait_ge(dn["dec"], d + 1)
                for c in range(NC):
                    nc.scalar.activation(kd_all[:, d, c, :], bank[4][0:C, c * P:(c + 1) * P], ACT.Copy,
                                         scale=dec[:, (c + 1) * C - 1:(c + 1) * C]).then_inc(dn["kt_out"], 1)
                act.wait_ge(dn["erow"], d + 1)
                st(nc.scalar.activation(g_last[:, d, :], e_row[:].rearrange("p (c t) -> p c t", c=NC)[:, :, C - 1],
                                        ACT.Copy))

            main(0)
            roots(0)
            value(0)
            out_gate(0)
            act.wait_ge(dn["bgt"], 1)
            nc.scalar.activation(bg_t[:], bank[5][0:C, 0:NC * 64], ACT.Copy).then_inc(dn["bgt_out"], 1)
            act.wait_ge(dn["bgt_out"], 1)
            nc.scalar.activation(eg_t[:], bg_t[:, :, 32:40], ACT.Exp).then_inc(dn["eg"], 1)

            def step(d):
                main(d)
                prep(d - 1)
                value(d)
                roots(d)
                out_gate(d)

            step(1)
            st.loop(2, DNH, 3, step)
            prep(DNH - 1)

            def level(lv):
                for hd in range(DNH):
                    g = lv * DNH + hd
                    act.wait_ge(dn["x"], g + 1)
                    wait(act, dn["dd"], g - 1)
                    nc.scalar.activation(x_st[:, hd % 2, :], bank[hd % 2][0:C, 0:TP], ACT.Copy).then_inc(dn["x_out"], 1)
            level(0)
            with act.Fori(1, LEVELS) as lv:
                level(lv)

            for c in range(NC):
                for hd in range(DNH + 1):
                    if hd < DNH:
                        g = c * DNH + hd
                        act.wait_ge(dn["u"], g + 1)
                        if g >= 2:
                            act.wait_ge(dn["o"], g - 1)
                            act.wait_ge(dn["s_up"], min(g - 1, 2 * DNH))
                        nc.scalar.activation(u_st[:, hd % 2, :], bank[2 + hd % 2][0:C, 0:P], ACT.Copy).then_inc(dn["u_out"], 1)
                    if hd:
                        g = c * DNH + hd - 1
                        act.wait_ge(dn["o"], g + 1)
                        nc.scalar.activation(o_raw[:, hd - 1, c * C:(c + 1) * C], bank[4 + (hd - 1) % 2][:, 0:C],
                                             ACT.Copy).then_inc(dn["o_out"], 1)
            for hd in range(DNH):
                act.wait_ge(dn["o_out"], 2 * DNH + hd + 1)
                wait(act, dn["osum"], hd - 1)
                nc.scalar.activation(sq[:, hd % 2, :], o_raw[:, hd, PAD:TP], ACT.Square).then_inc(dn["osq"], 1)
                if hd:
                    o_root(act, hd - 1)
            o_root(act, DNH - 1)
            out_act(act, "w_dn_out", "post2", (META - CONV_PAST, T))

        def o_root(act, hd):
            act.wait_ge(dn["osum"], hd + 1)
            wait(act, dn["ot"], hd - 1)
            dst = (root, root2)[hd % 2]
            nc.scalar.activation(dst[:], bank[6 + hd % 2][:, 0:T], ACT.Sqrt, bias=eps["rms"],
                                 scale=1.0 / P).then_inc(dn["oroot"], 1)

        def dn_dve(dve, st):
            bb = slice(32, 40)
            dve.wait_ge(small_done, 2)
            nc.vector.tensor_scalar(sp_c[bb], bank[4][bb, 0:T], pr("dt_bias")[bb], None, ALU.add).then_inc(z_known, 1)
            dve.wait_ge(dn["negexp"], 1)
            st(nc.vector.tensor_scalar(neg_a[bb], neg_a[bb], -1.0, None, ALU.mult))
            dve.wait_ge(ln_done, 2)
            st.settle()
            st(nc.vector.scalar_tensor_tensor(sp_c[bb], sp_c[bb], 0.0, sp_a[bb], ALU.max, ALU.add))
            st.settle()
            dve.wait_ge(dn["zero"], 1)
            st(nc.vector.tensor_scalar(g_pad[bb, PAD:TP], sp_c[bb], neg_a[bb], None, ALU.mult))
            st.settle()
            for c in range(NC):
                cc = slice(c * C, (c + 1) * C)
                ins = nc.vector.tensor_tensor_scan(bg[bb, cc], one_row[bb, 0:C], g_pad[bb, cc], 0.0, ALU.mult, ALU.add)
                st(ins) if c < NC - 1 else ins.then_inc(dn["bg"], 1)

            dve.wait_ge(dn["bg"], 2)
            st.settle()
            nc.vector.tensor_tensor(rows_d[:], bg[:].unsqueeze(1).to_broadcast([P, DNH, TP]),
                                    tb("own_head").unsqueeze(2).to_broadcast([P, DNH, TP]), ALU.mult).then_inc(rows_ready, 1)

            def conv(d, which, y):
                dve.wait_ge(dn["tap"], 3 * d + which + 1)
                for back in (1, 2, 3):
                    ins = nc.vector.scalar_tensor_tensor(y[:, back:T], bank[which][:, 0:T - back], dn_conv_w(d, which, 3 - back),
                                                         y[:, back:T], ALU.mult, ALU.add)
                    if back < 3:
                        st(ins)
                        st.settle()
                    else:
                        ins.then_inc(dn["conv"], 1)

            def norms(d):
                for which, (y, s, dst, scale) in enumerate(((q_y, q_sq, q_st, P ** -0.5), (k_y, k_sq, k_st, 1.0))):
                    dve.wait_ge(dn["root"], 2 * d + which + 1)
                    wait(dve, dn["st"], 2 * d + which)
                    st(nc.vector.reciprocal(t_sin[:, 0:T], s[:, 0:T]))
                    st.settle()
                    if which == 0 and not (isinstance(d, int) and d == 0):
                        dve.wait_ge(dn["kt"], d)
                        dve.wait_ge(dn["qd"], d)
                        dve.wait_ge(dn["kcopy"], d)
                    nc.vector.scalar_tensor_tensor(dst[:, PAD:TP], y[:, 0:T], scale, t_sin[:, 0:T], ALU.mult,
                                                   ALU.mult).then_inc(dn["st"], 1)

            def prep(d):
                dve.wait_ge(dn["erow"], d + 1)
                nc.vector.tensor_tensor(qd_all[:, d, :], q_st[:], e_row[:], ALU.mult).then_inc(dn["qd"], 1)
                nc.vector.tensor_copy(kn_all[:, d, :], k_st[:]).then_inc(dn["kcopy"], 1)
                for c in range(NC):
                    cc = slice(c * C, (c + 1) * C)
                    nc.vector.scalar_tensor_tensor(t_dec[:, cc], bank[4][0:C, cc], bg_t[:, c, bass.ds(d + 32, 1)], tb("later"),
                                                   ALU.subtract, ALU.add).then_inc(dn["dec_t"], 1)
                dve.wait_ge(dn["dec"], d + 1)
                dve.wait_ge(dn["kk"], d + 1)
                nc.vector.tensor_tensor(at_1[:], bank[6][0:C, 0:TP], dec[:], ALU.mult).then_inc(dn["a1"], 1)
                nc.vector.tensor_tensor(qk_all[:, d, :], bank[7][0:C, 0:TP], dec[:], ALU.mult).then_inc(dn["qk"], 1)
                dve.wait_ge(dn["a2"], d + 1)
                dve.wait_ge(dn["beta"], d + 1)
                nc.vector.tensor_tensor(a_tr[:, d, :], at_2[:], bank[5][0:C, 0:TP], ALU.mult).then_inc(dn["at"], 1)

            def convs(d):
                conv(d, 0, q_y)
                conv(d, 1, k_y)
                conv(d, 2, v_y)

            convs(0)
            norms(0)
            dve.wait_ge(dn["eg"], 1)
            st(nc.vector.scalar_tensor_tensor(nbz[:], eg_t[:], -1.0, bg_t[:, :, 0:8], ALU.mult, ALU.mult))

            def step(d):
                convs(d)
                prep(d - 1)
                norms(d)
            step(1)
            st.loop(2, DNH, 8, step)
            prep(DNH - 1)

            def level(lv):
                for hd in range(DNH):
                    g = lv * DNH + hd
                    dve.wait_ge(dn["dd"], g + 1)
                    st(nc.vector.tensor_tensor(d_in[:, hd, :], d_in[:, hd, :], bank[2 + hd % 2][0:C, 0:TP], ALU.subtract))
                    nc.vector.tensor_tensor(d_tr[:, hd, :], d_tr[:, hd, :], bank[4 + hd % 2][0:C, 0:TP],
                                            ALU.subtract).then_inc(dn["d"], 1)
            dve.wait_ge(dn["init"], 1)
            level(0)
            st.loop(1, LEVELS, DNH, level)

            for c in range(NC):
                def residual(hd):
                    g = (c - 1) * DNH + hd
                    dve.wait_ge(dn["ks"], g + 1)
                    dve.wait_ge(dn["u"], c * DNH + hd - 1)
                    nc.vector.scalar_tensor_tensor(r_st[:, hd % 2, :], bank[hd % 2][0:C, 0:P], nbz[:, c, hd:hd + 1],
                                                   vb_all[:, hd, c, :], ALU.mult, ALU.add).then_inc(dn["r"], 1)

                def state(hd):
                    g = c * DNH + hd
                    dve.wait_ge(dn["s_up"], g + 1)
                    if c == 0:
                        nc.vector.tensor_copy(s_t[:, hd, :], bank[6 + hd % 2][:, 0:P]).then_inc(dn["s_new"], 1)
                    else:
                        nc.vector.scalar_tensor_tensor(s_t[:, hd, :], s_t[:, hd, :], g_last[:, hd, c:c + 1],
                                                       bank[6 + hd % 2][:, 0:P], ALU.mult, ALU.add).then_inc(dn["s_new"], 1)
                for hd in range(DNH + 2):
                    if hd < DNH and c:
                        residual(hd)
                    if hd >= 2 and c < NC - 1:
                        state(hd - 2)
            for hd in range(DNH):
                dve.wait_ge(dn["oroot"], hd + 1)
                wait(dve, dn["ot"], hd)
                st(nc.vector.reciprocal(rstd[:], (root, root2)[hd % 2][:]))
                st.settle()
                st(nc.vector.scalar_tensor_tensor(t_sin[:], o_raw[:, hd, PAD:TP], pr("o_gain"), rstd[:], ALU.mult, ALU.mult))
                st.settle()
                nc.vector.tensor_tensor(o_t[:, hd, :], t_sin[:], o_gate[:, hd, :], ALU.mult).then_inc(dn["ot"], 1)

        g_pad = sb("g_pad", [TP], 64)

        def by_chunk(ap):
            return ap.rearrange("p (c t) -> p c t", c=NC)

        def by_block(at):
            return region[0:C, at:at + HD].rearrange("p (b t) -> p b t", t=C)

        def dn_pool(pool):
            def step(d):
                pool.wait_ge(dn["a1"], d + 1)
                wait(pool, dn["at"], d)
                nc.gpsimd.tensor_tensor(by_chunk(at_2), by_chunk(at_1), tb("strict").unsqueeze(1).to_broadcast([C, NC, C]),
                                        ALU.mult).then_inc(dn["a2"], 1)

            step(0)
            with pool.Fori(1, DNH) as d:
                step(d)
            nc.gpsimd.tensor_copy(by_block(HD), tb("ident_c").unsqueeze(1).to_broadcast([C, DNH * NC, C]))
            nc.gpsimd.tensor_copy(by_block(2 * HD), tb("ident_c").unsqueeze(1).to_broadcast([C, DNH * NC, C])).then_inc(dn["init"], 1)
            pool.wait_ge(dn["at"], DNH)

            def level(lv):
                for hd in range(DNH):
                    g = lv * DNH + hd
                    wait(pool, dn["x"], g - 1)
                    masks = tb("levels").rearrange("p (l t) -> p l t", l=LEVELS)
                    nc.gpsimd.tensor_tensor(by_chunk(l_st[:, hd % 2, :]), by_chunk(a_tr[:, hd, :]),
                                            masks[:, lv, :].unsqueeze(1).to_broadcast([C, NC, C]), ALU.mult).then_inc(dn["l"], 1)
            for lv in range(LEVELS):
                level(lv)

        def latent_pe(pe):
            c0, c1 = META, T
            base = 8 * out_stage["w_latent"]
            for u in range(2):
                ws = weights_here(pe, "w_latent", u)
                for q in range(4):
                    j = 4 * u + q
                    if j >= 2:
                        pe.wait_ge(sq_ready, sq0["lat_q"] + j - 1)
                    for k in range(KT):
                        if j == 0:
                            pe.wait_ge(h_ready, H_AFTER["post3"] - KT + k + 1)
                        mm = nc.tensor.matmul(bank[j % 2][:, c0:c1], ws[:, (q * KT + k) * P:(q * KT + k + 1) * P],
                                              h[:, k, c0:c1], start=k == 0, stop=k == KT - 1)
                    mm.then_inc(out_done, 1)
                    if j:
                        lat_sum(pe, j - 1)
            lat_sum(pe, KT - 1)
            for k in range(KT):
                mm = nc.tensor.matmul(bank[5][0:64, c0:c1], pr("w_k_rope")[:, 64 * k:64 * k + 64], h[:, k, c0:c1],
                                      start=k == 0, stop=k == KT - 1)
            mm.then_inc(small_done, 1)
            pe.wait_ge(kr_seen, 1)
            nc.tensor.matmul(bank[5][0:64, c0:c1], tb("rot32"), sp_a[:, 0:SEQ], start=True, stop=True).then_inc(kr_rot, 1)

        def lat_sum(pe, j):
            if j < QL:
                sum_tile(pe, "lat_q", j, QL, (META, T), where=7)
            else:
                sum_tile(pe, "lat_kv", j - QL, KVL, (META, T), where=6)

        def latent_act(act, st):
            c0, c1 = META, T
            base = 8 * out_stage["w_latent"]
            for j in range(KT):
                act.wait_ge(out_done, base + j + 1)
                nc.scalar.activation(m[:, j, c0:c1], bank[j % 2][:, c0:c1], ACT.Copy).then_inc(z_lat, 1)
                name, jj = ("lat_q", j) if j < QL else ("lat_kv", j - QL)
                square(act, bank[j % 2][:, c0:c1], name, jj, (c0, c1))
            rms_root(act, "lat_q", QL * P, (c0, c1), root)
            rms_root(act, "lat_kv", KVL * P, (c0, c1), root2, where=6)
            act.wait_ge(small_done, 3)
            nc.scalar.activation(sp_a[:, 0:SEQ], bank[5][0:64, c0:c1], ACT.Copy).then_inc(kr_seen, 1)

        z_lat = sem("z_lat")

        def latent_dve(dve, st):
            c0, c1 = META, T
            invert_root(dve, st, "lat_q", (c0, c1), root, rstd)
            invert_root(dve, st, "lat_kv", (c0, c1), root2, rstd2)
            dve.wait_ge(z_lat, KT)
            for j in range(KT):
                gain, r = (pr("q_lat")[:, j:j + 1], rstd) if j < QL else (pr("kv_lat")[:, j - QL:j - QL + 1], rstd2)
                nc.vector.scalar_tensor_tensor(a[:, j, c0:c1], m[:, j, c0:c1], gain, r[:, c0:c1], ALU.mult,
                                               ALU.mult).then_inc(a_ready, 1)
            dve.wait_ge(kr_seen, 1)
            st(nc.vector.tensor_tensor(sp_b[:, 0:SEQ], sp_a[:, 0:SEQ], tb("cos32"), ALU.mult))
            dve.wait_ge(kr_rot, 1)
            st(nc.vector.tensor_tensor(sp_c[:, 0:SEQ], bank[5][0:64, c0:c1], tb("sin32"), ALU.mult))
            st.settle()
            nc.vector.tensor_tensor(k_rp[:, 0:SEQ], sp_b[:, 0:SEQ], sp_c[:, 0:SEQ], ALU.add).then_inc(kr_ready, 1)

        gains = {"pre0": pr("mix_pre")[:, 0:KT], "post0": pr("mix_post")[:, 0:KT],
                 "pre1": pr("ffn_pre")[:, 0:KT], "post1": pr("ffn_post")[:, 0:KT],
                 "pre2": pr("mix_pre")[:, KT:], "post2": pr("mix_post")[:, KT:],
                 "pre3": pr("ffn_pre")[:, KT:], "post3": pr("ffn_post")[:, KT:]}
        FULL, TAIL, LAST = (0, T), (META - CONV_PAST, T), (META, T)

        @block.tensor
        def _(pe):
            pe.wait_ge(s_in, 48)
            sums_pe(pe, "pre0", KT, FULL)
            attention_pe(pe, 0)
            out_pe(pe, "w_attn_out", "post0", o_t, KT, FULL, lambda e, k: e.wait_ge(o_taken, k + 1))
            sums_pe(pe, "pre1", KT, FULL)
            ffn_pe(pe, 0)
            sums_pe(pe, "pre2", KT, FULL)
            dn_pe(pe)
            sums_pe(pe, "pre3", KT, TAIL)
            ffn_pe(pe, 1)
            latent_pe(pe)
            attention_pe(pe, 1)
            out_pe(pe, "w_mla_out", None, o_t, KT, LAST, lambda e, k: e.wait_ge(o_taken, 8 + k + 1), mean=True)
            sums_pe(pe, "var1", KT, LAST)
            attention_pe(pe, 2)
            out_pe(pe, "w_moba_out", None, o_t, KT, LAST, lambda e, k: e.wait_ge(o_taken, 16 + k + 1), mean=True)
            sums_pe(pe, "var2", KT, LAST)

        @block.scalar
        def _(act):
            st = Steps(act, act_step)
            pre_norm_act(act, "pre0", FULL, None)
            attention_act(act, st, 0)
            out_act(act, "w_attn_out", "post0", FULL)
            pre_norm_act(act, "pre1", FULL, 0)
            ffn_act(act, st, 0)
            pre_norm_act(act, "pre2", FULL, 8)
            dn_act(act, st)
            pre_norm_act(act, "pre3", TAIL, 16)
            ffn_act(act, st, 1)
            latent_act(act, st)
            attention_act(act, st, 1)
            ln_act(act, 1)
            attention_act(act, st, 2)
            ln_act(act, 2)

        @block.vector
        def _(dve):
            st = Steps(dve, dve_step)
            st(nc.vector.memset(one_row[:], 1.0))
            st(nc.vector.memset(rs[:], 1.0))
            st(nc.vector.memset(mx[:], 0.0))
            st.settle()
            dve.wait_ge(s_in, 48)
            pre_norm_dve(dve, st, "pre0", gains["pre0"], FULL)
            attention_dve(dve, st, 0)
            dve.wait_ge(m_ready, KT)
            post_norm_dve(dve, st, "post0", gains["post0"], FULL)
            dve.wait_ge(h_ready, 8)
            pre_norm_dve(dve, st, "pre1", gains["pre1"], FULL)
            ffn_dve(dve, st, 0)
            dve.wait_ge(m_ready, 2 * KT)
            post_norm_dve(dve, st, "post1", gains["post1"], FULL)
            dve.wait_ge(h_ready, 16)
            pre_norm_dve(dve, st, "pre2", gains["pre2"], FULL)
            dn_dve(dve, st)
            dve.wait_ge(m_ready, 3 * KT)
            post_norm_dve(dve, st, "post2", gains["post2"], TAIL)
            dve.wait_ge(h_ready, 24)
            pre_norm_dve(dve, st, "pre3", gains["pre3"], TAIL)
            ffn_dve(dve, st, 1)
            dve.wait_ge(m_ready, 4 * KT)
            post_norm_dve(dve, st, "post3", gains["post3"], LAST)
            latent_dve(dve, st)
            attention_dve(dve, st, 1)
            ln_dve(dve, st, "w_mla_out", 1)
            attention_dve(dve, st, 2)
            ln_dve(dve, st, "w_moba_out", 2)

        @block.gpsimd
        def _(pool):
            nc.gpsimd.memset(bg[:], 0.0)
            nc.gpsimd.memset(q_st[:], 0.0)
            nc.gpsimd.memset(k_st[:], 0.0)
            nc.gpsimd.memset(v_st[:], 0.0)
            nc.gpsimd.memset(g_pad[:], 0.0).then_inc(dn["zero"], 1)
            dn_pool(pool)


def lay_out(inp):
    f32 = np.float32

    def cols(wm, c0, n):
        b = wm[:, c0:c0 + n]
        return b.reshape(b.shape[0] // P, P, n).transpose(1, 0, 2).reshape(P, -1)

    def units(lists):
        return np.ascontiguousarray(np.stack([np.concatenate(x, 1) for x in lists])).astype(f32, copy=False)

    def outs(wm):
        return units([[cols(wm, (4 * u + q) * P, P) for q in range(4)] for u in range(2)])

    w = {}
    wa = inp["attn_w_in"][0]
    w["w_attn"] = units([[cols(wa, s * D + p * P, P) for s in range(4)] for p in range(PAIRS)])
    w["w_attn_out"] = outs(inp["attn_w_out"][0])
    wd = inp["dn_w_in"][0]
    w["w_dn"] = units([[cols(wd, s * D + p * P, P) for s in range(4)] for p in range(DNH)])
    w["w_dn_out"] = outs(inp["dn_w_out"][0])
    for f in range(2):
        up, down = inp["ffn_w_up"][f], inp["ffn_w_down"][f]
        w[f"w_up{f}"] = units([[cols(up, half * FFN + (2 * u + r) * P, P) for r in range(2) for half in range(2)]
                               for u in range(FT // 2)])
        w[f"w_down{f}"] = units([[cols(down, j * P, P)] for j in range(KT)])
    wm = inp["mla_w_in_2"][0]
    w["w_latent"] = outs(wm[:, 0:D])
    uq, ukv = inp["mla_w_uq_2"][0], inp["mla_w_ukv_2"][0]

    def gather(wm_, parts):
        return cols(np.concatenate([wm_[:, c:c + n] for c, n in parts], 1), 0, sum(n for _, n in parts))

    w["w_mla"] = units([[
        gather(uq, [((2 * p + i) * 96, 64) for i in range(2)]),
        gather(uq, [((2 * p + i) * 96 + 64, 32) for i in range(2)]),
        gather(ukv, [((2 * p + i) * 128, 64) for i in range(2)]),
        gather(ukv, [((2 * p + i) * 128 + 64, 64) for i in range(2)]),
        cols(wm, D + 32 + p * P, P)] for p in range(PAIRS)])
    w["w_mla_out"] = outs(inp["mla_w_o_2"][0])
    kv, wi = inp["moba_w_kv_2"], inp["moba_w_in_2"][0]
    w["w_moba"] = units([[cols(wi, p * P, P), cols(kv, p * P, P), cols(kv, D + p * P, P), cols(wi, D + p * P, P)]
                         for p in range(PAIRS)])
    w["w_moba_out"] = outs(inp["moba_w_o_2"][0])

    where, width = param_columns()
    par = np.zeros((P, width), f32)

    def put(name, a, r0=0):
        at, n = where[name]
        a = a.reshape(a.shape[0], -1)
        assert a.shape[1] == n, (name, a.shape, n)
        par[r0:r0 + a.shape[0], at:at + n] = a

    for name, src in (("mix_pre", "norm_mix_pre"), ("mix_post", "norm_mix_post"), ("ffn_pre", "norm_ffn_pre"),
                      ("ffn_post", "norm_ffn_post"), ("ln_g", "ln_g_2"), ("ln_b", "ln_b_2")):
        put(name, inp[src].reshape(2, KT, P).transpose(2, 0, 1))
    put("q_gain", np.tile(inp["attn_q_norm"][0], 2)[:, None])
    put("k_gain", np.tile(inp["attn_k_norm"][0], 2)[:, None])
    put("b_forget", inp["attn_b_forget"][0][:, None])
    put("a_log", inp["dn_a_log"][0][:, None], 32)
    put("dt_bias", inp["dn_dt_bias"][0][:, None], 32)
    put("o_gain", inp["dn_o_norm"][0][:, None])
    put("q_lat", inp["mla_q_norm_2"][0].reshape(QL, P).T)
    put("kv_lat", inp["mla_kv_norm_2"][0].reshape(KVL, P).T)
    put("dn_conv", inp["dn_conv"][0].reshape(4, 3, DNH, P).transpose(3, 2, 1, 0))
    put("ffn_conv", inp["ffn_conv"].reshape(2, 3, 2, FT, P).transpose(4, 0, 3, 2, 1))
    put("w_forget", cols(wa, 4 * D, 16))
    ba = np.zeros((D, 64), f32)
    ba[:, 0:8] = wd[:, 4 * D:4 * D + 8]
    ba[:, 32:40] = wd[:, 4 * D + 8:4 * D + 16]
    put("w_beta_a", cols(ba, 0, 64))
    kr = wm[:, D:D + 32]
    put("w_k_rope", cols(np.concatenate([kr, kr], 1), 0, 64))
    return w, par


def kernel(**inputs):
    import concourse.bacc as bacc
    from concourse.bass_utils import run_bass_kernel_spmd

    inp = {k: np.asarray(v) for k, v in inputs.items()}
    w, par = lay_out(inp)
    tw = table_columns()[1]
    table = np.zeros((P, tw), np.float32)
    for name, a in tables().items():
        rows, at, n = table_columns()[0][name]
        table[0:rows, at:at + n] = a
    x = np.concatenate([inp["meta_tokens"], inp["x"][0]], 0)
    arrays = {"x": np.ascontiguousarray(x.reshape(T, KT, P).transpose(2, 1, 0)), "table": table, "params": par, **w}
    nc = bacc.Bacc("TRN2", target_bir_lowering=False, num_devices=1)
    aps = {k: nc.dram_tensor(k, v.shape, F32, kind="ExternalInput").ap() for k, v in arrays.items()}
    out = nc.dram_tensor("out", (P, KT, SEQ), F32, kind="ExternalOutput").ap()
    build(nc, aps["x"], aps["table"], aps["params"], {k: aps[k] for k in w}, out)
    r = run_bass_kernel_spmd(nc, [arrays], core_ids=[0])
    got = r.results[0]["out"]
    return np.ascontiguousarray(got.transpose(2, 1, 0)).reshape(1, SEQ, D)
```

```python
from contextlib import ExitStack

import numpy as np

import concourse.bass as bass
from concourse import mybir

F32 = mybir.dt.float32
F32R = mybir.dt.float32r
ALU = mybir.AluOpType
ACT = mybir.ActivationFunctionType
AX = mybir.AxisListType.X

P = 128
D = 1024
KT = D // P
META = 16
SEQ = 256
T = META + SEQ
CONV_PAST = 2
FFN = 2816
FT = FFN // P
PAIRS = 8
DNH = 8
C = 96
NC = 3
TP = C * NC
PAD = TP - T
LEVELS = 7
CHUNK = 8 * P
NEG = -1e30
ALPHA = 4 ** 0.25
RMS_EPS = 1e-6
LN_EPS = 1e-5
QL, KVL = 6, 2

BLK_A = [(0, META), (META, META + P), (META + P, T)]
BLK_B = [(META, META + P), (META + P, T)]


def tables():
    t = {}
    t["ident"] = np.eye(P)
    t["ones"] = np.ones((P, P))
    t["head_ones"] = np.kron(np.eye(2), np.ones((64, 64)))

    def rot(dim, copies):
        m = np.zeros((dim, dim))
        for d in range(dim // 2):
            m[d + dim // 2, d] = -1.0
            m[d, d + dim // 2] = 1.0
        return np.kron(np.eye(copies), m)

    t["rot64"] = rot(64, 2)
    t["rot32"] = rot(32, 2)

    def angles(dim):
        inv = (np.float32(10000.0) ** (-np.arange(0, dim, 2, dtype=np.float32) / np.float32(dim))).astype(np.float32)
        a = np.arange(SEQ, dtype=np.float32)[:, None] * inv[None, :]
        a = np.concatenate([a, a], -1).T
        return np.concatenate([a, a], 0)

    t["cos64"], t["sin64"] = np.cos(angles(64)), np.sin(angles(64))
    t["cos32"], t["sin32"] = np.cos(angles(32)), np.sin(angles(32))

    def causal(blocks):
        parts = []
        for q0, q1 in blocks:
            q = np.arange(q0, q0 + P)[:, None]
            k = np.arange(blocks[0][0], q1)[None, :]
            parts.append(np.where(k <= q, 0.0, NEG))
        return np.concatenate(parts, 1)

    t["mask_a"] = causal(BLK_A)
    t["mask_b"] = causal(BLK_B)
    j, i = np.arange(C)[:, None], np.arange(C)[None, :]
    t["later"] = np.where(i >= j, 0.0, NEG)
    t["strict"] = (i > j) * 1.0
    lev = [((i // (2 * b) == j // (2 * b)) & (j % (2 * b) < b) & (i % (2 * b) >= b)) * 1.0
           for b in (1 << n for n in range(LEVELS))]
    t["levels"] = np.concatenate(lev, 1)
    t["ident_c"] = np.eye(C)
    sel = np.zeros((P, P))
    sel[32:40] = sel[96:104] = 1.0
    t["sum_gc"] = sel
    sel = np.zeros((P, C))
    sel[0:8] = sel[64:72] = 1.0
    t["sum_beta"] = sel
    own = np.zeros((P, DNH))
    for r0 in (0, 32, 64, 96):
        own[r0 + np.arange(8), np.arange(8)] = 1.0
    t["own_head"] = own
    t["own_head_a"] = np.kron(np.array([[1.0], [0.0], [1.0]] + [[0.0]] * 5), np.eye(16))
    t["rms_eps"] = np.full((P, 1), RMS_EPS)
    t["ln_eps"] = np.full((P, 1), LN_EPS)
    return t


def table_columns():
    at, where = 0, {}
    for name, a in tables().items():
        where[name] = (a.shape[0], at, a.shape[1])
        at += a.shape[1]
    return where, at


PARAMS = [("mix_pre", 2 * KT), ("mix_post", 2 * KT), ("ffn_pre", 2 * KT), ("ffn_post", 2 * KT),
          ("q_gain", 1), ("k_gain", 1), ("b_forget", 1), ("a_log", 1), ("dt_bias", 1), ("o_gain", 1),
          ("q_lat", QL), ("kv_lat", KVL), ("ln_g", 2 * KT), ("ln_b", 2 * KT),
          ("dn_conv", DNH * 3 * 4), ("ffn_conv", 2 * FT * 2 * 3)]


def param_columns():
    at, where = 0, {}
    for name, n in PARAMS:
        where[name] = (at, n)
        at += n
    return where, at


CHUNKS = {"attn": [8 * P] * 4, "out": [8 * P] * 4, "up": [8 * P] * 4, "down": [6 * P, 6 * P, 5 * P, 5 * P],
          "mla": [QL * P, (QL + 1) * 64, 2 * KVL * P, 8 * P], "s16": [2 * 16 + 112] * 4, "s64": [2 * 64 + 64] * 4}
STREAM = [("w_forget", "s16", 1), ("w_attn", "attn", PAIRS), ("w_attn_out", "out", 2), ("w_up0", "up", FT // 2),
          ("w_down0", "down", KT), ("w_beta_a", "s64", 1), ("w_dn", "attn", DNH), ("w_dn_out", "out", 2),
          ("w_up1", "up", FT // 2), ("w_down1", "down", KT), ("w_latent", "out", 2), ("w_k_rope", "s64", 1),
          ("w_mla", "mla", PAIRS), ("w_mla_out", "out", 2), ("w_moba", "attn", PAIRS), ("w_moba_out", "out", 2)]
KIND = {name: kind for name, kind, _ in STREAM}
UNITS = {name: n for name, _, n in STREAM}
NEXT = {a[0]: b[0] for a, b in zip(STREAM, STREAM[1:])}


class Steps:

    def __init__(self, eng, sem):
        self.eng, self.sem, self.base, self.n = eng, sem, 0, 0

    def __call__(self, ins):
        ins.then_inc(self.sem, 1)
        self.n += 1
        return self.n

    def settle(self, upto=None):
        self.eng.wait_ge(self.sem, self.base + (self.n if upto is None else upto))

    def loop(self, start, stop, per, body):
        before = self.base + self.n
        with self.eng.Fori(start, stop) as i:
            self.base, self.n = (i - start) * per + before, 0
            body(i)
            assert self.n == per, (self.n, per)
        self.base, self.n = 0, before + (stop - start) * per


def wait(eng, sem, value):
    if not isinstance(value, int) or value > 0:
        eng.wait_ge(sem, value)


def build(nc, x, table, params, w, out):
    tcol, tw = table_columns()
    pcol, pw = param_columns()
    unit0, at = {}, 0
    for name, kind, n in STREAM:
        unit0[name] = at
        at += n
    ctx = ExitStack()
    with ctx:
        def sb(name, shape, rows=P):
            return ctx.enter_context(nc.sbuf_tensor(name, [rows, *shape], F32))

        def sem(name):
            return ctx.enter_context(nc.semaphore(name))

        bank = [ctx.enter_context(nc.psum_tensor(f"bank{i}", [P, 512], F32)) for i in range(8)]
        ARENA = 73600
        X_AT, O_AT = ARENA, ARENA + 2 * 4 * KT * T
        SLAB = O_AT + 2 * 4 * KT * T
        slab_at = (nc.sbuf_base + 63) // 64 * 64
        ctx.enter_context(nc.sbuf_tensor("slab", [P, SLAB // 4 + 16], F32))

        class Place:

            def __init__(self, at, end):
                self.at, self.end = at, end

            def __call__(self, name, shape, rows=P, dtype=F32):
                got = nc.alloc_sbuf_tensor_at(name, [rows, *shape], dtype, offset=slab_at + self.at)
                self.at += (4 * int(np.prod(shape)) + 31) // 32 * 32
                assert self.at <= self.end, (name, self.at, self.end)
                return got

        tab = sb("tab", [tw])
        par = sb("par", [pw])
        raw = sb("raw", [4, CHUNK])
        w_hi = ctx.enter_context(nc.sbuf_tensor("w_hi", [P, 4, CHUNK], F32R))
        w_lo = ctx.enter_context(nc.sbuf_tensor("w_lo", [P, 4, CHUNK], F32R))
        h = sb("h", [KT, T])
        m = sb("m", [KT, T])
        put_x, put_o = Place(X_AT, O_AT), Place(O_AT, SLAB)
        x_hi, x_lo = put_x("x_hi", [KT, T], dtype=F32R), put_x("x_lo", [KT, T], dtype=F32R)
        o_hi, o_lo = put_o("o_hi", [KT, T], dtype=F32R), put_o("o_lo", [KT, T], dtype=F32R)
        x_op, o_op = (x_hi, x_lo), (o_hi, o_lo)
        sq = sb("sq", [2, T])
        root = sb("root", [T])
        rstd = sb("rstd", [T])
        root2 = sb("root2", [T])
        rstd2 = sb("rstd2", [T])
        ones_r = ctx.enter_context(nc.sbuf_tensor("ones_r", [P, P], F32R))
        sum_gc_r = ctx.enter_context(nc.sbuf_tensor("sum_gc_r", [P, P], F32R))
        sum_beta_r = ctx.enter_context(nc.sbuf_tensor("sum_beta_r", [P, C], F32R))

        def tb(name):
            rows, at, n = tcol[name]
            return tab[0:rows, at:at + n]

        def pr(name):
            at, n = pcol[name]
            return par[:, at:at + n]

        ident, ones, head_ones = tb("ident"), tb("ones"), tb("head_ones")
        eps = {"rms": tb("rms_eps"), "ln": tb("ln_eps")}

        s_in = sem("s_in")
        loaded = [sem(f"chunk{i}_loaded") for i in range(4)]
        hi_done, lo_done, chunk_used = sem("hi_done"), sem("lo_done"), sem("chunk_used")
        xt_ready, xh_ready, x_ready, ones_ready = sem("xt_ready"), sem("xh_ready"), sem("x_ready"), sem("ones_ready")
        act_step, dve_step, pool_step = sem("act_step"), sem("dve_step"), sem("pool_step")
        sq_ready, sq_used = sem("sq_ready"), sem("sq_used")
        sum_done, root_done = sem("sum_done"), sem("root_done")
        h_ready, m_ready = sem("h_ready"), sem("m_ready")
        z_ready = sem("z_ready")
        stored = sem("stored")

        put = Place(0, ARENA)
        q_raw, k_raw = sb("q_raw", [T]), sb("k_raw", [T])
        q_sq, k_sq = sb("q_sq", [T]), sb("k_sq", [T])
        t_sin, th = sb("t_sin", [T]), sb("th", [T])
        q_n, k_n = put("q_n", [T]), put("k_n", [T])
        q_rp, k_rp = put("q_rp", [T], 64), put("k_rp", [T], 64)
        rp_raw = put("rp_raw", [T], 64)
        v_s = put("v_s", [3, P])
        gate, o_tmp = put("gate", [T]), put("o_tmp", [T])
        s_m = put("s_m", [2, 432])
        p_e = put("p_e", [2, 432])
        mx, rs, ri = put("mx", [2, 3]), put("rs", [2, 3]), put("ri", [2, 3])
        pt = put("pt", [2, 384])
        pt0 = put("pt0", [2, T], META)
        rest = put.at
        rows_a = put("rows_a", [16, T], P, F32R)
        c_2 = put("c_2", [T])
        put.at = rest
        lat_op = put("lat_hi", [KT, T], dtype=F32R), put("lat_lo", [KT, T], dtype=F32R)
        kr_raw, kr_cos, kr_sin = (put(n, [SEQ], 64) for n in ("kr_raw", "kr_cos", "kr_sin"))

        q_copied, k_copied = sem("q_copied"), sem("k_copied")
        q_side, k_side = sem("q_side"), sem("k_side")
        qk_root = sem("qk_root")
        q_ready, k_ready, v_ready, gate_ready, th_ready = (sem(n) for n in (
            "q_ready", "k_ready", "v_ready", "gate_ready", "th_ready"))
        o_ready, lat_ready, lat_hi_ready, lat_t = sem("o_ready"), sem("lat_ready"), sem("lat_hi_ready"), sem("lat_t")
        s_done, s_taken, max_ready, exp_done, p_ready = (sem(n) for n in (
            "s_done", "s_taken", "max_ready", "exp_done", "p_ready"))
        pt_done, pt_taken, o_done, o_taken = (sem(n) for n in ("pt_done", "pt_taken", "o_done", "o_taken"))
        small_done, rows_ready, kr_seen, kr_rot, kr_ready = (sem(n) for n in (
            "small_done", "rows_ready", "kr_seen", "kr_rot", "kr_ready"))
        z_known, ln_done = sem("z_known"), sem("ln_done")

        put = Place(0, ARENA)
        hid_op = put("hid_hi", [FT, T], dtype=F32R), put("hid_lo", [FT, T], dtype=F32R)
        g_y, u_y, g_e, hid = (put(n, [2, T]) for n in ("g_y", "u_y", "g_e", "hid"))
        prod_ready, hid_hi_ready = sem("prod_ready"), sem("hid_hi_ready")
        tap_ready, conv_done, gelu_done, hid_ready = (sem(n) for n in (
            "tap_ready", "conv_done", "gelu_done", "hid_ready"))

        put = Place(0, ARENA)
        rows_d = put("rows_d", [DNH, TP], dtype=F32R)
        put.at = 0
        d_in = put("d_in", [DNH, TP], C)
        stage_at = put.at
        q_st, k_st, v_st = put("q_st", [TP]), put("k_st", [TP]), put("v_st", [TP])
        e_row = put("e_row", [TP])
        t_dec, dec = put("t_dec", [TP], C), put("dec", [TP], C)
        at_1, at_2 = put("at_1", [TP], C), put("at_2", [TP], C)
        put.at = stage_at
        d_tr = put("d_tr", [DNH, TP], C)
        a_tr = put("a_tr", [DNH, TP], C)
        kn_all, qd_all = put("kn_all", [DNH, TP]), put("qd_all", [DNH, TP])
        qk_all = put("qk_all", [DNH, TP], C)
        vb_all = put("vb_all", [DNH, NC, P], C)
        bg = put("bg", [TP])
        bg_t = put("bg_t", [NC, 64], C)
        eg_t, nbz = put("eg_t", [NC, DNH], C), put("nbz", [NC, DNH], C)
        g_last = put("g_last", [DNH, NC])
        put_o.at = O_AT
        kd_all = put_o("kd_all", [DNH, NC, P], C)
        put_x.at = X_AT
        l_st, x_st = put_x("l_st", [2, TP], C), put_x("x_st", [2, TP], C)
        s_t = put_x("s_t", [DNH, P])
        r_st, u_st = put_x("r_st", [2, P], C), put_x("u_st", [2, P], C)
        o_gate = m
        q_y, k_y, v_y = q_raw, k_raw, th
        neg_a = sb("neg_a", [1], 64)
        o_raw = kn_all
        sp_a, sp_b, sp_c = sb("sp_a", [T], 64), sb("sp_b", [T], 64), sb("sp_c", [T], 64)
        dn = {n: sem("dn_" + n) for n in (
            "tap", "conv", "sq", "ssq", "root", "st", "v_st", "gate", "row", "vt", "vt_out", "kk", "kt",
            "kt_out", "beta", "dec_t", "dec", "erow", "a1", "a2", "at", "qk", "qd", "kcopy", "prep", "bg", "bgt",
            "init", "l", "x", "x_out", "dd", "d", "ks", "r", "u", "u_out", "o", "o_out", "s_up", "s_new",
            "osq", "osum", "oroot", "zero", "negexp", "bgt_out", "eg", "ot")}

        block = ctx.enter_context(nc.Block())

        out_names = [n for n, kind, _ in STREAM if kind in ("out", "down")]
        out_stage = {n: i for i, n in enumerate(out_names)}

        def chunk(name, u, q):
            return u * 4 + (4 * unit0[name] + q)

        def chunk_width(name, q):
            return CHUNKS[KIND[name]][q]

        def split_hi(act, name, u, q):
            n, wd = chunk(name, u, q), chunk_width(name, q)
            act.wait_ge(loaded[q], u * 16 + 16 * (unit0[name] + 1))
            if unit0[name] or not isinstance(u, int) or u:
                act.wait_ge(chunk_used, n - 3)
            nc.scalar.activation(w_hi[:, q, 0:wd], raw[:, q, 0:wd], ACT.Copy).then_inc(hi_done, 1)

        def split_lo(dve, name, u, q):
            n, wd = chunk(name, u, q), chunk_width(name, q)
            dve.wait_ge(hi_done, n + 1)
            nc.vector.tensor_tensor(w_lo[:, q, 0:wd], raw[:, q, 0:wd], w_hi[:, q, 0:wd].bitcast(F32),
                                    ALU.subtract).then_inc(lo_done, 1)

        def following(name, u):
            if isinstance(u, int) and u == UNITS[name] - 1:
                return (NEXT[name], 0) if name in NEXT else None
            return name, u + 1

        def weights_here(pe, name, u, q):
            pe.wait_ge(lo_done, chunk(name, u, q) + 1)

        def product(dst, q, w0, src, k, cols, first, last, m_cols=P):
            c0, c1 = cols
            hi, lo = w_hi[:, q, w0:w0 + m_cols], w_lo[:, q, w0:w0 + m_cols]
            nc.tensor.matmul(dst, hi, src[0][:, k, c0:c1], start=first, stop=False)
            nc.tensor.matmul(dst, hi, src[1][:, k, c0:c1], start=False, stop=False)
            return nc.tensor.matmul(dst, lo, src[0][:, k, c0:c1], start=False, stop=last)

        @block.sync
        def _(sp):
            sp.dma_start(h[:], x).then_inc(s_in, 16)
            sp.dma_start(par[:], params).then_inc(s_in, 16)
            sp.dma_start(tab[:], table).then_inc(s_in, 16)
            for name, kind, n in STREAM:
                def load(u):
                    w0 = 0
                    for q in range(4):
                        wd = chunk_width(name, q)
                        if unit0[name] or not isinstance(u, int) or u:
                            sp.wait_ge(lo_done, chunk(name, u, q) - 3)
                        sp.dma_start(raw[:, q, 0:wd], w[name][u][:, w0:w0 + wd]).then_inc(loaded[q], 16)
                        w0 += wd

                load(0)
                if n > 1:
                    with sp.Fori(1, n) as u:
                        load(u)
            sp.wait_ge(h_ready, 6 * KT)
            sp.dma_start(out, h[:, :, META:T]).then_inc(stored, 16)
            sp.wait_ge(stored, 16)

        REDUCE = ([(f"pre{i}", KT) if k % 2 == 0 else (f"post{i}", KT) for i in range(4) for k in (0, 1)]
                  + [("lat_q", QL), ("lat_kv", KVL), ("var1", KT), ("var2", KT)])
        sq0, red_no, tot = {}, {}, 0
        for n_, (name, tiles) in enumerate(REDUCE):
            sq0[name], red_no[name] = tot, n_
            tot += tiles
        sum_order = [n for n, _ in REDUCE[:10]] + ["mean1", "var1", "mean2", "var2"]
        sum_no = {n: i + 1 for i, n in enumerate(sum_order)}
        root_no = {n: i + 1 for i, (n, _) in enumerate(REDUCE)}
        H_AFTER = {"post0": 8, "post1": 16, "post2": 24, "post3": 32, "ln1": 40, "ln2": 48}

        def square(act, src, name, j, cols):
            n = sq0[name] + j
            wait(act, sq_used, n - 1)
            par2 = (sq0[name] + (j if isinstance(j, int) else 0)) % 2
            nc.scalar.activation(sq[:, par2, cols[0]:cols[1]], src, ACT.Square).then_inc(sq_ready, 1)

        def sum_tile(pe, name, j, tiles, cols, static_j=None, where=7):
            n = sq0[name] + j
            pe.wait_ge(sq_ready, n + 1)
            sj = j if static_j is None else static_j
            first = static_j is None and j == 0
            last = static_j is None and j == tiles - 1
            mm = nc.tensor.matmul(bank[where][:, cols[0]:cols[1]], ones, sq[:, (sq0[name] + sj) % 2, cols[0]:cols[1]],
                                  start=first, stop=last)
            mm.then_inc(sq_used, 1)

        def rms_root(act, name, count, cols, dst, where=7, e="rms"):
            act.wait_ge(sq_used, sq0[name] + dict(REDUCE)[name])
            nc.scalar.activation(dst[:, cols[0]:cols[1]], bank[where][:, cols[0]:cols[1]], ACT.Sqrt,
                                 bias=eps[e], scale=1.0 / count).then_inc(root_done, 1)

        def invert_root(dve, st, name, cols, src, dst):
            dve.wait_ge(root_done, root_no[name])
            st(nc.vector.reciprocal(dst[:, cols[0]:cols[1]], src[:, cols[0]:cols[1]]))
            st.settle()

        def pre_norm_act(act, name, cols, h_base):
            for j in range(KT):
                if h_base is None:
                    if j == 0:
                        act.wait_ge(s_in, 48)
                else:
                    act.wait_ge(h_ready, h_base + j + 1)
                square(act, h[:, j, cols[0]:cols[1]], name, j, cols)
            rms_root(act, name, D, cols, root)
            x_split_act(act, m, cols, KT * int(name[3]), (xt_ready, KT * int(name[3])))

        def sums_pe(pe, name, tiles, cols, where=7):
            for j in range(tiles):
                sum_tile(pe, name, j, tiles, cols, where=where)

        def x_split_act(act, src, cols, base, ready):
            for j in range(KT):
                act.wait_ge(ready[0], ready[1] + j + 1)
                nc.scalar.activation(x_hi[:, j, cols[0]:cols[1]], src[:, j, cols[0]:cols[1]], ACT.Copy).then_inc(xh_ready, 1)

        def x_split_dve(dve, src, cols, base, j):
            dve.wait_ge(xh_ready, base + j + 1)
            nc.vector.tensor_tensor(x_lo[:, j, cols[0]:cols[1]], src[:, j, cols[0]:cols[1]],
                                    x_hi[:, j, cols[0]:cols[1]].bitcast(F32), ALU.subtract).then_inc(x_ready, 1)

        def pre_norm_dve(dve, st, name, gain, cols):
            invert_root(dve, st, name, cols, root, rstd)
            base = KT * int(name[3])
            for j in range(KT + 1):
                if j < KT:
                    nc.vector.scalar_tensor_tensor(m[:, j, cols[0]:cols[1]], h[:, j, cols[0]:cols[1]], gain[:, j:j + 1],
                                                   rstd[:, cols[0]:cols[1]], ALU.mult, ALU.mult).then_inc(xt_ready, 1)
                if j:
                    x_split_dve(dve, m, cols, base, j - 1)

        def post_norm_dve(dve, st, name, gain, cols):
            invert_root(dve, st, name, cols, root, rstd)
            c0, c1 = cols
            marks = []
            for j in range(KT + 2):
                if j < KT:
                    marks.append(st(nc.vector.scalar_tensor_tensor(
                        m[:, j, c0:c1], m[:, j, c0:c1], gain[:, j:j + 1], rstd[:, c0:c1], ALU.mult, ALU.mult)))
                if j >= 2:
                    st.settle(marks[j - 2])
                    nc.vector.tensor_tensor(h[:, j - 2, c0:c1], h[:, j - 2, c0:c1], m[:, j - 2, c0:c1],
                                            ALU.add).then_inc(h_ready, 1)

        def out_pe(pe, wname, norm, src, src_tiles, cols, first_wait, mean=False):
            down = src_tiles == FT
            b_out = 4 if down else 0
            c0, c1 = cols

            def tile(j, jr):
                if jr >= 2 or not isinstance(j, int):
                    pe.wait_ge(z_ready if mean else sq_ready, (ZB[wname] if mean else sq0[norm]) + j - 1)
                k = 0
                for q in (range(4) if down else (jr % 4,)):
                    weights_here(pe, wname, j if down else jr // 4, q)
                    for t_ in range(chunk_width(wname, q) // P):
                        if isinstance(j, int) and j == 0:
                            first_wait(pe, k)
                        mm = product(bank[b_out + jr % 2][:, c0:c1], q, t_ * P, src, k, cols, k == 0, k == src_tiles - 1)
                        k += 1
                    mm.then_inc(chunk_used, 1)

            def add(j, static=None):
                if mean:
                    pe.wait_ge(z_ready, ZB[wname] + j + 1)
                    mm = nc.tensor.matmul(bank[7][:, c0:c1], ones, m[:, j, c0:c1], start=j == 0, stop=j == KT - 1)
                    if j == KT - 1:
                        mm.then_inc(sum_done, 1)
                else:
                    sum_tile(pe, norm, j, KT, cols, static_j=static)

            if down:
                tile(0, 0)
                tile(1, 1)
                add(0)
                with pe.Fori(1, KT // 2) as i:
                    for r in range(2):
                        tile(i * 2 + r, r)
                        add(i * 2 + (r - 1), static=(r - 1) % 2)
                add(KT - 1)
            else:
                for j in range(KT):
                    tile(j, j)
                    if j:
                        add(j - 1)
                add(KT - 1)

        ZB = {"w_mla_out": 0, "w_moba_out": 8}

        def out_tile_done(wname, j):
            if KIND[wname] == "down":
                return chunk(wname, j, 3) + 1
            return chunk(wname, j // 4, j % 4) + 1 if isinstance(j, int) else chunk(wname, 0, 0) + j + 1

        def out_splits(eng, split, wname):
            def step(j):
                if KIND[wname] == "down":
                    f_ = following(wname, j)
                    for q in range(4):
                        split(eng, *f_, q)
                elif isinstance(j, int):
                    f_ = following(wname, j // 4)
                    if f_:
                        split(eng, *f_, j % 4)
            return step

        def out_act(act, wname, norm, cols):
            b_out = 4 if "down" in wname else 0
            c0, c1 = cols
            split = out_splits(act, split_hi, wname)

            def tile(j, r):
                if KIND[wname] == "down":
                    split(j)
                act.wait_ge(chunk_used, out_tile_done(wname, j))
                nc.scalar.activation(m[:, j, c0:c1], bank[b_out + r][:, c0:c1], ACT.Copy).then_inc(m_ready, 1)
                n = j + sq0[norm]
                wait(act, sq_used, n - 1)
                nc.scalar.activation(sq[:, (sq0[norm] + r) % 2, c0:c1], bank[b_out + r][:, c0:c1], ACT.Square).then_inc(sq_ready, 1)
                if KIND[wname] != "down":
                    split(j)

            tile(0, 0)
            tile(1, 1)
            if KIND[wname] == "down":
                with act.Fori(1, KT // 2 - 1) as i:
                    for r in range(2):
                        tile(i * 2 + r, r)
                tile(KT - 2, 0)
                tile(KT - 1, 1)
            else:
                for j in range(2, KT):
                    tile(j, j % 2)
            rms_root(act, norm, D, cols, root)

        def out_dve(dve, wname):
            split = out_splits(dve, split_lo, wname)
            if KIND[wname] == "down":
                with dve.Fori(0, KT - 1) as j:
                    split(j)
                split(KT - 1)
            else:
                for j in range(KT):
                    split(j)

        def ln_dve(dve, st, wname, n_ln):
            split = out_splits(dve, split_lo, wname)
            c0, c1 = META, T
            for j in range(KT):
                dve.wait_ge(chunk_used, out_tile_done(wname, j))
                nc.vector.scalar_tensor_tensor(m[:, j, c0:c1], h[:, j, c0:c1], ALPHA, bank[j % 2][:, c0:c1],
                                               ALU.mult, ALU.add).then_inc(z_ready, 1)
                split(j)
            dve.wait_ge(sum_done, n_ln)
            st(nc.vector.tensor_scalar(root2[:, c0:c1], bank[7][:, c0:c1], 1.0 / D, None, ALU.mult))
            st.settle()
            dve.wait_ge(z_ready, ZB[wname] + KT)
            for j in range(KT):
                nc.vector.tensor_tensor(m[:, j, c0:c1], m[:, j, c0:c1], root2[:, c0:c1],
                                        ALU.subtract).then_inc(m_ready, 1)
            invert_root(dve, st, f"var{n_ln}", (c0, c1), root, rstd)
            dve.wait_ge(m_ready, MB_LN[n_ln] + KT)
            g0 = (n_ln - 1) * KT
            for j in range(KT):
                st(nc.vector.scalar_tensor_tensor(m[:, j, c0:c1], m[:, j, c0:c1], pr("ln_g")[:, g0 + j:g0 + j + 1],
                                                  rstd[:, c0:c1], ALU.mult, ALU.mult))
            st.settle()
            for j in range(KT):
                nc.vector.tensor_scalar(h[:, j, c0:c1], m[:, j, c0:c1], pr("ln_b")[:, g0 + j:g0 + j + 1], None,
                                        ALU.add).then_inc(h_ready, 1)

        MB_LN = {1: 4 * KT, 2: 5 * KT}

        def ln_act(act, wname, n_ln):
            c0, c1 = META, T
            split = out_splits(act, split_hi, wname)
            for j in range(KT):
                split(j)
            for j in range(KT):
                act.wait_ge(m_ready, MB_LN[n_ln] + j + 1)
                square(act, m[:, j, c0:c1], f"var{n_ln}", j, (c0, c1))
            rms_root(act, f"var{n_ln}", D, (c0, c1), root, e="ln")

        SCALE = {0: 0.125, 1: 96 ** -0.5, 2: 0.125}

        def blocks(f):
            return BLK_A if f == 0 else BLK_B

        def span(f):
            return (0, T) if f == 0 else (META, T)

        def s_cols(f):
            at, res = 0, []
            for q0, q1 in blocks(f):
                n = q1 - blocks(f)[0][0]
                res.append((at, at + n))
                at += n
            return res

        def name_of(f):
            return ("w_attn", "w_mla", "w_moba")[f]

        def projected(f, p, which):
            q = {"q": (0, 1, 0), "k": (1, 2, 1), "v": (2, 2, 2), "g": (3, 3, 3)}[which][f]
            return chunk(name_of(f), p, q) + 1

        def pe_project(pe, f, p, aw):
            name = name_of(f)
            g = p + 8 * f
            cols = c0, c1 = span(f)
            src = {s: (q, 0, x_op, 0, KT) for q, s in enumerate("qkvg")}
            if f == 1:
                src = {"q": (0, 0, lat_op, 0, QL), "r": (1, 0, lat_op, 0, QL), "k": (2, 0, lat_op, QL, KVL),
                       "v": (2, KVL * P, lat_op, QL, KVL), "g": (3, 0, x_op, 0, KT)}

            def feature(s, dst, width=P, part=None):
                q, w0, op, t0, n = src[s]
                weights_here(pe, name, p, q)
                for k in part or range(n):
                    if s == "q" and isinstance(p, int) and p == 0:
                        aw(pe, k)
                    mm = product(dst, q, w0 + k * width, op, t0 + k, cols, k == 0, k == n - 1)
                return mm

            def queries():
                wait(pe, q_ready, g)
                feature("q", bank[0][:, 0:c1 - c0]).then_inc(chunk_used, 1)

            def keys():
                if f == 1:
                    feature("r", bank[0][:, 256:512], 64).then_inc(chunk_used, 1)
                wait(pe, k_ready, g)
                mm = feature("k", bank[1][:, 0:c1 - c0])
                if f != 1:
                    mm.then_inc(chunk_used, 1)

            def sides():
                n = c1 - c0
                if f != 1:
                    pe.wait_ge(q_copied, g + 1)
                k_seen = g + 1 if f == 0 else p + 9
                if f == 0:
                    nc.tensor.matmul(bank[0][:, 0:n], head_ones, q_sq[:, 0:n], start=True, stop=True).then_inc(q_side, 1)
                    pe.wait_ge(k_copied, k_seen)
                    nc.tensor.matmul(bank[1][:, 0:n], head_ones, k_sq[:, 0:n], start=True, stop=True).then_inc(k_side, 1)
                elif f == 1:
                    nc.tensor.matmul(bank[0][0:64, 256:512], tb("rot32"), rp_raw[:, 0:n], start=True, stop=True).then_inc(q_side, 1)
                else:
                    nc.tensor.matmul(bank[0][:, 0:n], tb("rot64"), q_raw[:, 0:n], start=True, stop=True).then_inc(q_side, 1)
                    pe.wait_ge(k_copied, k_seen)
                    nc.tensor.matmul(bank[1][:, 0:n], tb("rot64"), k_raw[:, 0:n], start=True, stop=True).then_inc(k_side, 1)

            def values():
                wait(pe, v_ready, g)
                q, w0, op, t0, n = src["v"]
                weights_here(pe, name, p, q)
                for b, (b0, b1) in enumerate(blocks(f)):
                    if f == 1 and b == 1:
                        pe.wait_ge(q_copied, g + 1)
                    dst = bank[2][:, b * P:(b + 1) * P]
                    for k in range(n):
                        hi, lo = (t_[:, t0 + k, b0:b0 + P] for t_ in op)
                        wk = slice(w0 + k * P, w0 + (k + 1) * P)
                        nc.tensor.matmul(dst, hi, w_hi[:, q, wk], start=k == 0, stop=False)
                        nc.tensor.matmul(dst, hi, w_lo[:, q, wk], start=False, stop=False)
                        mm = nc.tensor.matmul(dst, lo, w_hi[:, q, wk], start=False, stop=k == n - 1)
                mm.then_inc(chunk_used, 1)

            def gates(part=range(KT)):
                if 0 in part:
                    wait(pe, gate_ready, g)
                mm = feature("g", bank[3][:, 0:c1 - c0], part=part)
                if KT - 1 in part:
                    mm.then_inc(chunk_used, 1)

            return queries, keys, sides, values, gates

        def pe_scores(pe, f, p):
            g = p + 8 * f
            c0, c1 = span(f)
            pe.wait_ge(q_ready, g + 1)
            pe.wait_ge(k_ready, g + 1)
            wait(pe, o_taken, g)
            wait(pe, pt_taken, 2 * g)
            for hh in range(2):
                dst = bank[5 - hh]
                r = slice(64 * hh, 64 * hh + 64)
                for (q0, q1), (s0, s1) in zip(blocks(f), s_cols(f)):
                    n = s1 - s0
                    mm = nc.tensor.matmul(dst[:, s0:s1], q_n[r, q0 - c0:q0 - c0 + P], k_n[r, 0:n],
                                          start=True, stop=f == 2)
                    if f == 0:
                        mm = nc.tensor.matmul(dst[:, s0:s1], ones_r[:], rows_a[:, p * 2 + hh, 0:n],
                                              start=False, stop=True)
                    if f == 1:
                        r2 = slice(32 * hh, 32 * hh + 32)
                        mm = nc.tensor.matmul(dst[0:q1 - q0, s0:s1], q_rp[r2, q0 - c0:q1 - c0], k_rp[r2, 0:n],
                                              start=False, stop=True)
                mm.then_inc(s_done, 1)

        def pe_transposes(pe, f, p):
            g = p + 8 * f
            sc = s_cols(f)
            for hh in range(2):
                pe.wait_ge(p_ready, 2 * g + hh + 1)
                dst = (bank[6], bank[4])[hh]
                if f == 0:
                    lay = [(1, META, META + P, 0), (2, META, META + P, P), (2, META + P, T, 2 * P)]
                else:
                    lay = [(0, 0, P, 0), (1, 0, P, P), (1, P, 2 * P, 2 * P)]
                for b, k0, k1, at in lay:
                    mm = nc.tensor.transpose(dst[0:P, at:at + P], p_e[0:P, hh, sc[b][0] + k0:sc[b][0] + k1], ident)
                if f == 0:
                    for b in (1, 2):
                        mm = nc.tensor.transpose(bank[7][0:META, 256 * hh + (b - 1) * P:256 * hh + b * P],
                                                 p_e[0:P, hh, sc[b][0]:sc[b][0] + META], ident)
                    mm = nc.tensor.transpose(dst[0:META, 384:384 + META], p_e[0:META, hh, 0:META], ident[0:META, 0:META])
                mm.then_inc(pt_done, 1)

        def pe_outputs(pe, f, p):
            g = p + 8 * f
            pe.wait_ge(v_ready, g + 1)
            pe.wait_ge(pt_taken, 2 * g + 2)
            for hh in range(2):
                dst = bank[5][64 * hh:64 * hh + 64]
                vr = slice(64 * hh, 64 * hh + 64)
                if f == 0:
                    nc.tensor.matmul(dst[:, 0:T], v_s[0:META, 0, vr], pt0[:, hh, :], start=True, stop=False)
                    nc.tensor.matmul(dst[:, META:T], v_s[:, 1, vr], pt[:, hh, 0:256], start=False, stop=False)
                    mm = nc.tensor.matmul(dst[:, META + P:T], v_s[:, 2, vr], pt[:, hh, 256:384], start=False, stop=True)
                else:
                    nc.tensor.matmul(dst[:, 0:256], v_s[:, 0, vr], pt[:, hh, 0:256], start=True, stop=False)
                    mm = nc.tensor.matmul(dst[:, 128:256], v_s[:, 1, vr], pt[:, hh, 256:384], start=False, stop=True)
            mm.then_inc(o_done, 1)

        def attention_pe(pe, f):
            def aw(pe_, k):
                if f == 1 and k == 0:
                    pe_.wait_ge(lat_ready, KT)
                elif f == 2:
                    pe_.wait_ge(x_ready, X_BASE["ln1"] + k + 1)

            def step(p):
                first = isinstance(p, int) and p == 0
                queries, keys, sides, values, gates = pe_project(pe, f, p, aw)
                queries()
                if not first:
                    pe_scores(pe, f, p - 1)
                keys()
                values()
                sides()
                before = KT // 2 if f == 1 else 0
                if before:
                    gates(range(before))
                if not first:
                    pe_transposes(pe, f, p - 1)
                gates(range(before, KT))
                if not first:
                    pe_outputs(pe, f, p - 1)

            step(0)
            if f == 0:
                pe.wait_ge(rows_ready, 1)
            elif f == 1:
                pe.wait_ge(kr_ready, 1)
            step(1)
            with pe.Fori(2, PAIRS) as p:
                step(p)
            pe_scores(pe, f, PAIRS - 1)
            pe_transposes(pe, f, PAIRS - 1)
            pe_outputs(pe, f, PAIRS - 1)

        X_BASE = {"pre0": 0, "pre1": 8, "pre2": 16, "pre3": 24, "post3": 32, "ln1": 40}

        def small_pe(pe, name, dst, width):
            for q in range(4):
                weights_here(pe, name, 0, q)
                for t_ in range(2):
                    k = 2 * q + t_
                    pe.wait_ge(x_ready, {"w_forget": X_BASE["pre0"], "w_beta_a": X_BASE["pre2"],
                                         "w_k_rope": X_BASE["post3"]}[name] + k + 1)
                    mm = product(dst, q, t_ * width, x_op, k, (META, T) if name == "w_k_rope" else (0, T),
                                 k == 0, k == KT - 1)
                mm.then_inc(chunk_used, 1)

        def small_splits(eng, split, name):
            f_ = following(name, 0)
            for q in range(4):
                split(eng, *f_, q)

        def attention_act(act, st, f):
            c0, c1 = span(f)
            n = c1 - c0

            def copy_q(p):
                g = p + 8 * f
                if f == 1:
                    if not (isinstance(p, int) and p == 0):
                        act.wait_ge(s_done, 2 * g)
                    act.wait_ge(chunk_used, projected(f, p, "q"))
                    st(nc.scalar.activation(q_n[:, 0:n], bank[0][:, 0:n], ACT.Copy))
                    nc.scalar.activation(rp_raw[:, 0:n], bank[0][0:64, 256:512], ACT.Copy).then_inc(q_copied, 1)
                    return
                act.wait_ge(chunk_used, projected(f, p, "q"))
                if f == 0:
                    st(nc.scalar.activation(q_raw[:, 0:n], bank[0][:, 0:n], ACT.Copy))
                    nc.scalar.activation(q_sq[:, 0:n], bank[0][:, 0:n], ACT.Square).then_inc(q_copied, 1)
                else:
                    nc.scalar.activation(q_raw[:, 0:n], bank[0][:, 0:n], ACT.Copy).then_inc(q_copied, 1)

            def copy_k(p):
                if f == 1:
                    act.wait_ge(chunk_used, projected(f, p, "k"))
                    nc.scalar.activation(k_n[:, 0:n], bank[1][:, 0:n], ACT.Copy).then_inc(k_ready, 1)
                    return
                act.wait_ge(chunk_used, projected(f, p, "k"))
                if f == 0:
                    st(nc.scalar.activation(k_raw[:, 0:n], bank[1][:, 0:n], ACT.Copy))
                    nc.scalar.activation(k_sq[:, 0:n], bank[1][:, 0:n], ACT.Square).then_inc(k_copied, 1)
                else:
                    nc.scalar.activation(k_raw[:, 0:n], bank[1][:, 0:n], ACT.Copy).then_inc(k_copied, 1)

            def roots(p):
                if f == 0:
                    g = p
                    act.wait_ge(q_side, g + 1)
                    wait(act, q_ready, g)
                    nc.scalar.activation(q_sq[:, 0:n], bank[0][:, 0:n], ACT.Sqrt, bias=eps["rms"], scale=1.0 / 64).then_inc(qk_root, 1)
                    act.wait_ge(k_side, g + 1)
                    wait(act, k_ready, g)
                    nc.scalar.activation(k_sq[:, 0:n], bank[1][:, 0:n], ACT.Sqrt, bias=eps["rms"], scale=1.0 / 64).then_inc(qk_root, 1)

            def exps(p):
                g = p + 8 * f
                for hh in range(2):
                    act.wait_ge(max_ready, 2 * g + hh + 1)
                    bl = list(enumerate(zip(blocks(f), s_cols(f))))
                    for b, ((q0, q1), (s0, s1)) in bl:
                        r = slice(0, q1 - q0)
                        ins = nc.scalar.activation(p_e[r, hh, s0:s1], s_m[r, hh, s0:s1], ACT.Exp, bias=mx[r, hh, b:b + 1],
                                                   scale=SCALE[f], accum_out=rs[r, hh, b:b + 1])
                        if b == len(bl) - 1:
                            ins.then_inc(exp_done, 1)
                        else:
                            st(ins)

            def pt_copies(p):
                g = p + 8 * f
                for hh in range(2):
                    act.wait_ge(pt_done, 2 * g + hh + 1)
                    src = (bank[6], bank[4])[hh]
                    if f == 0:
                        nc.scalar.activation(pt0[:, hh, 0:META], src[0:META, 384:384 + META], ACT.Copy)
                        if hh:
                            nc.scalar.activation(pt0[:, :, META:T], bank[7][0:META, :].rearrange("p (h t) -> p h t", h=2),
                                                 ACT.Copy)
                    nc.scalar.activation(pt[:, hh, :], src[:, 0:384], ACT.Copy).then_inc(pt_taken, 1)

            def value_copy(p):
                g = p + 8 * f
                act.wait_ge(chunk_used, projected(f, p, "v"))
                if not (isinstance(p, int) and p == 0):
                    act.wait_ge(o_done, g)
                if f == 0:
                    nc.scalar.activation(v_s[0:META, 0, :], bank[2][0:META, 0:P], ACT.Copy)
                    nc.scalar.activation(v_s[:, 1:3, :], bank[2][:, P:3 * P], ACT.Copy).then_inc(v_ready, 1)
                else:
                    nc.scalar.activation(v_s[:, 0:2, :], bank[2][:, 0:2 * P], ACT.Copy).then_inc(v_ready, 1)
                act.wait_ge(chunk_used, projected(f, p, "g"))
                wait(act, gate_ready, g)
                nc.scalar.activation(th[:, 0:n], bank[3][:, 0:n], ACT.Tanh, scale=0.5).then_inc(th_ready, 1)

            def splits(p, qs):
                for q in qs:
                    split_hi(act, *following(name_of(f), p), q)

            copy_q(0)
            splits(0, (0,))
            copy_k(0)
            splits(0, (1, 2))
            roots(0)
            value_copy(0)
            splits(0, (3,))
            if f == 0:
                act.wait_ge(z_known, 1)
                st(nc.scalar.activation(sp_a[0:16], sp_c[0:16], ACT.Abs))
                st.settle()
                st(nc.scalar.activation(sp_b[0:16], sp_a[0:16], ACT.Exp, scale=-1.0))
                st.settle()
                nc.scalar.activation(sp_a[0:16], sp_b[0:16], ACT.Ln, bias=ones[0:16, 0:1]).then_inc(ln_done, 1)

            def step(p):
                if f == 1:
                    splits(p, (0,))
                    exps(p - 1)
                    copy_q(p)
                else:
                    copy_q(p)
                    splits(p, (0,))
                    exps(p - 1)
                copy_k(p)
                splits(p, (1, 2))
                roots(p)
                pt_copies(p - 1)
                value_copy(p)
                splits(p, (3,))

            nb = len(blocks(f)) - 1
            step(1)
            per = 2 * nb + (2 if f == 0 else 1 if f == 1 else 0)
            st.loop(2, PAIRS - 1, per, step)
            step(PAIRS - 1)
            exps(PAIRS - 1)
            pt_copies(PAIRS - 1)

        def attention_dve(dve, st, f):
            c0, c1 = span(f)
            n = c1 - c0
            sc = s_cols(f)
            mask = tb("mask_a") if f == 0 else tb("mask_b")

            def maxima(p):
                g = p + 8 * f
                for hh in range(2):
                    dve.wait_ge(s_done, 2 * g + hh + 1)
                    src = bank[5 - hh]
                    if f == 0:
                        r = slice(0, META)
                        st(nc.vector.tensor_tensor(s_m[r, hh, 0:META], src[r, 0:META], mask[r, 0:META], ALU.add))
                        lo = META
                    else:
                        lo = 0
                    hi = sc[-1][1]
                    nc.vector.tensor_tensor(s_m[:, hh, lo:hi], src[:, lo:hi], mask[:, lo:hi], ALU.add).then_inc(s_taken, 1)
                for hh in range(2):
                    dve.wait_ge(s_taken, 2 * g + hh + 1)
                    for b, ((q0, q1), (s0, s1)) in enumerate(zip(blocks(f), sc)):
                        r = slice(0, q1 - q0)
                        st(nc.vector.tensor_reduce(mx[r, hh, b:b + 1], s_m[r, hh, s0:s1], AX, ALU.max, negate=True))
                st.settle()
                for hh in range(2):
                    nc.vector.tensor_scalar(mx[:, hh, :], mx[:, hh, :], SCALE[f], None, ALU.mult).then_inc(max_ready, 1)

            def norm(p, which):
                g = p + 8 * f
                raw, t_, dst, side, ready, bk = {
                    "q": (q_raw, q_sq, q_n, q_side, q_ready, 0), "k": (k_raw, k_sq, k_n, k_side, k_ready, 1)}[which]
                if which == "q":
                    wait(dve, k_ready, g)
                elif f == 0:
                    dve.wait_ge(q_ready, g + 1)
                if f == 0:
                    dve.wait_ge(qk_root, 2 * g + (1 if which == "q" else 2))
                    st(nc.vector.reciprocal(t_sin[:, 0:n], t_[:, 0:n]))
                    st.settle()
                    gain = pr("q_gain" if which == "q" else "k_gain")
                    nc.vector.scalar_tensor_tensor(dst[:, 0:n], raw[:, 0:n], gain, t_sin[:, 0:n], ALU.mult,
                                                   ALU.mult).then_inc(ready, 1)
                    return
                if f == 1:
                    if which == "k":
                        return
                    raw, dst, src, rr = rp_raw, q_rp, bank[0][0:64, 256:512], slice(0, 64)
                    cos, sin = tb("cos32"), tb("sin32")
                else:
                    src, rr = bank[bk][:, 0:n], slice(0, P)
                    cos, sin = tb("cos64"), tb("sin64")
                dve.wait_ge(side, g + 1)
                st(nc.vector.tensor_tensor(t_sin[rr, 0:n], src, sin, ALU.mult))
                st(nc.vector.tensor_tensor(dst[rr, 0:n], raw[rr, 0:n], cos, ALU.mult))
                st.settle()
                nc.vector.tensor_tensor(dst[rr, 0:n], dst[rr, 0:n], t_sin[rr, 0:n], ALU.add).then_inc(ready, 1)

            def norm_k(p):
                if f == 2:
                    dve.wait_ge(q_ready, p + 17)
                    dve.wait_ge(k_side, p + 9)
                    st(nc.vector.tensor_tensor(t_sin[:, 0:n], bank[1][:, 0:n], tb("sin64"), ALU.mult))
                    st(nc.vector.tensor_tensor(k_n[:, 0:n], k_raw[:, 0:n], tb("cos64"), ALU.mult))
                    st.settle()
                    nc.vector.tensor_tensor(k_n[:, 0:n], k_n[:, 0:n], t_sin[:, 0:n], ALU.add).then_inc(k_ready, 1)
                else:
                    norm(p, "k")

            def probs(p):
                g = p + 8 * f
                for hh in range(2):
                    dve.wait_ge(exp_done, 2 * g + hh + 1)
                    st(nc.vector.reciprocal(ri[:, hh, :], rs[:, hh, :]))
                    st.settle()
                    for b, ((q0, q1), (s0, s1)) in enumerate(zip(blocks(f), sc)):
                        r = slice(0, q1 - q0)
                        ins = nc.vector.tensor_scalar(p_e[r, hh, s0:s1], p_e[r, hh, s0:s1], ri[r, hh, b:b + 1], None, ALU.mult)
                        if b == len(sc) - 1:
                            ins.then_inc(p_ready, 1)

            def outputs(p):
                g = p + 8 * f
                dve.wait_ge(o_done, g + 1)
                wait(dve, o_ready, g)
                st(nc.vector.scalar_tensor_tensor(o_tmp[:, 0:n], bank[5][:, 0:n], 0.5, gate[:, 0:n], ALU.mult, ALU.mult))
                nc.vector.scalar_tensor_tensor(o_hi[:, p, c0:c1], bank[5][:, 0:n], 0.5, gate[:, 0:n],
                                               ALU.mult, ALU.mult).then_inc(o_taken, 1)

            def outputs_lo(p):
                g = p + 8 * f
                dve.wait_ge(o_taken, g + 1)
                nc.vector.tensor_tensor(o_lo[:, p, c0:c1], o_tmp[:, 0:n], o_hi[:, p, c0:c1].bitcast(F32),
                                        ALU.subtract).then_inc(o_ready, 1)

            def gates(p):
                g = p + 8 * f
                dve.wait_ge(th_ready, g + 1)
                wait(dve, o_taken, g)
                if f == 0:
                    nc.vector.tensor_scalar(gate[:, 0:n], th[:, 0:n], 1.0, None, ALU.add).then_inc(gate_ready, 1)
                else:
                    nc.vector.scalar_tensor_tensor(gate[:, 0:n], th[:, 0:n], 1.0, bank[3][:, 0:n], ALU.add,
                                                   ALU.mult).then_inc(gate_ready, 1)

            def splits(p, qs):
                for q in qs:
                    split_lo(dve, *following(name_of(f), p), q)

            splits(0, (0, 1, 2))
            norm(0, "q")
            norm_k(0)
            gates(0)
            splits(0, (3,))
            if f == 0:
                z = sp_c[0:16]
                dve.wait_ge(ln_done, 1)
                dve.wait_ge(z_known, 1)
                st(nc.vector.scalar_tensor_tensor(sp_b[0:16], z, 0.0, sp_a[0:16], ALU.min, ALU.subtract))
                st.settle()
                st(nc.vector.tensor_tensor_scan(z, one_row[0:16, 0:T], sp_b[0:16], 0.0, ALU.mult, ALU.add))
                st.settle()
                st(nc.vector.memset(c_2[:], 0.0))
                st(nc.vector.tensor_scalar(sp_b[0:16], z, -8.0, None, ALU.mult))
                st.settle()
                st(nc.vector.tensor_scalar(rows_a[0:16, 0, :], z, -8.0, None, ALU.mult))
                st.settle()
                st(nc.vector.tensor_copy(c_2[0:16], rows_a[0:16, 0, :].bitcast(F32)))
                st(nc.vector.tensor_tensor(c_2[32:48], sp_b[0:16], rows_a[0:16, 0, :].bitcast(F32), ALU.subtract))
                st.settle()
                nc.vector.tensor_tensor(rows_a[:], c_2[:].unsqueeze(1).to_broadcast([P, 16, T]),
                                        tb("own_head_a").unsqueeze(2).to_broadcast([P, 16, T]),
                                        ALU.mult).then_inc(rows_ready, 1)

            def step(p):
                splits(p, (0,))
                maxima(p - 1)
                probs(p - 1)
                splits(p, (1, 2))
                norm(p, "q")
                norm_k(p)
                outputs(p - 1)
                outputs_lo(p - 1)
                gates(p)
                splits(p, (3,))

            per = 1 + (2 if f == 0 else 0) + 2 * len(sc) + 2 + {0: 2, 1: 2, 2: 4}[f]
            step(1)
            st.loop(2, PAIRS - 1, per, step)
            step(PAIRS - 1)
            maxima(PAIRS - 1)
            probs(PAIRS - 1)
            outputs(PAIRS - 1)
            outputs_lo(PAIRS - 1)

        one_row = sb("one_row", [T], 64)
        bg_split = sem("bg_split")

        def ffn_span(f):
            return (0, T) if f == 0 else (META - CONV_PAST, T)

        def ffn_pe(pe, f):
            cols = c0, c1 = ffn_span(f)
            name = f"w_up{f}"

            def unit(u):
                for r in range(2):
                    g = u * 2 + (r + FT * f)
                    if not (isinstance(u, int) and u == 0 and f == 0):
                        pe.wait_ge(conv_done, g - 1)
                    for half in range(2):
                        q = 2 * r + half
                        weights_here(pe, name, u, q)
                        for k in range(KT):
                            if isinstance(u, int) and u == 0 and q == 0:
                                pe.wait_ge(x_ready, X_BASE[f"pre{2 * f + 1}"] + k + 1)
                            mm = product(bank[q][:, c0:c1], q, k * P, x_op, k, cols, k == 0, k == KT - 1)
                        mm.then_inc(chunk_used, 1)

            unit(0)
            with pe.Fori(1, FT // 2) as u:
                unit(u)

            def hid_wait(pe_, k):
                pe_.wait_ge(hid_ready, FT * f + k + 1)

            out_pe(pe, f"w_down{f}", f"post{2 * f + 1}", hid_op, FT, (0, T) if f == 0 else (META, T), hid_wait)

        def conv_w(f, j, half, tap):
            cw = pr("ffn_conv").rearrange("p (f j a t) -> p f j a t", f=2, j=FT, a=2)
            return cw[:, f, j, half, tap:tap + 1]

        def ffn_act(act, st, f):
            c0, c1 = ffn_span(f)
            o0 = 0 if f == 0 else META

            def taps(u, r):
                g = u * 2 + (r + FT * f)
                for half, y in ((0, g_y), (1, u_y)):
                    act.wait_ge(chunk_used, chunk(f"w_up{f}", u, 2 * r + half) + 1)
                    if half == 0 and not (isinstance(u, int) and u == 0 and f == 0):
                        act.wait_ge(prod_ready, g - 1)
                    nc.scalar.activation(y[:, r, o0:T], bank[2 * r + half][:, o0:T], ACT.Copy,
                                         scale=conv_w(f, u * 2 + r, half, 2)).then_inc(tap_ready, 1)

            def rest(u, r):
                g = u * 2 + (r + FT * f)
                act.wait_ge(conv_done, g + 1)
                nc.scalar.activation(g_e[:, r, o0:T], g_y[:, r, o0:T], ACT.Gelu_apprx_tanh).then_inc(gelu_done, 1)
                split_hi(act, *following(f"w_up{f}", u), 2 * r)
                act.wait_ge(prod_ready, g + 1)
                nc.scalar.activation(hid_op[0][:, u * 2 + r, o0:T], hid[:, r, o0:T], ACT.Copy).then_inc(hid_hi_ready, 1)
                split_hi(act, *following(f"w_up{f}", u), 2 * r + 1)

            def unit(u):
                for r in range(2):
                    taps(u, r)
                    rest(u, r)

            unit(0)
            with act.Fori(1, FT // 2 - 1) as u:
                unit(u)
            unit(FT // 2 - 1)
            out_act(act, f"w_down{f}", f"post{2 * f + 1}", (0, T) if f == 0 else (META, T))

        def ffn_dve(dve, st, f):
            o0 = 0 if f == 0 else META

            def step(u, r):
                g = u * 2 + (r + FT * f)
                j = u * 2 + r
                dve.wait_ge(tap_ready, g * 2 + 2)
                for back in (1, 2):
                    lo = max(o0, back)
                    for half, y in ((0, g_y), (1, u_y)):
                        ins = nc.vector.scalar_tensor_tensor(y[:, r, lo:T], bank[2 * r + half][:, lo - back:T - back],
                                                             conv_w(f, j, half, 2 - back), y[:, r, lo:T], ALU.mult, ALU.add)
                        if back == 1:
                            st(ins)
                        elif half == 1:
                            ins.then_inc(conv_done, 1)
                    if back == 1:
                        st.settle()
                split_lo(dve, *following(f"w_up{f}", u), 2 * r)
                dve.wait_ge(hid_hi_ready, g + 1)
                nc.vector.tensor_tensor(hid_op[1][:, j, o0:T], hid[:, r, o0:T], hid_op[0][:, j, o0:T].bitcast(F32),
                                        ALU.subtract).then_inc(hid_ready, 1)
                split_lo(dve, *following(f"w_up{f}", u), 2 * r + 1)

            def unit(u):
                for r in range(2):
                    step(u, r)

            unit(0)
            st.loop(1, FT // 2 - 1, 4, unit)
            unit(FT // 2 - 1)
            out_dve(dve, f"w_down{f}")

        def ffn_pool(pool, f):
            o0 = 0 if f == 0 else META

            def unit(u):
                for r in range(2):
                    g = u * 2 + (r + FT * f)
                    pool.wait_ge(gelu_done, g + 1)
                    if not (isinstance(u, int) and u == 0 and f == 0):
                        pool.wait_ge(hid_ready, g - 1)
                    nc.gpsimd.tensor_tensor(hid[:, r, o0:T], g_e[:, r, o0:T], u_y[:, r, o0:T], ALU.mult).then_inc(prod_ready, 1)

            unit(0)
            with pool.Fori(1, FT // 2) as u:
                unit(u)

        def dn_pe(pe):
            def feature(d, which):
                weights_here(pe, "w_dn", d, which)
                for k in range(KT):
                    mm = product(bank[which][:, 0:T], which, k * P, x_op, k, (0, T), k == 0, k == KT - 1)
                mm.then_inc(chunk_used, 1)

            def prepare(d):
                pe.wait_ge(dn["st"], 2 * d + 2)
                pe.wait_ge(dn["v_st"], d + 1)
                pe.wait_ge(rows_ready, 2)
                wait(pe, dn["kt_out"], 3 * d)
                wait(pe, dn["at"], d)
                wait(pe, dn["qk"], d)
                nc.tensor.matmul(bank[4][:, 0:TP], sum_gc_r[:], rows_d[:, d, :], start=True, stop=True).then_inc(dn["row"], 1)
                for c in range(NC):
                    mm = nc.tensor.transpose(bank[5][0:C, c * P:(c + 1) * P], v_st[:, c * C:(c + 1) * C], ident)
                mm.then_inc(dn["vt"], 1)
                for b, src in ((6, k_st), (7, q_st)):
                    for c in range(NC):
                        cc = slice(c * C, (c + 1) * C)
                        mm = nc.tensor.matmul(bank[b][0:C, cc], k_st[:, cc], src[:, cc], start=True, stop=True)
                mm.then_inc(dn["kk"], 1)
                pe.wait_ge(dn["erow"], d + 1)
                pe.wait_ge(dn["dec_t"], 3 * d + 3)
                for c in range(NC):
                    mm = nc.tensor.transpose(bank[4][0:C, c * P:(c + 1) * P], k_st[:, c * C:(c + 1) * C], ident)
                mm.then_inc(dn["kt"], 1)
                pe.wait_ge(dn["vt_out"], 3 * d + 3)
                nc.tensor.matmul(bank[5][0:C, 0:TP], sum_beta_r[:], rows_d[:, d, :], start=True, stop=True).then_inc(dn["beta"], 1)

            def step(d):
                first = isinstance(d, int) and d == 0
                for which, b in ((0, 0), (1, 1), (2, 2)):
                    if which < 2:
                        wait(pe, dn["root"], 2 * d + which - 1 if not first else 0)
                    else:
                        wait(pe, dn["conv"], 3 * d if not first else 0)
                    feature(d, which)
                pe.wait_ge(dn["conv"], 3 * d + 1)
                pe.wait_ge(dn["sq"], 2 * d + 1)
                nc.tensor.matmul(bank[0][:, 0:T], ones, q_sq[:, 0:T], start=True, stop=True).then_inc(dn["ssq"], 1)
                pe.wait_ge(dn["conv"], 3 * d + 2)
                pe.wait_ge(dn["sq"], 2 * d + 2)
                nc.tensor.matmul(bank[1][:, 0:T], ones, k_sq[:, 0:T], start=True, stop=True).then_inc(dn["ssq"], 1)
                if not first:
                    prepare(d - 1)
                    pe.wait_ge(dn["gate"], d)
                feature(d, 3)

            small_pe(pe, "w_beta_a", bank[4][:, 0:T], 64)
            step(0)
            pe.wait_ge(dn["bg"], 2)
            for c in range(NC):
                mm = nc.tensor.transpose(bank[5][0:C, c * 64:(c + 1) * 64], bg[0:64, c * C:(c + 1) * C], ident[0:64, 0:64])
            mm.then_inc(dn["bgt"], 1)
            pe.wait_ge(dn["bgt_out"], 1)
            step(1)
            with pe.Fori(2, DNH) as d:
                step(d)
            prepare(DNH - 1)

            pe.wait_ge(dn["init"], 1)
            pe.wait_ge(dn["gate"], DNH)
            pe.wait_ge(dn["kt_out"], NC * DNH)

            def level(lv):
                def x_of(hd):
                    g = lv * DNH + hd
                    pe.wait_ge(dn["l"], g + 1)
                    if not (isinstance(lv, int) and lv == 0):
                        pe.wait_ge(dn["d"], g - DNH + 1)
                    wait(pe, dn["x_out"], g - 1)
                    for c in range(NC):
                        cc = slice(c * C, (c + 1) * C)
                        mm = nc.tensor.matmul(bank[hd % 2][0:C, cc], l_st[:, hd % 2, cc], d_in[:, hd, cc], start=True, stop=True)
                    mm.then_inc(dn["x"], 1)

                def update(hd):
                    g = lv * DNH + hd
                    pe.wait_ge(dn["x_out"], g + 1)
                    wait(pe, dn["d"], g - 1)
                    for c in range(NC):
                        cc = slice(c * C, (c + 1) * C)
                        nc.tensor.matmul(bank[2 + hd % 2][0:C, cc], d_tr[:, hd, cc], x_st[:, hd % 2, cc], start=True, stop=True)
                        mm = nc.tensor.matmul(bank[4 + hd % 2][0:C, cc], x_st[:, hd % 2, cc], d_tr[:, hd, cc], start=True, stop=True)
                    mm.then_inc(dn["dd"], 1)

                x_of(0)
                for hd in range(1, DNH):
                    x_of(hd)
                    update(hd - 1)
                update(DNH - 1)

            level(0)
            with pe.Fori(1, LEVELS) as lv:
                level(lv)

            for c in range(NC):
                cc = slice(c * C, (c + 1) * C)

                def first_half(hd):
                    g = c * DNH + hd
                    if c:
                        pe.wait_ge(dn["s_new"], g - DNH + 1)
                        wait(pe, dn["r"], g - 1 - DNH)
                        nc.tensor.matmul(bank[hd % 2][0:C, 0:P], kn_all[:, hd, cc], s_t[:, hd, :], start=True,
                                         stop=True).then_inc(dn["ks"], 1)

                def second_half(hd):
                    g = c * DNH + hd
                    if c:
                        pe.wait_ge(dn["r"], g + 1 - DNH)
                        rhs = r_st[:, hd % 2, :]
                    else:
                        rhs = vb_all[:, hd, 0, :]
                        if hd == 0:
                            pe.wait_ge(dn["d"], LEVELS * DNH)
                    wait(pe, dn["u_out"], g - 1)
                    nc.tensor.matmul(bank[2 + hd % 2][0:C, 0:P], d_tr[:, hd, cc], rhs, start=True, stop=True).then_inc(dn["u"], 1)

                def third(hd):
                    g = c * DNH + hd
                    pe.wait_ge(dn["u_out"], g + 1)
                    wait(pe, dn["o_out"], g - 1)
                    if c:
                        nc.tensor.matmul(bank[4 + hd % 2][:, 0:C], s_t[:, hd, :], qd_all[:, hd, cc], start=True, stop=False)
                    nc.tensor.matmul(bank[4 + hd % 2][:, 0:C], u_st[:, hd % 2, :], qk_all[:, hd, cc], start=c == 0,
                                     stop=True).then_inc(dn["o"], 1)
                    if c < NC - 1:
                        wait(pe, dn["s_new"], g - 1)
                        nc.tensor.matmul(bank[6 + hd % 2][:, 0:P], kd_all[:, hd, c, :], u_st[:, hd % 2, :], start=True,
                                         stop=True).then_inc(dn["s_up"], 1)

                for hd in range(DNH + 2):
                    if hd < DNH:
                        first_half(hd)
                    if 0 <= hd - 1 < DNH:
                        second_half(hd - 1)
                    if hd >= 2:
                        third(hd - 2)

            for hd in range(DNH):
                pe.wait_ge(dn["osq"], hd + 1)
                wait(pe, dn["oroot"], hd - 1)
                nc.tensor.matmul(bank[6 + hd % 2][:, 0:T], ones, sq[:, hd % 2, :], start=True, stop=True).then_inc(dn["osum"], 1)

            def o_wait(pe_, k):
                pe_.wait_ge(dn["ot"], k + 1)
            out_pe(pe, "w_dn_out", "post2", o_op, KT, (META - CONV_PAST, T), o_wait)

        def dn_conv_w(d, which, tap):
            cw = pr("dn_conv").rearrange("p (h a t) -> p h a t", h=DNH, a=3)
            return cw[:, d, which, tap:tap + 1]

        def dn_act(act, st):
            bb = slice(32, 40)
            small_splits(act, split_hi, "w_beta_a")
            act.wait_ge(chunk_used, chunk("w_beta_a", 0, 3) + 1)
            act.wait_ge(dn["zero"], 1)
            nc.scalar.activation(bg[0:8, PAD:TP], bank[4][0:8, 0:T], ACT.Sigmoid).then_inc(dn["bg"], 1)
            act.wait_ge(z_known, 2)
            st(nc.scalar.activation(sp_a[bb], sp_c[bb], ACT.Abs))
            st.settle()
            st(nc.scalar.activation(sp_b[bb], sp_a[bb], ACT.Exp, scale=-1.0))
            nc.scalar.activation(neg_a[bb], pr("a_log")[bb], ACT.Exp).then_inc(dn["negexp"], 1)
            st.settle()
            nc.scalar.activation(sp_a[bb], sp_b[bb], ACT.Ln, bias=ones[bb, 0:1]).then_inc(ln_done, 1)

            def tap(d, which, y):
                act.wait_ge(chunk_used, chunk("w_dn", d, which) + 1)
                nc.scalar.activation(y[:, 0:T], bank[which][:, 0:T], ACT.Copy, scale=dn_conv_w(d, which, 3)).then_inc(dn["tap"], 1)

            def silu_sq(d, which, y, s):
                act.wait_ge(dn["conv"], 3 * d + which + 1)
                st(nc.scalar.activation(y[:, 0:T], y[:, 0:T], ACT.Silu))
                st.settle()
                nc.scalar.activation(s[:, 0:T], y[:, 0:T], ACT.Square).then_inc(dn["sq"], 1)

            def main(d):
                first = isinstance(d, int) and d == 0
                wait(act, dn["st"], 2 * d if not first else 0)
                tap(d, 0, q_y)
                tap(d, 1, k_y)
                silu_sq(d, 0, q_y, q_sq)
                silu_sq(d, 1, k_y, k_sq)
                wait(act, dn["v_st"], d)
                tap(d, 2, v_y)

            def value(d):
                act.wait_ge(dn["conv"], 3 * d + 3)
                if not (isinstance(d, int) and d == 0):
                    act.wait_ge(dn["vt"], d)
                nc.scalar.activation(v_st[:, PAD:TP], v_y[:, 0:T], ACT.Silu).then_inc(dn["v_st"], 1)

            def roots(d):
                for which, s in ((0, q_sq), (1, k_sq)):
                    act.wait_ge(dn["ssq"], 2 * d + which + 1)
                    nc.scalar.activation(s[:, 0:T], bank[which][:, 0:T], ACT.Sqrt, bias=eps["rms"]).then_inc(dn["root"], 1)

            def out_gate(d):
                act.wait_ge(chunk_used, chunk("w_dn", d, 3) + 1)
                nc.scalar.activation(o_gate[:, d, :], bank[3][:, 0:T], ACT.Silu).then_inc(dn["gate"], 1)

            def prep(d):
                act.wait_ge(dn["row"], d + 1)
                wait(act, dn["qd"], d)
                st.settle()
                nc.scalar.activation(e_row[:], bank[4][:, 0:TP], ACT.Exp).then_inc(dn["erow"], 1)
                act.wait_ge(dn["vt"], d + 1)
                for c in range(NC):
                    nc.scalar.activation(vb_all[:, d, c, :], bank[5][0:C, c * P:(c + 1) * P], ACT.Copy,
                                         scale=bg_t[:, c, bass.ds(d, 1)]).then_inc(dn["vt_out"], 1)
                act.wait_ge(dn["erow"], d + 1)
                st(nc.scalar.activation(g_last[:, d, :], e_row[:].rearrange("p (c t) -> p c t", c=NC)[:, :, C - 1],
                                        ACT.Copy))
                act.wait_ge(dn["dec_t"], 3 * d + 3)
                nc.scalar.activation(dec[:], t_dec[:], ACT.Exp).then_inc(dn["dec"], 1)
                act.wait_ge(dn["kt"], d + 1)
                act.wait_ge(dn["dec"], d + 1)
                for c in range(NC):
                    nc.scalar.activation(kd_all[:, d, c, :], bank[4][0:C, c * P:(c + 1) * P], ACT.Copy,
                                         scale=dec[:, (c + 1) * C - 1:(c + 1) * C]).then_inc(dn["kt_out"], 1)

            def splits(d, qs):
                for q in qs:
                    split_hi(act, *following("w_dn", d), q)

            main(0)
            splits(0, (0, 1))
            roots(0)
            value(0)
            splits(0, (2,))
            out_gate(0)
            splits(0, (3,))
            act.wait_ge(dn["bgt"], 1)
            nc.scalar.activation(bg_t[:], bank[5][0:C, 0:NC * 64], ACT.Copy).then_inc(dn["bgt_out"], 1)
            act.wait_ge(dn["bgt_out"], 1)
            nc.scalar.activation(eg_t[:], bg_t[:, :, 32:40], ACT.Exp).then_inc(dn["eg"], 1)

            def step(d):
                main(d)
                splits(d, (0, 1))
                prep(d - 1)
                value(d)
                splits(d, (2,))
                roots(d)
                out_gate(d)
                splits(d, (3,))

            step(1)
            st.loop(2, DNH - 1, 3, step)
            step(DNH - 1)
            prep(DNH - 1)

            def level(lv):
                for hd in range(DNH):
                    g = lv * DNH + hd
                    act.wait_ge(dn["x"], g + 1)
                    wait(act, dn["dd"], g - 1)
                    nc.scalar.activation(x_st[:, hd % 2, :], bank[hd % 2][0:C, 0:TP], ACT.Copy).then_inc(dn["x_out"], 1)
            level(0)
            with act.Fori(1, LEVELS) as lv:
                level(lv)

            for c in range(NC):
                for hd in range(DNH + 1):
                    if hd < DNH:
                        g = c * DNH + hd
                        act.wait_ge(dn["u"], g + 1)
                        if g >= 2:
                            act.wait_ge(dn["o"], g - 1)
                            act.wait_ge(dn["s_up"], min(g - 1, 2 * DNH))
                        nc.scalar.activation(u_st[:, hd % 2, :], bank[2 + hd % 2][0:C, 0:P], ACT.Copy).then_inc(dn["u_out"], 1)
                    if hd:
                        g = c * DNH + hd - 1
                        act.wait_ge(dn["o"], g + 1)
                        nc.scalar.activation(o_raw[:, hd - 1, c * C:(c + 1) * C], bank[4 + (hd - 1) % 2][:, 0:C],
                                             ACT.Copy).then_inc(dn["o_out"], 1)
            for hd in range(DNH):
                act.wait_ge(dn["o_out"], 2 * DNH + hd + 1)
                wait(act, dn["osum"], hd - 1)
                nc.scalar.activation(sq[:, hd % 2, :], o_raw[:, hd, PAD:TP], ACT.Square).then_inc(dn["osq"], 1)
                if hd:
                    o_root(act, hd - 1)
            o_root(act, DNH - 1)
            out_act(act, "w_dn_out", "post2", (META - CONV_PAST, T))

        def o_root(act, hd):
            act.wait_ge(dn["osum"], hd + 1)
            wait(act, dn["ot"], hd - 1)
            dst = (root, root2)[hd % 2]
            nc.scalar.activation(dst[:], bank[6 + hd % 2][:, 0:T], ACT.Sqrt, bias=eps["rms"],
                                 scale=1.0 / P).then_inc(dn["oroot"], 1)

        def dn_dve(dve, st):
            bb = slice(32, 40)
            small_splits(dve, split_lo, "w_beta_a")
            dve.wait_ge(chunk_used, chunk("w_beta_a", 0, 3) + 1)
            nc.vector.tensor_scalar(sp_c[bb], bank[4][bb, 0:T], pr("dt_bias")[bb], None, ALU.add).then_inc(z_known, 1)
            dve.wait_ge(dn["negexp"], 1)
            st(nc.vector.tensor_scalar(neg_a[bb], neg_a[bb], -1.0, None, ALU.mult))
            dve.wait_ge(ln_done, 2)
            st.settle()
            st(nc.vector.scalar_tensor_tensor(sp_c[bb], sp_c[bb], 0.0, sp_a[bb], ALU.max, ALU.add))
            st.settle()
            dve.wait_ge(dn["zero"], 1)
            st(nc.vector.tensor_scalar(g_pad[bb, PAD:TP], sp_c[bb], neg_a[bb], None, ALU.mult))
            st.settle()
            for c in range(NC):
                cc = slice(c * C, (c + 1) * C)
                ins = nc.vector.tensor_tensor_scan(bg[bb, cc], one_row[bb, 0:C], g_pad[bb, cc], 0.0, ALU.mult, ALU.add)
                st(ins) if c < NC - 1 else ins.then_inc(dn["bg"], 1)

            def conv(d, which, y):
                dve.wait_ge(dn["tap"], 3 * d + which + 1)
                for back in (1, 2, 3):
                    ins = nc.vector.scalar_tensor_tensor(y[:, back:T], bank[which][:, 0:T - back], dn_conv_w(d, which, 3 - back),
                                                         y[:, back:T], ALU.mult, ALU.add)
                    if back < 3:
                        st(ins)
                        st.settle()
                    else:
                        ins.then_inc(dn["conv"], 1)

            def norms(d):
                for which, (y, s, dst, scale) in enumerate(((q_y, q_sq, q_st, P ** -0.5), (k_y, k_sq, k_st, 1.0))):
                    dve.wait_ge(dn["root"], 2 * d + which + 1)
                    wait(dve, dn["st"], 2 * d + which)
                    st(nc.vector.reciprocal(t_sin[:, 0:T], s[:, 0:T]))
                    st.settle()
                    if which == 0 and not (isinstance(d, int) and d == 0):
                        dve.wait_ge(dn["kt"], d)
                        dve.wait_ge(dn["qd"], d)
                        dve.wait_ge(dn["kcopy"], d)
                    nc.vector.scalar_tensor_tensor(dst[:, PAD:TP], y[:, 0:T], scale, t_sin[:, 0:T], ALU.mult,
                                                   ALU.mult).then_inc(dn["st"], 1)

            def prep(d):
                dve.wait_ge(dn["erow"], d + 1)
                nc.vector.tensor_tensor(qd_all[:, d, :], q_st[:], e_row[:], ALU.mult).then_inc(dn["qd"], 1)
                nc.vector.tensor_copy(kn_all[:, d, :], k_st[:]).then_inc(dn["kcopy"], 1)
                for c in range(NC):
                    cc = slice(c * C, (c + 1) * C)
                    nc.vector.scalar_tensor_tensor(t_dec[:, cc], bank[4][0:C, cc], bg_t[:, c, bass.ds(d + 32, 1)], tb("later"),
                                                   ALU.subtract, ALU.add).then_inc(dn["dec_t"], 1)
                dve.wait_ge(dn["dec"], d + 1)
                dve.wait_ge(dn["kk"], d + 1)
                nc.vector.tensor_tensor(at_1[:], bank[6][0:C, 0:TP], dec[:], ALU.mult).then_inc(dn["a1"], 1)
                nc.vector.tensor_tensor(qk_all[:, d, :], bank[7][0:C, 0:TP], dec[:], ALU.mult).then_inc(dn["qk"], 1)
                dve.wait_ge(dn["a2"], d + 1)
                dve.wait_ge(dn["beta"], d + 1)
                nc.vector.tensor_tensor(a_tr[:, d, :], at_2[:], bank[5][0:C, 0:TP], ALU.mult).then_inc(dn["at"], 1)

            def convs(d):
                conv(d, 0, q_y)
                conv(d, 1, k_y)
                conv(d, 2, v_y)

            def splits(d, qs):
                for q in qs:
                    split_lo(dve, *following("w_dn", d), q)

            convs(0)
            splits(0, (0, 1, 2))
            norms(0)
            splits(0, (3,))
            dve.wait_ge(dn["bg"], 2)
            st.settle()
            st(nc.vector.tensor_copy(rows_d[0:64, 0, :], bg[0:64]))
            st.settle()
            nc.vector.tensor_tensor(bg[64:128], bg[0:64], rows_d[0:64, 0, :].bitcast(F32), ALU.subtract).then_inc(bg_split, 1)
            dve.wait_ge(bg_split, 1)
            dve.wait_ge(dn["bgt"], 1)
            st(nc.vector.tensor_copy(bg[0:64], rows_d[0:64, 0, :].bitcast(F32)))
            st.settle()
            nc.vector.tensor_tensor(rows_d[:], bg[:].unsqueeze(1).to_broadcast([P, DNH, TP]),
                                    tb("own_head").unsqueeze(2).to_broadcast([P, DNH, TP]), ALU.mult).then_inc(rows_ready, 1)
            dve.wait_ge(dn["eg"], 1)
            st(nc.vector.scalar_tensor_tensor(nbz[:], eg_t[:], -1.0, bg_t[:, :, 0:8], ALU.mult, ALU.mult))

            def step(d):
                convs(d)
                splits(d, (0, 1))
                prep(d - 1)
                splits(d, (2,))
                norms(d)
                splits(d, (3,))
            step(1)
            st.loop(2, DNH - 1, 8, step)
            step(DNH - 1)
            prep(DNH - 1)

            def level(lv):
                for hd in range(DNH):
                    g = lv * DNH + hd
                    dve.wait_ge(dn["dd"], g + 1)
                    st(nc.vector.tensor_tensor(d_in[:, hd, :], d_in[:, hd, :], bank[2 + hd % 2][0:C, 0:TP], ALU.subtract))
                    nc.vector.tensor_tensor(d_tr[:, hd, :], d_tr[:, hd, :], bank[4 + hd % 2][0:C, 0:TP],
                                            ALU.subtract).then_inc(dn["d"], 1)
            dve.wait_ge(dn["init"], 1)
            level(0)
            st.loop(1, LEVELS, DNH, level)

            for c in range(NC):
                def residual(hd):
                    g = (c - 1) * DNH + hd
                    dve.wait_ge(dn["ks"], g + 1)
                    dve.wait_ge(dn["u"], c * DNH + hd - 1)
                    nc.vector.scalar_tensor_tensor(r_st[:, hd % 2, :], bank[hd % 2][0:C, 0:P], nbz[:, c, hd:hd + 1],
                                                   vb_all[:, hd, c, :], ALU.mult, ALU.add).then_inc(dn["r"], 1)

                def state(hd):
                    g = c * DNH + hd
                    dve.wait_ge(dn["s_up"], g + 1)
                    if c == 0:
                        nc.vector.tensor_copy(s_t[:, hd, :], bank[6 + hd % 2][:, 0:P]).then_inc(dn["s_new"], 1)
                    else:
                        nc.vector.scalar_tensor_tensor(s_t[:, hd, :], s_t[:, hd, :], g_last[:, hd, c:c + 1],
                                                       bank[6 + hd % 2][:, 0:P], ALU.mult, ALU.add).then_inc(dn["s_new"], 1)
                for hd in range(DNH + 2):
                    if hd < DNH and c:
                        residual(hd)
                    if hd >= 2 and c < NC - 1:
                        state(hd - 2)
            for hd in range(DNH):
                dve.wait_ge(dn["oroot"], hd + 1)
                wait(dve, dn["ot"], hd)
                st(nc.vector.reciprocal(rstd[:], (root, root2)[hd % 2][:]))
                st.settle()
                st(nc.vector.scalar_tensor_tensor(t_sin[:], o_raw[:, hd, PAD:TP], pr("o_gain"), rstd[:], ALU.mult, ALU.mult))
                st.settle()
                st(nc.vector.tensor_tensor(o_hi[:, hd, :], t_sin[:], o_gate[:, hd, :], ALU.mult))
                st(nc.vector.tensor_tensor(o_gate[:, hd, :], t_sin[:], o_gate[:, hd, :], ALU.mult))
                st.settle()
                nc.vector.tensor_tensor(o_lo[:, hd, :], o_gate[:, hd, :], o_hi[:, hd, :].bitcast(F32),
                                        ALU.subtract).then_inc(dn["ot"], 1)
            out_dve(dve, "w_dn_out")

        g_pad = sb("g_pad", [TP], 64)

        def by_chunk(ap):
            return ap.rearrange("p (c t) -> p c t", c=NC)

        def by_block(at):
            return at[:].rearrange("p h (c t) -> p (h c) t", c=NC)

        def dn_pool(pool):
            def step(d):
                pool.wait_ge(dn["a1"], d + 1)
                wait(pool, dn["at"], d)
                nc.gpsimd.tensor_tensor(by_chunk(at_2[:]), by_chunk(at_1[:]), tb("strict").unsqueeze(1).to_broadcast([C, NC, C]),
                                        ALU.mult).then_inc(dn["a2"], 1)

            step(0)
            with pool.Fori(1, DNH) as d:
                step(d)
            pool.wait_ge(dn["kt_out"], NC * DNH)
            pool.wait_ge(dn["at"], DNH)
            pool.wait_ge(dn["qk"], DNH)
            pool.wait_ge(dn["kcopy"], DNH)
            nc.gpsimd.tensor_copy(by_block(d_in), tb("ident_c").unsqueeze(1).to_broadcast([C, DNH * NC, C]))
            nc.gpsimd.tensor_copy(by_block(d_tr), tb("ident_c").unsqueeze(1).to_broadcast([C, DNH * NC, C])).then_inc(dn["init"], 1)
            pool.wait_ge(dn["at"], DNH)

            def level(lv):
                for hd in range(DNH):
                    g = lv * DNH + hd
                    wait(pool, dn["x"], g - 1)
                    masks = tb("levels").rearrange("p (l t) -> p l t", l=LEVELS)
                    nc.gpsimd.tensor_tensor(by_chunk(l_st[:, hd % 2, :]), by_chunk(a_tr[:, hd, :]),
                                            masks[:, lv, :].unsqueeze(1).to_broadcast([C, NC, C]), ALU.mult).then_inc(dn["l"], 1)
            for lv in range(LEVELS):
                level(lv)

        def latent_pe(pe):
            c0, c1 = META, T
            for j in range(KT):
                if j >= 2:
                    pe.wait_ge(sq_ready, sq0["lat_q"] + j - 1)
                weights_here(pe, "w_latent", j // 4, j % 4)
                for k in range(KT):
                    if j == 0:
                        pe.wait_ge(x_ready, X_BASE["post3"] + k + 1)
                    mm = product(bank[j % 2][:, c0:c1], j % 4, k * P, x_op, k, (c0, c1), k == 0, k == KT - 1)
                mm.then_inc(chunk_used, 1)
                if j:
                    lat_sum(pe, j - 1)
            lat_sum(pe, KT - 1)
            small_pe(pe, "w_k_rope", bank[5][:, c0:c1], 64)
            pe.wait_ge(kr_seen, 1)
            nc.tensor.matmul(bank[5][0:64, c0:c1], tb("rot32"), kr_raw[:], start=True, stop=True).then_inc(kr_rot, 1)

        def lat_sum(pe, j):
            if j < QL:
                sum_tile(pe, "lat_q", j, QL, (META, T), where=7)
            else:
                sum_tile(pe, "lat_kv", j - QL, KVL, (META, T), where=6)

        z_lat = sem("z_lat")

        def latent_act(act, st):
            c0, c1 = META, T
            x_split_act(act, h, (c0, c1), X_BASE["post3"], (h_ready, 3 * KT))
            split = out_splits(act, split_hi, "w_latent")
            for j in range(KT):
                act.wait_ge(chunk_used, out_tile_done("w_latent", j))
                nc.scalar.activation(m[:, j, c0:c1], bank[j % 2][:, c0:c1], ACT.Copy).then_inc(z_lat, 1)
                name, jj = ("lat_q", j) if j < QL else ("lat_kv", j - QL)
                square(act, bank[j % 2][:, c0:c1], name, jj, (c0, c1))
                split(j)
            rms_root(act, "lat_q", QL * P, (c0, c1), root)
            rms_root(act, "lat_kv", KVL * P, (c0, c1), root2, where=6)
            small_splits(act, split_hi, "w_k_rope")
            act.wait_ge(chunk_used, chunk("w_k_rope", 0, 3) + 1)
            nc.scalar.activation(kr_raw[:], bank[5][0:64, c0:c1], ACT.Copy).then_inc(kr_seen, 1)
            for j in range(KT):
                act.wait_ge(lat_t, j + 1)
                nc.scalar.activation(lat_op[0][:, j, c0:c1], m[:, j, c0:c1], ACT.Copy).then_inc(lat_hi_ready, 1)

        def latent_dve(dve, st):
            c0, c1 = META, T
            for j in range(KT):
                x_split_dve(dve, h, (c0, c1), X_BASE["post3"], j)
            split = out_splits(dve, split_lo, "w_latent")
            for j in range(KT):
                split(j)
            invert_root(dve, st, "lat_q", (c0, c1), root, rstd)
            invert_root(dve, st, "lat_kv", (c0, c1), root2, rstd2)
            dve.wait_ge(z_lat, KT)
            small_splits(dve, split_lo, "w_k_rope")
            for j in range(KT + 1):
                if j < KT:
                    gain, r = (pr("q_lat")[:, j:j + 1], rstd) if j < QL else (pr("kv_lat")[:, j - QL:j - QL + 1], rstd2)
                    nc.vector.scalar_tensor_tensor(m[:, j, c0:c1], m[:, j, c0:c1], gain, r[:, c0:c1], ALU.mult,
                                                   ALU.mult).then_inc(lat_t, 1)
                if j:
                    dve.wait_ge(lat_hi_ready, j)
                    nc.vector.tensor_tensor(lat_op[1][:, j - 1, c0:c1], m[:, j - 1, c0:c1],
                                            lat_op[0][:, j - 1, c0:c1].bitcast(F32), ALU.subtract).then_inc(lat_ready, 1)
            dve.wait_ge(kr_seen, 1)
            st(nc.vector.tensor_tensor(kr_cos[:], kr_raw[:], tb("cos32"), ALU.mult))
            dve.wait_ge(kr_rot, 1)
            st(nc.vector.tensor_tensor(kr_sin[:], bank[5][0:64, c0:c1], tb("sin32"), ALU.mult))
            st.settle()
            nc.vector.tensor_tensor(k_rp[:, 0:SEQ], kr_cos[:], kr_sin[:], ALU.add).then_inc(kr_ready, 1)

        gains = {"pre0": pr("mix_pre")[:, 0:KT], "post0": pr("mix_post")[:, 0:KT],
                 "pre1": pr("ffn_pre")[:, 0:KT], "post1": pr("ffn_post")[:, 0:KT],
                 "pre2": pr("mix_pre")[:, KT:], "post2": pr("mix_post")[:, KT:],
                 "pre3": pr("ffn_pre")[:, KT:], "post3": pr("ffn_post")[:, KT:]}
        FULL, TAIL, LAST = (0, T), (META - CONV_PAST, T), (META, T)

        @block.tensor
        def _(pe):
            pe.wait_ge(s_in, 48)
            sums_pe(pe, "pre0", KT, FULL)
            pe.wait_ge(ones_ready, 3)
            small_pe(pe, "w_forget", bank[7][:, 0:T], 16)
            attention_pe(pe, 0)
            out_pe(pe, "w_attn_out", "post0", o_op, KT, FULL, lambda e, k: e.wait_ge(o_ready, k + 1))
            sums_pe(pe, "pre1", KT, FULL)
            ffn_pe(pe, 0)
            sums_pe(pe, "pre2", KT, FULL)
            dn_pe(pe)
            sums_pe(pe, "pre3", KT, TAIL)
            ffn_pe(pe, 1)
            latent_pe(pe)
            attention_pe(pe, 1)
            out_pe(pe, "w_mla_out", None, o_op, KT, LAST, lambda e, k: e.wait_ge(o_ready, 8 + k + 1), mean=True)
            sums_pe(pe, "var1", KT, LAST)
            attention_pe(pe, 2)
            out_pe(pe, "w_moba_out", None, o_op, KT, LAST, lambda e, k: e.wait_ge(o_ready, 16 + k + 1), mean=True)
            sums_pe(pe, "var2", KT, LAST)

        @block.scalar
        def _(act):
            st = Steps(act, act_step)
            act.wait_ge(s_in, 48)
            nc.scalar.activation(ones_r[:], ones, ACT.Copy).then_inc(ones_ready, 1)
            nc.scalar.activation(sum_gc_r[:], tb("sum_gc"), ACT.Copy).then_inc(ones_ready, 1)
            nc.scalar.activation(sum_beta_r[:], tb("sum_beta"), ACT.Copy).then_inc(ones_ready, 1)
            for q in range(4):
                split_hi(act, "w_forget", 0, q)
            pre_norm_act(act, "pre0", FULL, None)
            small_splits(act, split_hi, "w_forget")
            act.wait_ge(chunk_used, chunk("w_forget", 0, 3) + 1)
            nc.scalar.activation(sp_c[0:16], bank[7][0:16, 0:T], ACT.Identity, bias=pr("b_forget")[0:16]).then_inc(z_known, 1)
            attention_act(act, st, 0)
            out_act(act, "w_attn_out", "post0", FULL)
            pre_norm_act(act, "pre1", FULL, 0)
            ffn_act(act, st, 0)
            pre_norm_act(act, "pre2", FULL, 8)
            dn_act(act, st)
            pre_norm_act(act, "pre3", TAIL, 16)
            ffn_act(act, st, 1)
            latent_act(act, st)
            attention_act(act, st, 1)
            ln_act(act, "w_mla_out", 1)
            x_split_act(act, h, LAST, X_BASE["ln1"], (h_ready, 4 * KT))
            attention_act(act, st, 2)
            ln_act(act, "w_moba_out", 2)

        @block.vector
        def _(dve):
            st = Steps(dve, dve_step)
            st(nc.vector.memset(one_row[:], 1.0))
            st(nc.vector.memset(rs[:], 1.0))
            st(nc.vector.memset(mx[:], 0.0))
            st.settle()
            dve.wait_ge(s_in, 48)
            for q in range(4):
                split_lo(dve, "w_forget", 0, q)
            pre_norm_dve(dve, st, "pre0", gains["pre0"], FULL)
            small_splits(dve, split_lo, "w_forget")
            attention_dve(dve, st, 0)
            out_dve(dve, "w_attn_out")
            dve.wait_ge(m_ready, KT)
            post_norm_dve(dve, st, "post0", gains["post0"], FULL)
            dve.wait_ge(h_ready, 8)
            pre_norm_dve(dve, st, "pre1", gains["pre1"], FULL)
            ffn_dve(dve, st, 0)
            dve.wait_ge(m_ready, 2 * KT)
            post_norm_dve(dve, st, "post1", gains["post1"], FULL)
            dve.wait_ge(h_ready, 16)
            pre_norm_dve(dve, st, "pre2", gains["pre2"], FULL)
            dn_dve(dve, st)
            dve.wait_ge(m_ready, 3 * KT)
            post_norm_dve(dve, st, "post2", gains["post2"], TAIL)
            dve.wait_ge(h_ready, 24)
            pre_norm_dve(dve, st, "pre3", gains["pre3"], TAIL)
            ffn_dve(dve, st, 1)
            dve.wait_ge(m_ready, 4 * KT)
            post_norm_dve(dve, st, "post3", gains["post3"], LAST)
            latent_dve(dve, st)
            st(nc.vector.memset(rs[:], 1.0))
            st(nc.vector.memset(mx[:], 0.0))
            st.settle()
            attention_dve(dve, st, 1)
            ln_dve(dve, st, "w_mla_out", 1)
            for j in range(KT):
                x_split_dve(dve, h, LAST, X_BASE["ln1"], j)
            attention_dve(dve, st, 2)
            ln_dve(dve, st, "w_moba_out", 2)

        @block.gpsimd
        def _(pool):
            nc.gpsimd.memset(g_pad[:], 0.0)
            ffn_pool(pool, 0)
            pool.wait_ge(chunk_used, chunk("w_down0", KT - 1, 3) + 1)
            nc.gpsimd.memset(bg[:], 0.0)
            nc.gpsimd.memset(q_st[:], 0.0)
            nc.gpsimd.memset(k_st[:], 0.0)
            nc.gpsimd.memset(v_st[:], 0.0).then_inc(dn["zero"], 1)
            dn_pool(pool)
            ffn_pool(pool, 1)


def lay_out(inp):
    f32 = np.float32

    def cols(wm, c0, n):
        b = wm[:, c0:c0 + n]
        return b.reshape(b.shape[0] // P, P, n).transpose(1, 0, 2).reshape(P, -1)

    def units(lists):
        return np.ascontiguousarray(np.stack([np.concatenate(x, 1) for x in lists])).astype(f32, copy=False)

    def outs(wm):
        return units([[cols(wm, (4 * u + q) * P, P) for q in range(4)] for u in range(2)])

    w = {}
    wa = inp["attn_w_in"][0]
    w["w_attn"] = units([[cols(wa, s * D + p * P, P) for s in range(4)] for p in range(PAIRS)])
    w["w_attn_out"] = outs(inp["attn_w_out"][0])
    wd = inp["dn_w_in"][0]
    w["w_dn"] = units([[cols(wd, s * D + p * P, P) for s in range(4)] for p in range(DNH)])
    w["w_dn_out"] = outs(inp["dn_w_out"][0])
    for f in range(2):
        up, down = inp["ffn_w_up"][f], inp["ffn_w_down"][f]
        w[f"w_up{f}"] = units([[cols(up, half * FFN + (2 * u + r) * P, P) for r in range(2) for half in range(2)]
                               for u in range(FT // 2)])
        w[f"w_down{f}"] = units([[cols(down, j * P, P)] for j in range(KT)])
    wm = inp["mla_w_in_2"][0]
    w["w_latent"] = outs(wm[:, 0:D])
    uq, ukv = inp["mla_w_uq_2"][0], inp["mla_w_ukv_2"][0]

    def gather(wm_, parts):
        return cols(np.concatenate([wm_[:, c:c + n] for c, n in parts], 1), 0, sum(n for _, n in parts))

    w["w_mla"] = units([[
        gather(uq, [((2 * p + i) * 96, 64) for i in range(2)]),
        gather(uq, [((2 * p + i) * 96 + 64, 32) for i in range(2)]), np.zeros((P, 64), f32),
        gather(ukv, [((2 * p + i) * 128, 64) for i in range(2)]),
        gather(ukv, [((2 * p + i) * 128 + 64, 64) for i in range(2)]),
        cols(wm, D + 32 + p * P, P)] for p in range(PAIRS)])
    w["w_mla_out"] = outs(inp["mla_w_o_2"][0])
    kv, wi = inp["moba_w_kv_2"], inp["moba_w_in_2"][0]
    w["w_moba"] = units([[cols(wi, p * P, P), cols(kv, p * P, P), cols(kv, D + p * P, P), cols(wi, D + p * P, P)]
                         for p in range(PAIRS)])
    w["w_moba_out"] = outs(inp["moba_w_o_2"][0])

    where, width = param_columns()
    par = np.zeros((P, width), f32)

    def put(name, a, r0=0):
        at, n = where[name]
        a = a.reshape(a.shape[0], -1)
        assert a.shape[1] == n, (name, a.shape, n)
        par[r0:r0 + a.shape[0], at:at + n] = a

    for name, src in (("mix_pre", "norm_mix_pre"), ("mix_post", "norm_mix_post"), ("ffn_pre", "norm_ffn_pre"),
                      ("ffn_post", "norm_ffn_post"), ("ln_g", "ln_g_2"), ("ln_b", "ln_b_2")):
        put(name, inp[src].reshape(2, KT, P).transpose(2, 0, 1))
    put("q_gain", np.tile(inp["attn_q_norm"][0], 2)[:, None])
    put("k_gain", np.tile(inp["attn_k_norm"][0], 2)[:, None])
    put("b_forget", inp["attn_b_forget"][0][:, None])
    put("a_log", inp["dn_a_log"][0][:, None], 32)
    put("dt_bias", inp["dn_dt_bias"][0][:, None], 32)
    put("o_gain", inp["dn_o_norm"][0][:, None])
    put("q_lat", inp["mla_q_norm_2"][0].reshape(QL, P).T)
    put("kv_lat", inp["mla_kv_norm_2"][0].reshape(KVL, P).T)
    put("dn_conv", inp["dn_conv"][0].reshape(4, 3, DNH, P).transpose(3, 2, 1, 0))
    put("ffn_conv", inp["ffn_conv"].reshape(2, 3, 2, FT, P).transpose(4, 0, 3, 2, 1))

    def small(wm_, n):
        c_ = cols(wm_, 0, n).reshape(P, 4, 2 * n)
        return np.ascontiguousarray(np.concatenate([c_, np.zeros((P, 4, P - n), f32)], 2).reshape(1, P, -1))

    w["w_forget"] = small(wa[:, 4 * D:4 * D + 16], 16)
    ba = np.zeros((D, 64), f32)
    ba[:, 0:8] = wd[:, 4 * D:4 * D + 8]
    ba[:, 32:40] = wd[:, 4 * D + 8:4 * D + 16]
    w["w_beta_a"] = small(ba, 64)
    kr = wm[:, D:D + 32]
    w["w_k_rope"] = small(np.concatenate([kr, kr], 1), 64)
    return w, par


def kernel(**inputs):
    import concourse.bacc as bacc
    from concourse.bass_utils import run_bass_kernel_spmd

    inp = {k: np.asarray(v) for k, v in inputs.items()}
    w, par = lay_out(inp)
    tw = table_columns()[1]
    table = np.zeros((P, tw), np.float32)
    for name, a in tables().items():
        rows, at, n = table_columns()[0][name]
        table[0:rows, at:at + n] = a
    x = np.concatenate([inp["meta_tokens"], inp["x"][0]], 0)
    arrays = {"x": np.ascontiguousarray(x.reshape(T, KT, P).transpose(2, 1, 0)), "table": table, "params": par, **w}
    nc = bacc.Bacc("TRN2", target_bir_lowering=False, num_devices=1)
    aps = {k: nc.dram_tensor(k, v.shape, F32, kind="ExternalInput").ap() for k, v in arrays.items()}
    out = nc.dram_tensor("out", (P, KT, SEQ), F32, kind="ExternalOutput").ap()
    build(nc, aps["x"], aps["table"], aps["params"], {k: aps[k] for k in w}, out)
    r = run_bass_kernel_spmd(nc, [arrays], core_ids=[0])
    got = r.results[0]["out"]
    return np.ascontiguousarray(got.transpose(2, 1, 0)).reshape(1, SEQ, D)
```

```python
from contextlib import ExitStack

import numpy as np

import concourse.bass as bass
from concourse import mybir

F32 = mybir.dt.float32
F32R = mybir.dt.float32r
ALU = mybir.AluOpType
ACT = mybir.ActivationFunctionType
AX = mybir.AxisListType.X

P = 128
D = 1024
KT = D // P
META = 16
SEQ = 256
T = META + SEQ
CONV_PAST = 2
FFN = 2816
FT = FFN // P
PAIRS = 8
DNH = 8
C = 96
NC = 3
TP = C * NC
PAD = TP - T
SLOTS = 3
LEVELS = 7
CHUNK = 8 * P
NEG = -1e30
ALPHA = 4 ** 0.25
RMS_EPS = 1e-6
LN_EPS = 1e-5
QL, KVL = 6, 2

BLK_A = [(0, META), (META, META + P), (META + P, T)]
BLK_B = [(META, META + P), (META + P, T)]


def tables():
    t = {}
    t["ident"] = np.eye(P)
    t["ones"] = np.ones((P, P))
    t["head_ones"] = np.kron(np.eye(2), np.ones((64, 64)))
    sel = np.zeros((P, P))
    sel[32:40] = sel[96:104] = 1.0
    t["sum_gc"] = sel
    sel = np.zeros((P, C))
    sel[0:8] = sel[64:72] = 1.0
    t["sum_beta"] = sel
    t["own_head_a"] = np.kron(np.array([[1.0], [0.0], [1.0]] + [[0.0]] * 5), np.eye(16))
    t["rms_eps"] = np.full((P, 1), RMS_EPS)
    t["ln_eps"] = np.full((P, 1), LN_EPS)

    def rot(dim, copies):
        m = np.zeros((dim, dim))
        for d in range(dim // 2):
            m[d + dim // 2, d] = -1.0
            m[d, d + dim // 2] = 1.0
        return np.kron(np.eye(copies), m)

    t["rot64"] = rot(64, 2)
    t["rot32"] = rot(32, 2)

    def angles(dim):
        inv = (np.float32(10000.0) ** (-np.arange(0, dim, 2, dtype=np.float32) / np.float32(dim))).astype(np.float32)
        a = np.arange(SEQ, dtype=np.float32)[:, None] * inv[None, :]
        a = np.concatenate([a, a], -1).T
        return np.concatenate([a, a], 0)

    t["cos64"], t["sin64"] = np.cos(angles(64)), np.sin(angles(64))
    t["cos32"], t["sin32"] = np.cos(angles(32)), np.sin(angles(32))

    def causal(blocks):
        parts = []
        for q0, q1 in blocks:
            q = np.arange(q0, q0 + P)[:, None]
            k = np.arange(blocks[0][0], q1)[None, :]
            parts.append(np.where(k <= q, 0.0, NEG))
        return np.concatenate(parts, 1)

    t["mask_a"] = causal(BLK_A)
    t["mask_b"] = causal(BLK_B)
    j, i = np.arange(C)[:, None], np.arange(C)[None, :]
    t["later"] = np.where(i >= j, 0.0, NEG)
    t["strict"] = (i > j) * 1.0
    lev = [((j // (2 * b) == i // (2 * b)) & (i % (2 * b) < b) & (j % (2 * b) >= b)) * 1.0
           for b in (1 << n for n in range(1, LEVELS))]
    t["levels"] = np.concatenate(lev, 1)
    t["pairs"] = ((i == j + 1) & (j % 2 == 0)) * 1.0
    t["ident_c"] = np.eye(C)
    t["row_of"] = np.tile(np.eye(DNH).reshape(1, -1), (P, 1))
    t["row_to"] = np.repeat(np.eye(DNH), P, 1)
    own = np.zeros((P, DNH))
    for r0 in (0, 32, 64, 96):
        own[r0 + np.arange(8), np.arange(8)] = 1.0
    t["own_head"] = own
    return t


def table_columns():
    at, where = 0, {}
    for name, a in tables().items():
        where[name] = (a.shape[0], at, a.shape[1])
        at += a.shape[1]
    return where, at


PARAMS = [("mix_pre", 2 * KT), ("mix_post", 2 * KT), ("ffn_pre", 2 * KT), ("ffn_post", 2 * KT),
          ("q_gain", 1), ("k_gain", 1), ("b_forget", 1), ("a_log", 1), ("dt_bias", 1), ("o_gain", 1),
          ("q_lat", QL), ("kv_lat", KVL), ("ln_g", 2 * KT), ("ln_b", 2 * KT),
          ("dn_conv", DNH * 3 * 4), ("ffn_conv", 2 * FT * 2 * 3)]


def param_columns():
    at, where = 0, {}
    for name, n in PARAMS:
        where[name] = (at, n)
        at += n
    return where, at


CHUNKS = {"attn": [8 * P] * 4, "out": [8 * P] * 4, "up": [8 * P] * 4, "down": [6 * P, 6 * P, 5 * P, 5 * P],
          "mla": [QL * P, (QL + 1) * 64, 2 * KVL * P, 8 * P], "s16": [2 * 16 + 112] * 4, "s64": [2 * 64 + 64] * 4}
STREAM = [("w_forget", "s16", 1), ("w_attn", "attn", PAIRS), ("w_attn_out", "out", 2), ("w_up0", "up", FT // 2),
          ("w_down0", "down", KT), ("w_beta_a", "s64", 1), ("w_dn", "attn", DNH), ("w_dn_out", "out", 2),
          ("w_up1", "up", FT // 2), ("w_down1", "down", KT), ("w_latent", "out", 2), ("w_k_rope", "s64", 1),
          ("w_mla", "mla", PAIRS), ("w_mla_out", "out", 2), ("w_moba", "attn", PAIRS), ("w_moba_out", "out", 2)]
KIND = {name: kind for name, kind, _ in STREAM}
UNITS = {name: n for name, _, n in STREAM}
NEXT = {a[0]: b[0] for a, b in zip(STREAM, STREAM[1:])}


class Steps:

    def __init__(self, eng, sem):
        self.eng, self.sem, self.base, self.n = eng, sem, 0, 0

    def __call__(self, ins):
        ins.then_inc(self.sem, 1)
        self.n += 1
        return self.n

    def settle(self, upto=None):
        self.eng.wait_ge(self.sem, self.base + (self.n if upto is None else upto))

    def loop(self, start, stop, per, body):
        before = self.base + self.n
        with self.eng.Fori(start, stop) as i:
            self.base, self.n = (i - start) * per + before, 0
            body(i)
            assert self.n == per, (self.n, per)
        self.base, self.n = 0, before + (stop - start) * per


def wait(eng, sem, value):
    if not isinstance(value, int) or value > 0:
        eng.wait_ge(sem, value)


def build(nc, x, table, params, w, out):
    tcol, tw = table_columns()
    pcol, pw = param_columns()
    unit0, at = {}, 0
    for name, kind, n in STREAM:
        unit0[name] = at
        at += n
    ctx = ExitStack()
    with ctx:
        def sb(name, shape, rows=P):
            return ctx.enter_context(nc.sbuf_tensor(name, [rows, *shape], F32))

        def sem(name):
            return ctx.enter_context(nc.semaphore(name))

        bank = [ctx.enter_context(nc.psum_tensor(f"bank{i}", [P, 512], F32)) for i in range(8)]
        ARENA = 73600
        X_AT, O_AT = ARENA, ARENA + 2 * 4 * KT * T
        SLAB = O_AT + 2 * 4 * KT * T
        slab_at = (nc.sbuf_base + 63) // 64 * 64
        ctx.enter_context(nc.sbuf_tensor("slab", [P, SLAB // 4 + 16], F32))

        class Place:

            def __init__(self, at, end):
                self.at, self.end = at, end

            def __call__(self, name, shape, rows=P, dtype=F32):
                got = nc.alloc_sbuf_tensor_at(name, [rows, *shape], dtype, offset=slab_at + self.at)
                self.at += (4 * int(np.prod(shape)) + 31) // 32 * 32
                assert self.at <= self.end, (name, self.at, self.end)
                return got

        tab = sb("tab", [tw])
        par = sb("par", [pw])
        raw = sb("raw", [4, CHUNK])
        w_hi = ctx.enter_context(nc.sbuf_tensor("w_hi", [P, 4, CHUNK], F32R))
        w_lo = ctx.enter_context(nc.sbuf_tensor("w_lo", [P, 4, CHUNK], F32R))
        h = sb("h", [KT, T])
        m = sb("m", [KT, T])
        put_x, put_o = Place(X_AT, O_AT), Place(O_AT, SLAB)
        x_hi, x_lo = put_x("x_hi", [KT, T], dtype=F32R), put_x("x_lo", [KT, T], dtype=F32R)
        o_hi, o_lo = put_o("o_hi", [KT, T], dtype=F32R), put_o("o_lo", [KT, T], dtype=F32R)
        x_op, o_op = (x_hi, x_lo), (o_hi, o_lo)
        sq = sb("sq", [SLOTS, T])
        root = sb("root", [T])
        rstd = sb("rstd", [T])
        root2 = sb("root2", [T])
        rstd2 = sb("rstd2", [T])
        ones_r = ctx.enter_context(nc.sbuf_tensor("ones_r", [P, P], F32R))
        sum_gc_r = ctx.enter_context(nc.sbuf_tensor("sum_gc_r", [P, P], F32R))
        sum_beta_r = ctx.enter_context(nc.sbuf_tensor("sum_beta_r", [P, C], F32R))

        def tb(name):
            rows, at, n = tcol[name]
            return tab[0:rows, at:at + n]

        def pr(name):
            at, n = pcol[name]
            return par[:, at:at + n]

        ident, ones, head_ones = tb("ident"), tb("ones"), tb("head_ones")
        eps = {"rms": tb("rms_eps"), "ln": tb("ln_eps")}

        tokens_in = [sem("tokens_in_0"), sem("tokens_in_1")]
        prime_out = sb("prime_out", [1])
        primed = sem("primed")
        s_in, tables_in = sem("s_in"), sem("tables_in")
        early = tcol["rot64"][1]
        loaded = [sem(f"chunk{i}_loaded") for i in range(4)]
        hi_done, lo_done, chunk_used = sem("hi_done"), sem("lo_done"), sem("chunk_used")
        xt_ready, xh_ready, x_ready, ones_ready = sem("xt_ready"), sem("xh_ready"), sem("x_ready"), sem("ones_ready")
        act_step, dve_step, pool_step = sem("act_step"), sem("dve_step"), sem("pool_step")
        sq_ready, sq_used = sem("sq_ready"), sem("sq_used")
        sum_done, root_done = sem("sum_done"), sem("root_done")
        h_ready, m_ready = sem("h_ready"), sem("m_ready")
        z_ready = sem("z_ready")
        stored = sem("stored")

        put = Place(0, ARENA)
        q_raw, k_raw = sb("q_raw", [T]), sb("k_raw", [T])
        q_sq, k_sq = sb("q_sq", [T]), sb("k_sq", [T])
        t_sin, th = sb("t_sin", [T]), sb("th", [T])
        q_n, k_n = put("q_n", [T]), put("k_n", [T])
        q_rp, k_rp = put("q_rp", [T], 64), put("k_rp", [T], 64)
        rp_raw = put("rp_raw", [T], 64)
        v_s = put("v_s", [3, P])
        gate, o_tmp = put("gate", [T]), put("o_tmp", [T])
        s_m = put("s_m", [2, 432])
        p_e = put("p_e", [2, 432])
        mx, rs, ri = put("mx", [2, 3]), put("rs", [2, 3]), put("ri", [2, 3])
        pt = put("pt", [2, 384])
        pt0 = put("pt0", [2, T], META)
        sp_a, sp_b, sp_c = (put(n, [T], 64) for n in ("sp_a", "sp_b", "sp_c"))
        rest = put.at
        rows_a = put("rows_a", [16, T], P, F32R)
        c_2 = put("c_2", [T])
        put.at = rest
        lat_op = put("lat_hi", [KT, T], dtype=F32R), put("lat_lo", [KT, T], dtype=F32R)
        kr_raw, kr_cos, kr_sin = (put(n, [SEQ], 64) for n in ("kr_raw", "kr_cos", "kr_sin"))

        q_copied, k_copied = sem("q_copied"), sem("k_copied")
        q_side, k_side = sem("q_side"), sem("k_side")
        qk_root = sem("qk_root")
        q_ready, k_ready, v_ready, gate_ready, th_ready = (sem(n) for n in (
            "q_ready", "k_ready", "v_ready", "gate_ready", "th_ready"))
        o_ready, lat_ready, lat_hi_ready, lat_t = sem("o_ready"), sem("lat_ready"), sem("lat_hi_ready"), sem("lat_t")
        s_done, s_taken, max_ready, exp_done, p_ready = (sem(n) for n in (
            "s_done", "s_taken", "max_ready", "exp_done", "p_ready"))
        pt_done, pt_taken, o_done, o_taken = (sem(n) for n in ("pt_done", "pt_taken", "o_done", "o_taken"))
        small_done, rows_ready, kr_seen, kr_rot, kr_ready = (sem(n) for n in (
            "small_done", "rows_ready", "kr_seen", "kr_rot", "kr_ready"))
        ln_scaled = sem("ln_scaled")
        z_known, ln_done = sem("z_known"), sem("ln_done")

        put = Place(0, ARENA)
        hid_op = put("hid_hi", [FT, T], dtype=F32R), put("hid_lo", [FT, T], dtype=F32R)
        g_y, u_y, g_e, hid = (put(n, [2, T]) for n in ("g_y", "u_y", "g_e", "hid"))
        prod_ready, hid_hi_ready = sem("prod_ready"), sem("hid_hi_ready")
        tap_ready, conv_done, gelu_done, hid_ready = (sem(n) for n in (
            "tap_ready", "conv_done", "gelu_done", "hid_ready"))

        put = Place(0, ARENA)
        rows_d = put("rows_d", [DNH, TP], dtype=F32R)
        put.at = 0
        d_in = put("d_in", [DNH, TP], C)
        stage_at = put.at
        q_st, k_st, v_st = put("q_st", [TP]), put("k_st", [TP]), put("v_st", [TP])
        e_row = put("e_row", [TP])
        t_dec, dec = put("t_dec", [TP], C), put("dec", [TP], C)
        at_1, at_2 = put("at_1", [TP], C), put("at_2", [TP], C)
        put.at = stage_at
        d_tr = put("d_tr", [DNH, TP], C)
        a_tr = put("a_tr", [DNH, TP], C)
        kn_all, qd_all = put("kn_all", [DNH, TP]), put("qd_all", [DNH, TP])
        qk_all = put("qk_all", [DNH, TP], C)
        vb_all = put("vb_all", [DNH, NC, P], C)
        bg = put("bg", [TP])
        bg_t = put("bg_t", [NC, 64], C)
        eg_t, nbz = put("eg_t", [NC, DNH], C), put("nbz", [NC, DNH], C)
        g_last = put("g_last", [DNH, NC])
        put_o.at = O_AT
        kd_all = put_o("kd_all", [DNH, NC, P], C)
        g_pad = put_o("g_pad", [TP], 64)
        sd_a, sd_b, sd_c = (put_o(n, [T], 64) for n in ("sd_a", "sd_b", "sd_c"))
        put_x.at = X_AT
        x_st = put_x("x_st", [4, TP], C)
        s_t = put_x("s_t", [DNH, P])
        r_st, u_st = put_x("r_st", [2, P], C), put_x("u_st", [2, P], C)
        o_gate = m
        q_y, k_y, v_y = q_raw, k_raw, th
        neg_a = sb("neg_a", [1], 64)
        o_raw = kn_all
        dn = {n: sem("dn_" + n) for n in (
            "tap", "conv", "sq", "ssq", "root", "st", "v_st", "gate", "row", "vt", "vt_out", "kk", "kt",
            "kt_out", "beta", "dec_t", "dec", "erow", "a1", "a2", "at", "qk", "qd", "kcopy", "prep", "bg", "bgt",
            "pair", "clear", "x", "x_out", "dd", "d", "t", "d_in", "ks", "r", "u", "u_out", "o", "o_out", "s_up", "s_new",
            "osq", "osum", "oroot", "ohi", "olo", "oinv", "onorm", "ospread", "zero", "negexp", "bgt_out", "eg", "ot")}

        block = ctx.enter_context(nc.Block())

        out_names = [n for n, kind, _ in STREAM if kind in ("out", "down")]
        out_stage = {n: i for i, n in enumerate(out_names)}

        def chunk(name, u, q):
            return u * 4 + (4 * unit0[name] + q)

        def chunk_width(name, q):
            return CHUNKS[KIND[name]][q]

        def split_hi(act, name, u, q):
            n, wd = chunk(name, u, q), chunk_width(name, q)
            act.wait_ge(loaded[q], u * 16 + 16 * (unit0[name] + 1))
            if unit0[name] or not isinstance(u, int) or u:
                act.wait_ge(chunk_used, n - 3)
            nc.scalar.activation(w_hi[:, q, 0:wd], raw[:, q, 0:wd], ACT.Copy).then_inc(hi_done, 1)

        def split_lo(dve, name, u, q):
            n, wd = chunk(name, u, q), chunk_width(name, q)
            dve.wait_ge(hi_done, n + 1)
            nc.vector.tensor_tensor(w_lo[:, q, 0:wd], raw[:, q, 0:wd], w_hi[:, q, 0:wd].bitcast(F32),
                                    ALU.subtract).then_inc(lo_done, 1)

        def following(name, u):
            if isinstance(u, int) and u == UNITS[name] - 1:
                return (NEXT[name], 0) if name in NEXT else None
            return name, u + 1

        def weights_here(pe, name, u, q):
            pe.wait_ge(lo_done, chunk(name, u, q) + 1)

        def product(dst, q, w0, src, k, cols, first, last, m_cols=P):
            c0, c1 = cols
            hi, lo = w_hi[:, q, w0:w0 + m_cols], w_lo[:, q, w0:w0 + m_cols]
            nc.tensor.matmul(dst, hi, src[0][:, k, c0:c1], start=first, stop=False)
            nc.tensor.matmul(dst, hi, src[1][:, k, c0:c1], start=False, stop=False)
            return nc.tensor.matmul(dst, lo, src[0][:, k, c0:c1], start=False, stop=last)

        @block.sync
        def _(sp):
            half = KT // 2
            sp.dma_start(h[:, 0:half], x[:, 0:half]).then_inc(tokens_in[0], 16)
            sp.dma_start(tab[:, 0:early], table[:, 0:early]).then_inc(s_in, 16)
            sp.dma_start(par[:], params).then_inc(s_in, 16)
            sp.dma_start(h[:, half:], x[:, half:]).then_inc(tokens_in[1], 16)
            for name, kind, n in STREAM:
                def load(u):
                    w0 = 0
                    for q in range(4):
                        wd = chunk_width(name, q)
                        if unit0[name] or not isinstance(u, int) or u:
                            sp.wait_ge(lo_done, chunk(name, u, q) - 3)
                        sp.dma_start(raw[:, q, 0:wd], w[name][u][:, w0:w0 + wd]).then_inc(loaded[q], 16)
                        w0 += wd

                load(0)
                if name == "w_attn":
                    sp.dma_start(tab[:, early:], table[:, early:]).then_inc(tables_in, 16)
                if n > 1:
                    with sp.Fori(1, n) as u:
                        load(u)
            for part in range(0, KT, 2):
                sp.wait_ge(h_ready, 5 * KT + part + 2)
                sp.dma_start(out[:, part:part + 2, :], h[:, part:part + 2, META:T]).then_inc(stored, 16)
            sp.wait_ge(stored, KT // 2 * 16)

        REDUCE = ([(f"pre{i}", KT) if k % 2 == 0 else (f"post{i}", KT) for i in range(4) for k in (0, 1)]
                  + [("lat_q", QL), ("lat_kv", KVL), ("var1", KT), ("var2", KT)])
        sq0, red_no, tot = {}, {}, 0
        for n_, (name, tiles) in enumerate(REDUCE):
            sq0[name], red_no[name] = tot, n_
            tot += tiles
        sum_order = [n for n, _ in REDUCE[:10]] + ["mean1", "var1", "mean2", "var2"]
        sum_no = {n: i + 1 for i, n in enumerate(sum_order)}
        root_no = {n: i + 1 for i, (n, _) in enumerate(REDUCE)}
        H_AFTER = {"post0": 8, "post1": 16, "post2": 24, "post3": 32, "ln1": 40, "ln2": 48}

        def square(act, src, name, j, cols):
            n = sq0[name] + j
            wait(act, sq_used, n - SLOTS + 1)
            nc.scalar.activation(sq[:, n % SLOTS, cols[0]:cols[1]], src, ACT.Square).then_inc(sq_ready, 1)

        def sum_tile(pe, name, j, tiles, cols, static_j=None, where=7):
            n = sq0[name] + j
            pe.wait_ge(sq_ready, n + 1)
            sj = j if static_j is None else static_j
            first = static_j is None and j == 0
            last = static_j is None and j == tiles - 1
            slot = sj % 2 if name in ("post0", "post1", "post2", "post3") else n % SLOTS
            mm = nc.tensor.matmul(bank[where][:, cols[0]:cols[1]], ones, sq[:, slot, cols[0]:cols[1]],
                                  start=first, stop=last)
            mm.then_inc(sq_used, 1)

        def prime(act, name):
            n = PRIMES.index(name)
            wait(act, primed, n)
            nc.scalar.activation(prime_out[:], eps["rms"], ACT.Sqrt).then_inc(primed, 1)

        PRIMES = ["pre0", "post0", "post1", "post2", "post3", "lat_q", "var1", "var2"]

        def rms_root(act, name, count, cols, dst, where=7, e="rms"):
            act.wait_ge(sq_used, sq0[name] + dict(REDUCE)[name])
            nc.scalar.activation(dst[:, cols[0]:cols[1]], bank[where][:, cols[0]:cols[1]], ACT.Sqrt,
                                 bias=eps[e], scale=1.0 / count).then_inc(root_done, 1)

        def invert_root(dve, st, name, cols, src, dst):
            dve.wait_ge(root_done, root_no[name])
            st(nc.vector.reciprocal(dst[:, cols[0]:cols[1]], src[:, cols[0]:cols[1]]))
            st.settle()

        def pre_norm_act(act, name, cols, h_base, between=None):
            for j in range(KT):
                if h_base is None:
                    if j % (KT // 2) == 0:
                        act.wait_ge(tokens_in[j // (KT // 2)], 16)
                else:
                    act.wait_ge(h_ready, h_base + j + 1)
                square(act, h[:, j, cols[0]:cols[1]], name, j, cols)
            if between:
                between()
            rms_root(act, name, D, cols, root)
            x_split_act(act, m, cols, KT * int(name[3]), (xt_ready, KT * int(name[3])))

        def sums_pe(pe, name, tiles, cols, where=7):
            for j in range(tiles):
                sum_tile(pe, name, j, tiles, cols, where=where)

        def x_split_act(act, src, cols, base, ready):
            for j in range(KT):
                act.wait_ge(ready[0], ready[1] + j + 1)
                nc.scalar.activation(x_hi[:, j, cols[0]:cols[1]], src[:, j, cols[0]:cols[1]], ACT.Copy).then_inc(xh_ready, 1)

        def x_split_dve(dve, src, cols, base, j):
            dve.wait_ge(xh_ready, base + j + 1)
            nc.vector.tensor_tensor(x_lo[:, j, cols[0]:cols[1]], src[:, j, cols[0]:cols[1]],
                                    x_hi[:, j, cols[0]:cols[1]].bitcast(F32), ALU.subtract).then_inc(x_ready, 1)

        def pre_norm_dve(dve, st, name, gain, cols):
            invert_root(dve, st, name, cols, root, rstd)
            base = KT * int(name[3])
            for j in range(KT + 1):
                if j < KT:
                    nc.vector.scalar_tensor_tensor(m[:, j, cols[0]:cols[1]], h[:, j, cols[0]:cols[1]], gain[:, j:j + 1],
                                                   rstd[:, cols[0]:cols[1]], ALU.mult, ALU.mult).then_inc(xt_ready, 1)
                if j:
                    x_split_dve(dve, m, cols, base, j - 1)

        def post_norm_dve(dve, st, name, gain, cols):
            invert_root(dve, st, name, cols, root, rstd)
            c0, c1 = cols
            marks = []
            for j in range(KT + (4 if name == "post3" else 2)):
                if j < KT:
                    marks.append(st(nc.vector.scalar_tensor_tensor(
                        m[:, j, c0:c1], m[:, j, c0:c1], gain[:, j:j + 1], rstd[:, c0:c1], ALU.mult, ALU.mult)))
                if 2 <= j < KT + 2:
                    st.settle(marks[j - 2])
                    nc.vector.tensor_tensor(h[:, j - 2, c0:c1], h[:, j - 2, c0:c1], m[:, j - 2, c0:c1],
                                            ALU.add).then_inc(h_ready, 1)
                if name == "post3" and j >= 4:
                    x_split_dve(dve, h, cols, X_BASE["post3"], j - 4)

        def out_pe(pe, wname, norm, src, src_tiles, cols, first_wait, mean=False):
            down = src_tiles == FT
            b_out = 4 if down else 0
            c0, c1 = cols

            def tile(j, jr):
                if jr >= 2 or not isinstance(j, int):
                    pe.wait_ge(z_ready if mean else sq_ready, (ZB[wname] if mean else sq0[norm]) + j - 1)
                k = 0
                for q in (range(4) if down else (jr % 4,)):
                    weights_here(pe, wname, j if down else jr // 4, q)
                    for t_ in range(chunk_width(wname, q) // P):
                        if isinstance(j, int) and j == 0:
                            first_wait(pe, k)
                        mm = product(bank[b_out + jr % 2][:, c0:c1], q, t_ * P, src, k, cols, k == 0, k == src_tiles - 1)
                        k += 1
                    mm.then_inc(chunk_used, 1)

            def add(j, static=None):
                if mean:
                    pe.wait_ge(z_ready, ZB[wname] + j + 1)
                    mm = nc.tensor.matmul(bank[7][:, c0:c1], ones, m[:, j, c0:c1], start=j == 0, stop=j == KT - 1)
                    if j == KT - 1:
                        mm.then_inc(sum_done, 1)
                else:
                    sum_tile(pe, norm, j, KT, cols, static_j=static)

            if down:
                tile(0, 0)
                tile(1, 1)
                add(0)
                with pe.Fori(1, KT // 2) as i:
                    for r in range(2):
                        tile(i * 2 + r, r)
                        add(i * 2 + (r - 1), static=(r - 1) % 2)
                add(KT - 1)
            else:
                for j in range(KT):
                    tile(j, j)
                    if j:
                        add(j - 1)
                add(KT - 1)

        ZB = {"w_mla_out": 0, "w_moba_out": 8}

        def out_tile_done(wname, j):
            if KIND[wname] == "down":
                return chunk(wname, j, 3) + 1
            return chunk(wname, j // 4, j % 4) + 1 if isinstance(j, int) else chunk(wname, 0, 0) + j + 1

        def out_splits(eng, split, wname):
            def step(j):
                if KIND[wname] == "down":
                    f_ = following(wname, j)
                    for q in range(4):
                        split(eng, *f_, q)
                elif isinstance(j, int):
                    f_ = following(wname, j // 4)
                    if f_:
                        split(eng, *f_, j % 4)
            return step

        def out_act(act, wname, norm, cols):
            b_out = 4 if "down" in wname else 0
            c0, c1 = cols
            split = out_splits(act, split_hi, wname)

            def tile(j, r):
                if KIND[wname] == "down":
                    split(j)
                act.wait_ge(chunk_used, out_tile_done(wname, j))
                nc.scalar.activation(m[:, j, c0:c1], bank[b_out + r][:, c0:c1], ACT.Copy).then_inc(m_ready, 1)
                n = j + sq0[norm]
                wait(act, sq_used, n - 1)
                nc.scalar.activation(sq[:, r, c0:c1], bank[b_out + r][:, c0:c1], ACT.Square).then_inc(sq_ready, 1)
                if KIND[wname] != "down":
                    split(j)

            tile(0, 0)
            tile(1, 1)
            if KIND[wname] == "down":
                with act.Fori(1, KT // 2 - 1) as i:
                    for r in range(2):
                        tile(i * 2 + r, r)
                tile(KT - 2, 0)
                prime(act, norm)
                tile(KT - 1, 1)
            else:
                for j in range(2, KT):
                    if j == KT - 1:
                        prime(act, norm)
                    tile(j, j % 2)
            rms_root(act, norm, D, cols, root)

        def out_dve(dve, wname):
            split = out_splits(dve, split_lo, wname)
            if KIND[wname] == "down":
                with dve.Fori(0, KT - 1) as j:
                    split(j)
                split(KT - 1)
            else:
                for j in range(KT):
                    split(j)

        def ln_dve(dve, st, wname, n_ln):
            split = out_splits(dve, split_lo, wname)
            c0, c1 = META, T
            for j in range(KT):
                dve.wait_ge(chunk_used, out_tile_done(wname, j))
                nc.vector.scalar_tensor_tensor(m[:, j, c0:c1], h[:, j, c0:c1], ALPHA, bank[j % 2][:, c0:c1],
                                               ALU.mult, ALU.add).then_inc(z_ready, 1)
                split(j)
            dve.wait_ge(sum_done, n_ln)
            st(nc.vector.tensor_scalar(root2[:, c0:c1], bank[7][:, c0:c1], 1.0 / D, None, ALU.mult))
            st.settle()
            dve.wait_ge(z_ready, ZB[wname] + KT)
            for j in range(KT):
                nc.vector.tensor_tensor(m[:, j, c0:c1], m[:, j, c0:c1], root2[:, c0:c1],
                                        ALU.subtract).then_inc(m_ready, 1)
            invert_root(dve, st, f"var{n_ln}", (c0, c1), root, rstd)
            dve.wait_ge(m_ready, MB_LN[n_ln] + KT)
            g0 = (n_ln - 1) * KT
            for j in range(KT + 2):
                if j < KT:
                    nc.vector.scalar_tensor_tensor(m[:, j, c0:c1], m[:, j, c0:c1], pr("ln_g")[:, g0 + j:g0 + j + 1],
                                                   rstd[:, c0:c1], ALU.mult, ALU.mult).then_inc(ln_scaled, 1)
                if j >= 2 and n_ln == 1:
                    dve.wait_ge(h_ready, 4 * KT + j - 1)
                    x_split_dve(dve, h, (c0, c1), X_BASE["ln1"], j - 2)

        MB_LN = {1: 4 * KT, 2: 5 * KT}

        def ln_act(act, wname, n_ln):
            c0, c1 = META, T
            split = out_splits(act, split_hi, wname)
            for j in range(KT):
                split(j)
            prime(act, f"var{n_ln}")
            for j in range(KT):
                act.wait_ge(m_ready, MB_LN[n_ln] + j + 1)
                square(act, m[:, j, c0:c1], f"var{n_ln}", j, (c0, c1))
            rms_root(act, f"var{n_ln}", D, (c0, c1), root, e="ln")
            g0 = (n_ln - 1) * KT
            for j in range(KT):
                act.wait_ge(ln_scaled, g0 + j + 1)
                bias = pr("ln_b")[:, g0 + j:g0 + j + 1]
                nc.scalar.activation(h[:, j, c0:c1], m[:, j, c0:c1], ACT.Identity, bias=bias).then_inc(h_ready, 1)
                if n_ln == 1:
                    nc.scalar.activation(x_hi[:, j, c0:c1], m[:, j, c0:c1], ACT.Identity, bias=bias).then_inc(xh_ready, 1)

        SCALE = {0: 0.125, 1: 96 ** -0.5, 2: 0.125}

        def blocks(f):
            return BLK_A if f == 0 else BLK_B

        def span(f):
            return (0, T) if f == 0 else (META, T)

        def s_cols(f):
            at, res = 0, []
            for q0, q1 in blocks(f):
                n = q1 - blocks(f)[0][0]
                res.append((at, at + n))
                at += n
            return res

        def name_of(f):
            return ("w_attn", "w_mla", "w_moba")[f]

        def projected(f, p, which):
            q = {"q": (0, 1, 0), "k": (1, 2, 1), "v": (2, 2, 2), "g": (3, 3, 3)}[which][f]
            return chunk(name_of(f), p, q) + 1

        def pe_project(pe, f, p, aw):
            name = name_of(f)
            g = p + 8 * f
            cols = c0, c1 = span(f)
            src = {s: (q, 0, x_op, 0, KT) for q, s in enumerate("qkvg")}
            if f == 1:
                src = {"q": (0, 0, lat_op, 0, QL), "r": (1, 0, lat_op, 0, QL), "k": (2, 0, lat_op, QL, KVL),
                       "v": (2, KVL * P, lat_op, QL, KVL), "g": (3, 0, x_op, 0, KT)}

            def feature(s, dst, width=P, part=None):
                q, w0, op, t0, n = src[s]
                weights_here(pe, name, p, q)
                for k in part or range(n):
                    if s == "q" and isinstance(p, int) and p == 0:
                        aw(pe, k)
                    mm = product(dst, q, w0 + k * width, op, t0 + k, cols, k == 0, k == n - 1)
                return mm

            def queries():
                wait(pe, q_ready, g)
                feature("q", bank[0][:, 0:c1 - c0]).then_inc(chunk_used, 1)

            def keys():
                if f == 1:
                    feature("r", bank[0][:, 256:512], 64).then_inc(chunk_used, 1)
                wait(pe, k_ready, g)
                if f == 1 and isinstance(p, int) and p == 0:
                    pe.wait_ge(lat_ready, KT)
                mm = feature("k", bank[1][:, 0:c1 - c0])
                if f != 1:
                    mm.then_inc(chunk_used, 1)

            def sides():
                n = c1 - c0
                if f != 1:
                    pe.wait_ge(q_copied, g + 1)
                k_seen = g + 1 if f == 0 else p + 9
                if f == 0:
                    nc.tensor.matmul(bank[0][:, 0:n], head_ones, q_sq[:, 0:n], start=True, stop=True).then_inc(q_side, 1)
                    pe.wait_ge(k_copied, k_seen)
                    nc.tensor.matmul(bank[1][:, 0:n], head_ones, k_sq[:, 0:n], start=True, stop=True).then_inc(k_side, 1)
                elif f == 1:
                    nc.tensor.matmul(bank[0][0:64, 256:512], tb("rot32"), rp_raw[:, 0:n], start=True, stop=True).then_inc(q_side, 1)
                else:
                    nc.tensor.matmul(bank[0][:, 0:n], tb("rot64"), q_raw[:, 0:n], start=True, stop=True).then_inc(q_side, 1)
                    pe.wait_ge(k_copied, k_seen)
                    nc.tensor.matmul(bank[1][:, 0:n], tb("rot64"), k_raw[:, 0:n], start=True, stop=True).then_inc(k_side, 1)

            def values():
                wait(pe, v_ready, g)
                q, w0, op, t0, n = src["v"]
                weights_here(pe, name, p, q)
                for b, (b0, b1) in enumerate(blocks(f)):
                    if f == 1 and b == 1:
                        pe.wait_ge(q_copied, g + 1)
                    dst = bank[2][:, b * P:(b + 1) * P]
                    for k in range(n):
                        hi, lo = (t_[:, t0 + k, b0:b0 + P] for t_ in op)
                        wk = slice(w0 + k * P, w0 + (k + 1) * P)
                        nc.tensor.matmul(dst, hi, w_hi[:, q, wk], start=k == 0, stop=False)
                        nc.tensor.matmul(dst, hi, w_lo[:, q, wk], start=False, stop=False)
                        mm = nc.tensor.matmul(dst, lo, w_hi[:, q, wk], start=False, stop=k == n - 1)
                mm.then_inc(chunk_used, 1)

            def gates(part=range(KT)):
                if 0 in part:
                    wait(pe, gate_ready, g)
                mm = feature("g", bank[3][:, 0:c1 - c0], part=part)
                if KT - 1 in part:
                    mm.then_inc(chunk_used, 1)

            return queries, keys, sides, values, gates

        def pe_scores(pe, f, p):
            g = p + 8 * f
            c0, c1 = span(f)
            pe.wait_ge(q_ready, g + 1)
            pe.wait_ge(k_ready, g + 1)
            wait(pe, o_taken, g)
            wait(pe, pt_taken, 2 * g)
            if f < 2:
                pe.wait_ge((rows_ready, kr_ready)[f], 1 if f == 1 or isinstance(p, int) and p == 0 else 2)
            for hh in range(2):
                dst = bank[5 - hh]
                r = slice(64 * hh, 64 * hh + 64)
                for (q0, q1), (s0, s1) in zip(blocks(f), s_cols(f)):
                    n = s1 - s0
                    mm = nc.tensor.matmul(dst[:, s0:s1], q_n[r, q0 - c0:q0 - c0 + P], k_n[r, 0:n],
                                          start=True, stop=f == 2)
                    if f == 0:
                        mm = nc.tensor.matmul(dst[:, s0:s1], ones_r[:], rows_a[:, p * 2 + hh, 0:n],
                                              start=False, stop=True)
                    if f == 1:
                        r2 = slice(32 * hh, 32 * hh + 32)
                        mm = nc.tensor.matmul(dst[0:q1 - q0, s0:s1], q_rp[r2, q0 - c0:q1 - c0], k_rp[r2, 0:n],
                                              start=False, stop=True)
                mm.then_inc(s_done, 1)

        def pe_transposes(pe, f, p):
            g = p + 8 * f
            sc = s_cols(f)
            for hh in range(2):
                pe.wait_ge(p_ready, 2 * g + hh + 1)
                dst = (bank[6], bank[4])[hh]
                if f == 0:
                    lay = [(1, META, META + P, 0), (2, META, META + P, P), (2, META + P, T, 2 * P)]
                else:
                    lay = [(0, 0, P, 0), (1, 0, P, P), (1, P, 2 * P, 2 * P)]
                for b, k0, k1, at in lay:
                    mm = nc.tensor.transpose(dst[0:P, at:at + P], p_e[0:P, hh, sc[b][0] + k0:sc[b][0] + k1], ident)
                if f == 0:
                    for b in (1, 2):
                        mm = nc.tensor.transpose(bank[7][0:META, 256 * hh + (b - 1) * P:256 * hh + b * P],
                                                 p_e[0:P, hh, sc[b][0]:sc[b][0] + META], ident)
                    mm = nc.tensor.transpose(dst[0:META, 384:384 + META], p_e[0:META, hh, 0:META], ident[0:META, 0:META])
                mm.then_inc(pt_done, 1)

        def pe_outputs(pe, f, p):
            g = p + 8 * f
            pe.wait_ge(v_ready, g + 1)
            pe.wait_ge(pt_taken, 2 * g + 2)
            for hh in range(2):
                dst = bank[5][64 * hh:64 * hh + 64]
                vr = slice(64 * hh, 64 * hh + 64)
                if f == 0:
                    nc.tensor.matmul(dst[:, 0:T], v_s[0:META, 0, vr], pt0[:, hh, :], start=True, stop=False)
                    nc.tensor.matmul(dst[:, META:T], v_s[:, 1, vr], pt[:, hh, 0:256], start=False, stop=False)
                    mm = nc.tensor.matmul(dst[:, META + P:T], v_s[:, 2, vr], pt[:, hh, 256:384], start=False, stop=True)
                else:
                    nc.tensor.matmul(dst[:, 0:256], v_s[:, 0, vr], pt[:, hh, 0:256], start=True, stop=False)
                    mm = nc.tensor.matmul(dst[:, 128:256], v_s[:, 1, vr], pt[:, hh, 256:384], start=False, stop=True)
            mm.then_inc(o_done, 1)

        def attention_pe(pe, f):
            def aw(pe_, k):
                if f == 1:
                    pe_.wait_ge(lat_ready, k + 1)
                elif f == 2:
                    pe_.wait_ge(x_ready, X_BASE["ln1"] + k + 1)

            def step(p):
                first = isinstance(p, int) and p == 0
                queries, keys, sides, values, gates = pe_project(pe, f, p, aw)
                queries()
                if not first:
                    pe_scores(pe, f, p - 1)
                keys()
                values()
                sides()
                before = KT // 2 if f == 1 else 0
                if before:
                    gates(range(before))
                if not first:
                    pe_transposes(pe, f, p - 1)
                gates(range(before, KT))
                if not first:
                    pe_outputs(pe, f, p - 1)

            step(0)
            step(1)
            with pe.Fori(2, PAIRS) as p:
                step(p)
            pe_scores(pe, f, PAIRS - 1)
            pe_transposes(pe, f, PAIRS - 1)
            pe_outputs(pe, f, PAIRS - 1)

        X_BASE = {"pre0": 0, "pre1": 8, "pre2": 16, "pre3": 24, "post3": 32, "ln1": 40}

        def small_pe(pe, name, dst, width):
            for q in range(4):
                weights_here(pe, name, 0, q)
                for t_ in range(2):
                    k = 2 * q + t_
                    pe.wait_ge(x_ready, {"w_forget": X_BASE["pre0"], "w_beta_a": X_BASE["pre2"],
                                         "w_k_rope": X_BASE["post3"]}[name] + k + 1)
                    mm = product(dst, q, t_ * width, x_op, k, (META, T) if name == "w_k_rope" else (0, T),
                                 k == 0, k == KT - 1)
                mm.then_inc(chunk_used, 1)

        def small_splits(eng, split, name):
            f_ = following(name, 0)
            for q in range(4):
                split(eng, *f_, q)

        def attention_act(act, st, f):
            c0, c1 = span(f)
            n = c1 - c0

            def copy_q(p):
                g = p + 8 * f
                if f == 1:
                    if not (isinstance(p, int) and p == 0):
                        act.wait_ge(s_done, 2 * g)
                    act.wait_ge(chunk_used, projected(f, p, "q"))
                    st(nc.scalar.activation(q_n[:, 0:n], bank[0][:, 0:n], ACT.Copy))
                    nc.scalar.activation(rp_raw[:, 0:n], bank[0][0:64, 256:512], ACT.Copy).then_inc(q_copied, 1)
                    return
                act.wait_ge(chunk_used, projected(f, p, "q"))
                if f == 0:
                    st(nc.scalar.activation(q_raw[:, 0:n], bank[0][:, 0:n], ACT.Copy))
                    nc.scalar.activation(q_sq[:, 0:n], bank[0][:, 0:n], ACT.Square).then_inc(q_copied, 1)
                else:
                    nc.scalar.activation(q_raw[:, 0:n], bank[0][:, 0:n], ACT.Copy).then_inc(q_copied, 1)

            def copy_k(p):
                if f == 1:
                    act.wait_ge(chunk_used, projected(f, p, "k"))
                    nc.scalar.activation(k_n[:, 0:n], bank[1][:, 0:n], ACT.Copy).then_inc(k_ready, 1)
                    return
                act.wait_ge(chunk_used, projected(f, p, "k"))
                if f == 0:
                    st(nc.scalar.activation(k_raw[:, 0:n], bank[1][:, 0:n], ACT.Copy))
                    nc.scalar.activation(k_sq[:, 0:n], bank[1][:, 0:n], ACT.Square).then_inc(k_copied, 1)
                else:
                    nc.scalar.activation(k_raw[:, 0:n], bank[1][:, 0:n], ACT.Copy).then_inc(k_copied, 1)

            def roots(p):
                if f == 0:
                    g = p
                    act.wait_ge(q_side, g + 1)
                    wait(act, q_ready, g)
                    nc.scalar.activation(q_sq[:, 0:n], bank[0][:, 0:n], ACT.Sqrt, bias=eps["rms"], scale=1.0 / 64).then_inc(qk_root, 1)
                    act.wait_ge(k_side, g + 1)
                    wait(act, k_ready, g)
                    nc.scalar.activation(k_sq[:, 0:n], bank[1][:, 0:n], ACT.Sqrt, bias=eps["rms"], scale=1.0 / 64).then_inc(qk_root, 1)

            def exps(p):
                g = p + 8 * f
                for hh in range(2):
                    act.wait_ge(max_ready, 2 * g + hh + 1)
                    bl = list(enumerate(zip(blocks(f), s_cols(f))))
                    for b, ((q0, q1), (s0, s1)) in bl:
                        r = slice(0, q1 - q0)
                        ins = nc.scalar.activation(p_e[r, hh, s0:s1], s_m[r, hh, s0:s1], ACT.Exp, bias=mx[r, hh, b:b + 1],
                                                   scale=SCALE[f], accum_out=rs[r, hh, b:b + 1])
                        if b == len(bl) - 1:
                            ins.then_inc(exp_done, 1)
                        else:
                            st(ins)

            def pt_copies(p):
                g = p + 8 * f
                for hh in range(2):
                    act.wait_ge(pt_done, 2 * g + hh + 1)
                    src = (bank[6], bank[4])[hh]
                    if f == 0:
                        nc.scalar.activation(pt0[:, hh, 0:META], src[0:META, 384:384 + META], ACT.Copy)
                        if hh:
                            nc.scalar.activation(pt0[:, :, META:T], bank[7][0:META, :].rearrange("p (h t) -> p h t", h=2),
                                                 ACT.Copy)
                    nc.scalar.activation(pt[:, hh, :], src[:, 0:384], ACT.Copy).then_inc(pt_taken, 1)

            def value_copy(p):
                g = p + 8 * f
                act.wait_ge(chunk_used, projected(f, p, "v"))
                if not (isinstance(p, int) and p == 0):
                    act.wait_ge(o_done, g)
                if f == 0:
                    nc.scalar.activation(v_s[0:META, 0, :], bank[2][0:META, 0:P], ACT.Copy)
                    nc.scalar.activation(v_s[:, 1:3, :], bank[2][:, P:3 * P], ACT.Copy).then_inc(v_ready, 1)
                else:
                    nc.scalar.activation(v_s[:, 0:2, :], bank[2][:, 0:2 * P], ACT.Copy).then_inc(v_ready, 1)
                act.wait_ge(chunk_used, projected(f, p, "g"))
                wait(act, gate_ready, g)
                nc.scalar.activation(th[:, 0:n], bank[3][:, 0:n], ACT.Tanh, scale=0.5).then_inc(th_ready, 1)

            def splits(p, qs):
                for q in qs:
                    split_hi(act, *following(name_of(f), p), q)

            copy_q(0)
            splits(0, (0,))
            copy_k(0)
            splits(0, (1, 2))
            roots(0)
            value_copy(0)
            splits(0, (3,))
            def step(p):
                if f == 1:
                    splits(p, (0,))
                    exps(p - 1)
                    copy_q(p)
                else:
                    copy_q(p)
                    splits(p, (0,))
                    exps(p - 1)
                copy_k(p)
                splits(p, (1, 2))
                roots(p)
                pt_copies(p - 1)
                value_copy(p)
                splits(p, (3,))

            nb = len(blocks(f)) - 1
            step(1)
            per = 2 * nb + (2 if f == 0 else 1 if f == 1 else 0)
            st.loop(2, PAIRS - 1, per, step)
            step(PAIRS - 1)
            exps(PAIRS - 1)
            pt_copies(PAIRS - 1)

        def attention_dve(dve, st, f):
            c0, c1 = span(f)
            n = c1 - c0
            sc = s_cols(f)
            mask = tb("mask_a") if f == 0 else tb("mask_b")

            def maxima(p):
                g = p + 8 * f
                if f == 0 and isinstance(p, int) and p == 0:
                    dve.wait_ge(tables_in, 16)
                for hh in range(2):
                    dve.wait_ge(s_done, 2 * g + hh + 1)
                    src = bank[5 - hh]
                    if f == 0:
                        r = slice(0, META)
                        st(nc.vector.tensor_tensor(s_m[r, hh, 0:META], src[r, 0:META], mask[r, 0:META], ALU.add))
                        lo = META
                    else:
                        lo = 0
                    hi = sc[-1][1]
                    nc.vector.tensor_tensor(s_m[:, hh, lo:hi], src[:, lo:hi], mask[:, lo:hi], ALU.add).then_inc(s_taken, 1)
                    dve.wait_ge(s_taken, 2 * g + hh + 1)
                    for b, ((q0, q1), (s0, s1)) in enumerate(zip(blocks(f), sc)):
                        r = slice(0, q1 - q0)
                        st(nc.vector.tensor_reduce(mx[r, hh, b:b + 1], s_m[r, hh, s0:s1], AX, ALU.max, negate=True))
                    st.settle()
                    nc.vector.tensor_scalar(mx[:, hh, :], mx[:, hh, :], SCALE[f], None, ALU.mult).then_inc(max_ready, 1)

            def norm(p, which):
                g = p + 8 * f
                raw, t_, dst, side, ready, bk = {
                    "q": (q_raw, q_sq, q_n, q_side, q_ready, 0), "k": (k_raw, k_sq, k_n, k_side, k_ready, 1)}[which]
                if which == "q":
                    wait(dve, k_ready, g)
                elif f == 0:
                    dve.wait_ge(q_ready, g + 1)
                if f == 0:
                    dve.wait_ge(qk_root, 2 * g + (1 if which == "q" else 2))
                    st(nc.vector.reciprocal(t_sin[:, 0:n], t_[:, 0:n]))
                    st.settle()
                    gain = pr("q_gain" if which == "q" else "k_gain")
                    nc.vector.scalar_tensor_tensor(dst[:, 0:n], raw[:, 0:n], gain, t_sin[:, 0:n], ALU.mult,
                                                   ALU.mult).then_inc(ready, 1)
                    return
                if f == 1:
                    if which == "k":
                        return
                    raw, dst, src, rr = rp_raw, q_rp, bank[0][0:64, 256:512], slice(0, 64)
                    cos, sin = tb("cos32"), tb("sin32")
                else:
                    src, rr = bank[bk][:, 0:n], slice(0, P)
                    cos, sin = tb("cos64"), tb("sin64")
                dve.wait_ge(side, g + 1)
                st(nc.vector.tensor_tensor(t_sin[rr, 0:n], src, sin, ALU.mult))
                st(nc.vector.tensor_tensor(dst[rr, 0:n], raw[rr, 0:n], cos, ALU.mult))
                st.settle()
                nc.vector.tensor_tensor(dst[rr, 0:n], dst[rr, 0:n], t_sin[rr, 0:n], ALU.add).then_inc(ready, 1)

            def norm_k(p):
                if f == 2:
                    dve.wait_ge(q_ready, p + 17)
                    dve.wait_ge(k_side, p + 9)
                    st(nc.vector.tensor_tensor(t_sin[:, 0:n], bank[1][:, 0:n], tb("sin64"), ALU.mult))
                    st(nc.vector.tensor_tensor(k_n[:, 0:n], k_raw[:, 0:n], tb("cos64"), ALU.mult))
                    st.settle()
                    nc.vector.tensor_tensor(k_n[:, 0:n], k_n[:, 0:n], t_sin[:, 0:n], ALU.add).then_inc(k_ready, 1)
                else:
                    norm(p, "k")

            def probs(p):
                g = p + 8 * f
                for hh in range(2):
                    dve.wait_ge(exp_done, 2 * g + hh + 1)
                    st(nc.vector.reciprocal(ri[:, hh, :], rs[:, hh, :]))
                    st.settle()
                    for b, ((q0, q1), (s0, s1)) in enumerate(zip(blocks(f), sc)):
                        r = slice(0, q1 - q0)
                        ins = nc.vector.tensor_scalar(p_e[r, hh, s0:s1], p_e[r, hh, s0:s1], ri[r, hh, b:b + 1], None, ALU.mult)
                        if b == len(sc) - 1:
                            ins.then_inc(p_ready, 1)

            def outputs(p):
                g = p + 8 * f
                dve.wait_ge(o_done, g + 1)
                wait(dve, o_ready, g)
                st(nc.vector.scalar_tensor_tensor(o_tmp[:, 0:n], bank[5][:, 0:n], 0.5, gate[:, 0:n], ALU.mult, ALU.mult))
                nc.vector.scalar_tensor_tensor(o_hi[:, p, c0:c1], bank[5][:, 0:n], 0.5, gate[:, 0:n],
                                               ALU.mult, ALU.mult).then_inc(o_taken, 1)

            def outputs_lo(p):
                g = p + 8 * f
                dve.wait_ge(o_taken, g + 1)
                nc.vector.tensor_tensor(o_lo[:, p, c0:c1], o_tmp[:, 0:n], o_hi[:, p, c0:c1].bitcast(F32),
                                        ALU.subtract).then_inc(o_ready, 1)

            def gates(p):
                g = p + 8 * f
                dve.wait_ge(th_ready, g + 1)
                wait(dve, o_taken, g)
                if f == 0:
                    nc.vector.tensor_scalar(gate[:, 0:n], th[:, 0:n], 1.0, None, ALU.add).then_inc(gate_ready, 1)
                else:
                    nc.vector.scalar_tensor_tensor(gate[:, 0:n], th[:, 0:n], 1.0, bank[3][:, 0:n], ALU.add,
                                                   ALU.mult).then_inc(gate_ready, 1)

            def splits(p, qs):
                for q in qs:
                    split_lo(dve, *following(name_of(f), p), q)

            splits(0, (0, 1, 2))
            if f == 0:
                z = sp_c[0:16]
                dve.wait_ge(ln_done, 1)
                dve.wait_ge(z_known, 1)
                st(nc.vector.scalar_tensor_tensor(sp_b[0:16], z, 0.0, sp_a[0:16], ALU.min, ALU.subtract))
                st.settle()
                st(nc.vector.tensor_tensor_scan(z, one_row[0:16, 0:T], sp_b[0:16], 0.0, ALU.mult, ALU.add))
                st.settle()
                st(nc.vector.memset(c_2[:], 0.0))
                st(nc.vector.tensor_scalar(sp_b[0:16], z, -8.0, None, ALU.mult))
                st.settle()
                st(nc.vector.tensor_scalar(rows_a[0:16, 0, :], z, -8.0, None, ALU.mult))
                st.settle()
                st(nc.vector.tensor_copy(c_2[0:16], rows_a[0:16, 0, :].bitcast(F32)))
                st(nc.vector.tensor_tensor(c_2[32:48], sp_b[0:16], rows_a[0:16, 0, :].bitcast(F32), ALU.subtract))
                st.settle()
                nc.vector.tensor_tensor(rows_a[:, 0:2, :], c_2[:].unsqueeze(1).to_broadcast([P, 2, T]),
                                        tb("own_head_a")[:, 0:2].unsqueeze(2).to_broadcast([P, 2, T]),
                                        ALU.mult).then_inc(rows_ready, 1)
            norm(0, "q")
            norm_k(0)
            gates(0)
            splits(0, (3,))
            def step(p):
                splits(p, (0,))
                maxima(p - 1)
                probs(p - 1)
                splits(p, (1, 2))
                norm(p, "q")
                norm_k(p)
                outputs(p - 1)
                outputs_lo(p - 1)
                gates(p)
                splits(p, (3,))

            per = 1 + (2 if f == 0 else 0) + 2 * len(sc) + 2 + {0: 2, 1: 2, 2: 4}[f]
            step(1)
            st.loop(2, PAIRS - 1, per, step)
            step(PAIRS - 1)
            maxima(PAIRS - 1)
            probs(PAIRS - 1)
            outputs(PAIRS - 1)
            outputs_lo(PAIRS - 1)

        one_row = sb("one_row", [T], 64)
        bg_split = sem("bg_split")

        def ffn_span(f):
            return (0, T) if f == 0 else (META - CONV_PAST, T)

        def ffn_pe(pe, f):
            cols = c0, c1 = ffn_span(f)
            name = f"w_up{f}"

            def unit(u):
                for r in range(2):
                    g = u * 2 + (r + FT * f)
                    if not (isinstance(u, int) and u == 0 and f == 0):
                        pe.wait_ge(conv_done, g - 1)
                    for half in range(2):
                        q = 2 * r + half
                        weights_here(pe, name, u, q)
                        for k in range(KT):
                            if isinstance(u, int) and u == 0 and q == 0:
                                pe.wait_ge(x_ready, X_BASE[f"pre{2 * f + 1}"] + k + 1)
                            mm = product(bank[q][:, c0:c1], q, k * P, x_op, k, cols, k == 0, k == KT - 1)
                        mm.then_inc(chunk_used, 1)

            unit(0)
            with pe.Fori(1, FT // 2) as u:
                unit(u)

            def hid_wait(pe_, k):
                pe_.wait_ge(hid_ready, FT * f + k + 1)

            out_pe(pe, f"w_down{f}", f"post{2 * f + 1}", hid_op, FT, (0, T) if f == 0 else (META, T), hid_wait)

        def conv_w(f, j, half, tap):
            cw = pr("ffn_conv").rearrange("p (f j a t) -> p f j a t", f=2, j=FT, a=2)
            return cw[:, f, j, half, tap:tap + 1]

        def ffn_act(act, st, f):
            c0, c1 = ffn_span(f)
            o0 = 0 if f == 0 else META

            def taps(u, r):
                g = u * 2 + (r + FT * f)
                for half, y in ((0, g_y), (1, u_y)):
                    act.wait_ge(chunk_used, chunk(f"w_up{f}", u, 2 * r + half) + 1)
                    if half == 0 and not (isinstance(u, int) and u == 0 and f == 0):
                        act.wait_ge(prod_ready, g - 1)
                    nc.scalar.activation(y[:, r, o0:T], bank[2 * r + half][:, o0:T], ACT.Copy,
                                         scale=conv_w(f, u * 2 + r, half, 2)).then_inc(tap_ready, 1)

            def rest(u, r):
                g = u * 2 + (r + FT * f)
                split_hi(act, *following(f"w_up{f}", u), 2 * r)
                act.wait_ge(conv_done, g + 1)
                nc.scalar.activation(g_e[:, r, o0:T], g_y[:, r, o0:T], ACT.Gelu_apprx_tanh).then_inc(gelu_done, 1)
                split_hi(act, *following(f"w_up{f}", u), 2 * r + 1)
                act.wait_ge(prod_ready, g + 1)
                nc.scalar.activation(hid_op[0][:, u * 2 + r, o0:T], hid[:, r, o0:T], ACT.Copy).then_inc(hid_hi_ready, 1)

            def unit(u):
                for r in range(2):
                    taps(u, r)
                    rest(u, r)

            unit(0)
            with act.Fori(1, FT // 2 - 1) as u:
                unit(u)
            unit(FT // 2 - 1)
            out_act(act, f"w_down{f}", f"post{2 * f + 1}", (0, T) if f == 0 else (META, T))

        def ffn_dve(dve, st, f):
            o0 = 0 if f == 0 else META

            def step(u, r):
                g = u * 2 + (r + FT * f)
                j = u * 2 + r
                dve.wait_ge(tap_ready, g * 2 + 2)
                for back in (1, 2):
                    lo = max(o0, back)
                    for half, y in ((0, g_y), (1, u_y)):
                        ins = nc.vector.scalar_tensor_tensor(y[:, r, lo:T], bank[2 * r + half][:, lo - back:T - back],
                                                             conv_w(f, j, half, 2 - back), y[:, r, lo:T], ALU.mult, ALU.add)
                        if back == 1:
                            st(ins)
                        elif half == 1:
                            ins.then_inc(conv_done, 1)
                    if back == 1:
                        st.settle()
                split_lo(dve, *following(f"w_up{f}", u), 2 * r)
                split_lo(dve, *following(f"w_up{f}", u), 2 * r + 1)
                dve.wait_ge(hid_hi_ready, g + 1)
                nc.vector.tensor_tensor(hid_op[1][:, j, o0:T], hid[:, r, o0:T], hid_op[0][:, j, o0:T].bitcast(F32),
                                        ALU.subtract).then_inc(hid_ready, 1)

            def unit(u):
                for r in range(2):
                    step(u, r)

            unit(0)
            st.loop(1, FT // 2 - 1, 4, unit)
            unit(FT // 2 - 1)
            out_dve(dve, f"w_down{f}")

        def ffn_pool(pool, f):
            o0 = 0 if f == 0 else META

            def unit(u):
                for r in range(2):
                    g = u * 2 + (r + FT * f)
                    pool.wait_ge(gelu_done, g + 1)
                    if not (isinstance(u, int) and u == 0 and f == 0):
                        pool.wait_ge(hid_ready, g - 1)
                    nc.gpsimd.tensor_tensor(hid[:, r, o0:T], g_e[:, r, o0:T], u_y[:, r, o0:T], ALU.mult).then_inc(prod_ready, 1)

            unit(0)
            with pool.Fori(1, FT // 2) as u:
                unit(u)

        def dn_pe(pe):
            def feature(d, which):
                weights_here(pe, "w_dn", d, which)
                for k in range(KT):
                    mm = product(bank[which][:, 0:T], which, k * P, x_op, k, (0, T), k == 0, k == KT - 1)
                mm.then_inc(chunk_used, 1)

            def prepare(d):
                pe.wait_ge(dn["st"], 2 * d + 2)
                pe.wait_ge(dn["v_st"], d + 1)
                pe.wait_ge(rows_ready, 3)
                pe.wait_ge(dn["bgt_out"], 1)
                wait(pe, dn["kt_out"], 3 * d)
                wait(pe, dn["at"], d)
                wait(pe, dn["qk"], d)
                nc.tensor.matmul(bank[4][:, 0:TP], sum_gc_r[:], rows_d[:, d, :], start=True, stop=True).then_inc(dn["row"], 1)
                for c in range(NC):
                    mm = nc.tensor.transpose(bank[5][0:C, c * P:(c + 1) * P], v_st[:, c * C:(c + 1) * C], ident)
                mm.then_inc(dn["vt"], 1)
                for b, src in ((6, k_st), (7, q_st)):
                    for c in range(NC):
                        cc = slice(c * C, (c + 1) * C)
                        mm = nc.tensor.matmul(bank[b][0:C, cc], k_st[:, cc], src[:, cc], start=True, stop=True)
                mm.then_inc(dn["kk"], 1)

            def prepare_keys(d):
                pe.wait_ge(dn["vt_out"], 3 * d + 3)
                for c in range(NC):
                    mm = nc.tensor.transpose(bank[5][0:C, c * P:(c + 1) * P], k_st[:, c * C:(c + 1) * C], ident)
                mm.then_inc(dn["kt"], 1)
                pe.wait_ge(dn["erow"], d + 1)
                pe.wait_ge(dn["dec_t"], 3 * d + 3)
                nc.tensor.matmul(bank[4][0:C, 0:TP], sum_beta_r[:], rows_d[:, d, :], start=True, stop=True).then_inc(dn["beta"], 1)

            def step(d):
                first = isinstance(d, int) and d == 0
                for which, b in ((0, 0), (1, 1), (2, 2)):
                    if which < 2:
                        wait(pe, dn["root"], 2 * d + which - 1 if not first else 0)
                    else:
                        wait(pe, dn["conv"], 3 * d if not first else 0)
                    feature(d, which)
                if not first:
                    prepare(d - 1)
                    pe.wait_ge(dn["gate"], d)
                feature(d, 3)
                pe.wait_ge(dn["conv"], 3 * d + 1)
                pe.wait_ge(dn["sq"], 2 * d + 1)
                nc.tensor.matmul(bank[0][:, 0:T], ones, q_sq[:, 0:T], start=True, stop=True).then_inc(dn["ssq"], 1)
                pe.wait_ge(dn["conv"], 3 * d + 2)
                pe.wait_ge(dn["sq"], 2 * d + 2)
                nc.tensor.matmul(bank[1][:, 0:T], ones, k_sq[:, 0:T], start=True, stop=True).then_inc(dn["ssq"], 1)
                if not first:
                    prepare_keys(d - 1)

            small_pe(pe, "w_beta_a", bank[4][:, 0:T], 64)
            step(0)
            pe.wait_ge(dn["bg"], 2)
            for c in range(NC):
                mm = nc.tensor.transpose(bank[5][0:C, c * 64:(c + 1) * 64], bg[0:64, c * C:(c + 1) * C], ident[0:64, 0:64])
            mm.then_inc(dn["bgt"], 1)
            step(1)
            with pe.Fori(2, DNH) as d:
                step(d)
            prepare(DNH - 1)
            prepare_keys(DNH - 1)

            pe.wait_ge(dn["gate"], DNH)
            pe.wait_ge(dn["kt_out"], NC * DNH)

            def x_of(n):
                pe.wait_ge(dn["d_in"], n - DNH + 1)
                wait(pe, dn["x_out"], n - DNH - 1)
                for c in range(NC):
                    cc = slice(c * C, (c + 1) * C)
                    mm = nc.tensor.matmul(bank[n % 2][0:C, cc], a_tr[:, n % DNH, cc], d_in[:, n % DNH, cc], start=True, stop=True)
                mm.then_inc(dn["x"], 1)

            def update(n):
                pe.wait_ge(dn["x_out"], n - DNH + 1)
                pe.wait_ge(dn["d"], n - 1)
                for c in range(NC):
                    cc = slice(c * C, (c + 1) * C)
                    mm = nc.tensor.matmul(bank[2 + n % 2][0:C, cc], x_slot(n)[:, cc], d_tr[:, n % DNH, cc], start=True, stop=True)
                mm.then_inc(dn["dd"], 1)

            def turn(n):
                pe.wait_ge(dn["d"], n + 1)
                wait(pe, dn["d_in"], n - 1)
                for c in range(NC):
                    cc = slice(c * C, (c + 1) * C)
                    mm = nc.tensor.transpose(bank[4 + n % 2][0:C, cc], d_tr[:, n % DNH, cc], ident[0:C, 0:C])
                mm.then_inc(dn["t"], 1)

            for n in range(LEVELS * DNH + 3):
                if DNH <= n < LEVELS * DNH:
                    x_of(n)
                if DNH <= n - 1 < LEVELS * DNH:
                    update(n - 1)
                back = n - (0 if n < DNH else 2)
                if n < DNH or DNH <= back < (LEVELS - 1) * DNH:
                    turn(back)

            def squares(hd):
                pe.wait_ge(dn["osq"], hd + 1)
                if hd == 0:
                    pe.wait_ge(dn["s_new"], 2 * DNH)
                nc.tensor.matmul(bank[6][0:DNH, 0:T], tb("row_of")[:, hd * DNH:(hd + 1) * DNH], sq[:, hd % 2, :],
                                 start=hd == 0, stop=hd == DNH - 1).then_inc(dn["osum"], 1)

            for c in range(NC):
                cc = slice(c * C, (c + 1) * C)

                def first_half(hd):
                    g = c * DNH + hd
                    if c:
                        pe.wait_ge(dn["s_new"], g - DNH + 1)
                        wait(pe, dn["r"], g - 1 - DNH)
                        nc.tensor.matmul(bank[hd % 2][0:C, 0:P], kn_all[:, hd, cc], s_t[:, hd, :], start=True,
                                         stop=True).then_inc(dn["ks"], 1)

                def second_half(hd):
                    g = c * DNH + hd
                    if c:
                        pe.wait_ge(dn["r"], g + 1 - DNH)
                        rhs = r_st[:, hd % 2, :]
                    else:
                        rhs = vb_all[:, hd, 0, :]
                        if hd == 0:
                            pe.wait_ge(dn["d"], LEVELS * DNH)
                    wait(pe, dn["u_out"], g - 1)
                    nc.tensor.matmul(bank[2 + hd % 2][0:C, 0:P], d_tr[:, hd, cc], rhs, start=True, stop=True).then_inc(dn["u"], 1)

                def third(hd):
                    g = c * DNH + hd
                    pe.wait_ge(dn["u_out"], g + 1)
                    wait(pe, dn["o_out"], g - 1)
                    if c:
                        nc.tensor.matmul(bank[4 + hd % 2][:, 0:C], s_t[:, hd, :], qd_all[:, hd, cc], start=True, stop=False)
                    nc.tensor.matmul(bank[4 + hd % 2][:, 0:C], u_st[:, hd % 2, :], qk_all[:, hd, cc], start=c == 0,
                                     stop=True).then_inc(dn["o"], 1)
                    if c < NC - 1:
                        wait(pe, dn["s_new"], g - 1)
                        nc.tensor.matmul(bank[6 + hd % 2][:, 0:P], kd_all[:, hd, c, :], u_st[:, hd % 2, :], start=True,
                                         stop=True).then_inc(dn["s_up"], 1)

                for hd in range(DNH + (2 if c < NC - 1 else 4)):
                    if hd < DNH:
                        first_half(hd)
                    if 0 <= hd - 1 < DNH:
                        second_half(hd - 1)
                    if 0 <= hd - 2 < DNH:
                        third(hd - 2)
                    if c == NC - 1 and hd >= 4:
                        squares(hd - 4)

            pe.wait_ge(dn["oinv"], 1)
            for hd in range(DNH):
                wait(pe, dn["onorm"], hd - 1)
                nc.tensor.matmul(bank[4 + hd % 2][:, 0:T], tb("row_to")[:, hd * P:(hd + 1) * P], rstd[0:DNH, 0:T],
                                 start=True, stop=True).then_inc(dn["ospread"], 1)

            def o_wait(pe_, k):
                pe_.wait_ge(dn["olo"], k + 1)
            out_pe(pe, "w_dn_out", "post2", o_op, KT, (META - CONV_PAST, T), o_wait)

        def dn_conv_w(d, which, tap):
            cw = pr("dn_conv").rearrange("p (h a t) -> p h a t", h=DNH, a=3)
            return cw[:, d, which, tap:tap + 1]

        def dn_act(act, st):
            bb = slice(32, 40)
            small_splits(act, split_hi, "w_beta_a")
            act.wait_ge(chunk_used, chunk("w_beta_a", 0, 3) + 1)
            act.wait_ge(dn["zero"], 1)
            nc.scalar.activation(bg[0:8, PAD:TP], bank[4][0:8, 0:T], ACT.Sigmoid).then_inc(dn["bg"], 1)
            act.wait_ge(z_known, 2)
            st(nc.scalar.activation(sd_a[bb], sd_c[bb], ACT.Abs))
            st.settle()
            st(nc.scalar.activation(sd_b[bb], sd_a[bb], ACT.Exp, scale=-1.0))
            nc.scalar.activation(neg_a[bb], pr("a_log")[bb], ACT.Exp).then_inc(dn["negexp"], 1)
            st.settle()
            nc.scalar.activation(sd_a[bb], sd_b[bb], ACT.Ln, bias=ones[bb, 0:1]).then_inc(ln_done, 1)

            def tap(d, which, y):
                act.wait_ge(chunk_used, chunk("w_dn", d, which) + 1)
                nc.scalar.activation(y[:, 0:T], bank[which][:, 0:T], ACT.Copy, scale=dn_conv_w(d, which, 3)).then_inc(dn["tap"], 1)

            def silu_sq(d, which, y, s):
                act.wait_ge(dn["conv"], 3 * d + which + 1)
                st(nc.scalar.activation(y[:, 0:T], y[:, 0:T], ACT.Silu))
                st.settle()
                nc.scalar.activation(s[:, 0:T], y[:, 0:T], ACT.Square).then_inc(dn["sq"], 1)

            def main(d):
                first = isinstance(d, int) and d == 0
                wait(act, dn["st"], 2 * d if not first else 0)
                tap(d, 0, q_y)
                tap(d, 1, k_y)
                silu_sq(d, 0, q_y, q_sq)
                silu_sq(d, 1, k_y, k_sq)
                wait(act, dn["v_st"], d)
                tap(d, 2, v_y)

            def value(d):
                act.wait_ge(dn["conv"], 3 * d + 3)
                if not (isinstance(d, int) and d == 0):
                    act.wait_ge(dn["vt"], d)
                nc.scalar.activation(v_st[:, PAD:TP], v_y[:, 0:T], ACT.Silu).then_inc(dn["v_st"], 1)

            def roots(d):
                for which, s in ((0, q_sq), (1, k_sq)):
                    act.wait_ge(dn["ssq"], 2 * d + which + 1)
                    nc.scalar.activation(s[:, 0:T], bank[which][:, 0:T], ACT.Sqrt, bias=eps["rms"]).then_inc(dn["root"], 1)

            def out_gate(d):
                act.wait_ge(chunk_used, chunk("w_dn", d, 3) + 1)
                nc.scalar.activation(o_gate[:, d, :], bank[3][:, 0:T], ACT.Silu).then_inc(dn["gate"], 1)

            def prep_values(d):
                act.wait_ge(dn["vt"], d + 1)
                for c in range(NC):
                    nc.scalar.activation(vb_all[:, d, c, :], bank[5][0:C, c * P:(c + 1) * P], ACT.Copy,
                                         scale=bg_t[:, c, bass.ds(d, 1)]).then_inc(dn["vt_out"], 1)

            def prep_decays(d):
                act.wait_ge(dn["dec_t"], 3 * d + 3)
                wait(act, dn["qd"], d)
                st.settle()
                nc.scalar.activation(e_row[:], bank[4][:, 0:TP], ACT.Exp).then_inc(dn["erow"], 1)
                nc.scalar.activation(dec[:], t_dec[:], ACT.Exp).then_inc(dn["dec"], 1)
                act.wait_ge(dn["erow"], d + 1)
                st(nc.scalar.activation(g_last[:, d, :], e_row[:].rearrange("p (c t) -> p c t", c=NC)[:, :, C - 1],
                                        ACT.Copy))

            def prep_keys(d):
                act.wait_ge(dn["kt"], d + 1)
                act.wait_ge(dn["dec"], d + 1)
                for c in range(NC):
                    nc.scalar.activation(kd_all[:, d, c, :], bank[5][0:C, c * P:(c + 1) * P], ACT.Copy,
                                         scale=dec[:, (c + 1) * C - 1:(c + 1) * C]).then_inc(dn["kt_out"], 1)

            def splits(d, qs):
                for q in qs:
                    split_hi(act, *following("w_dn", d), q)

            main(0)
            splits(0, (0, 1, 2))
            value(0)
            roots(0)
            out_gate(0)
            splits(0, (3,))
            act.wait_ge(dn["bgt"], 1)
            nc.scalar.activation(bg_t[:], bank[5][0:C, 0:NC * 64], ACT.Copy).then_inc(dn["bgt_out"], 1)
            act.wait_ge(dn["bgt_out"], 1)
            nc.scalar.activation(eg_t[:], bg_t[:, :, 32:40], ACT.Exp).then_inc(dn["eg"], 1)

            def step(d):
                main(d)
                splits(d, (0,))
                prep_values(d - 1)
                value(d)
                prep_decays(d - 1)
                st(nc.scalar.activation(prime_out[:], eps["rms"], ACT.Sqrt))
                roots(d)
                splits(d, (1,))
                prep_keys(d - 1)
                splits(d, (2,))
                out_gate(d)
                splits(d, (3,))

            step(1)
            st.loop(2, DNH - 1, 4, step)
            step(DNH - 1)
            prep_values(DNH - 1)
            prep_decays(DNH - 1)
            prep_keys(DNH - 1)

            for n in range((LEVELS - 1) * DNH):
                act.wait_ge(dn["t"], n + 1)
                src, dst = by_chunk(bank[4 + n % 2][0:C, 0:TP]), by_chunk(d_in[:, n % DNH, :])
                if n >= DNH:
                    src, dst = lower(src, n // DNH), lower(dst, n // DNH)
                nc.scalar.activation(dst, src, ACT.Copy).then_inc(dn["d_in"], 1)

            for c in range(NC):
                for hd in range(DNH + (1 if c < NC - 1 else 2)):
                    if hd < DNH:
                        g = c * DNH + hd
                        act.wait_ge(dn["u"], g + 1)
                        if g >= 2:
                            act.wait_ge(dn["o"], g - 1)
                            act.wait_ge(dn["s_up"], min(g - 1, 2 * DNH))
                        nc.scalar.activation(u_st[:, hd % 2, :], bank[2 + hd % 2][0:C, 0:P], ACT.Copy).then_inc(dn["u_out"], 1)
                    if 1 <= hd <= DNH:
                        g = c * DNH + hd - 1
                        act.wait_ge(dn["o"], g + 1)
                        nc.scalar.activation(o_raw[:, hd - 1, c * C:(c + 1) * C], bank[4 + (hd - 1) % 2][:, 0:C],
                                             ACT.Copy).then_inc(dn["o_out"], 1)
                    if c == NC - 1 and hd >= 2:
                        act.wait_ge(dn["o_out"], 2 * DNH + hd - 1)
                        wait(act, dn["osum"], hd - 3)
                        nc.scalar.activation(sq[:, hd % 2, :], o_raw[:, hd - 2, PAD:TP], ACT.Square).then_inc(dn["osq"], 1)
            act.wait_ge(dn["osum"], DNH)
            nc.scalar.activation(root[0:DNH, 0:T], bank[6][0:DNH, 0:T], ACT.Sqrt, bias=eps["rms"][0:DNH],
                                 scale=1.0 / P).then_inc(dn["oroot"], 1)
            for hd in range(DNH):
                act.wait_ge(dn["ot"], hd + 1)
                nc.scalar.activation(o_hi[:, hd, :], o_gate[:, hd, :], ACT.Copy).then_inc(dn["ohi"], 1)
            out_act(act, "w_dn_out", "post2", (META - CONV_PAST, T))

        def dn_dve(dve, st):
            bb = slice(32, 40)
            small_splits(dve, split_lo, "w_beta_a")
            dve.wait_ge(chunk_used, chunk("w_beta_a", 0, 3) + 1)
            nc.vector.tensor_scalar(sd_c[bb], bank[4][bb, 0:T], pr("dt_bias")[bb], None, ALU.add).then_inc(z_known, 1)
            dve.wait_ge(dn["negexp"], 1)
            st(nc.vector.tensor_scalar(neg_a[bb], neg_a[bb], -1.0, None, ALU.mult))
            dve.wait_ge(ln_done, 2)
            st.settle()
            st(nc.vector.scalar_tensor_tensor(sd_c[bb], sd_c[bb], 0.0, sd_a[bb], ALU.max, ALU.add))
            st.settle()
            dve.wait_ge(dn["zero"], 1)
            st(nc.vector.tensor_scalar(g_pad[bb, PAD:TP], sd_c[bb], neg_a[bb], None, ALU.mult))
            st.settle()
            for c in range(NC):
                cc = slice(c * C, (c + 1) * C)
                ins = nc.vector.tensor_tensor_scan(bg[bb, cc], one_row[bb, 0:C], g_pad[bb, cc], 0.0, ALU.mult, ALU.add)
                st(ins) if c < NC - 1 else ins.then_inc(dn["bg"], 1)

            def conv(d, which, y):
                dve.wait_ge(dn["tap"], 3 * d + which + 1)
                for back in (1, 2, 3):
                    ins = nc.vector.scalar_tensor_tensor(y[:, back:T], bank[which][:, 0:T - back], dn_conv_w(d, which, 3 - back),
                                                         y[:, back:T], ALU.mult, ALU.add)
                    if back < 3:
                        st(ins)
                        st.settle()
                    else:
                        ins.then_inc(dn["conv"], 1)

            def norms(d):
                for which, (y, s, dst, scale) in enumerate(((q_y, q_sq, q_st, P ** -0.5), (k_y, k_sq, k_st, 1.0))):
                    dve.wait_ge(dn["root"], 2 * d + which + 1)
                    wait(dve, dn["st"], 2 * d + which)
                    st(nc.vector.reciprocal(t_sin[:, 0:T], s[:, 0:T]))
                    st.settle()
                    if which == 0 and not (isinstance(d, int) and d == 0):
                        dve.wait_ge(dn["kt"], d)
                        dve.wait_ge(dn["qd"], d)
                        dve.wait_ge(dn["kcopy"], d)
                    nc.vector.scalar_tensor_tensor(dst[:, PAD:TP], y[:, 0:T], scale, t_sin[:, 0:T], ALU.mult,
                                                   ALU.mult).then_inc(dn["st"], 1)

            def prep_decays(d):
                dve.wait_ge(dn["row"], d + 1)
                wait(dve, dn["dec"], d)
                for c in range(NC):
                    cc = slice(c * C, (c + 1) * C)
                    nc.vector.scalar_tensor_tensor(t_dec[:, cc], bank[4][0:C, cc], bg_t[:, c, bass.ds(d + 32, 1)], tb("later"),
                                                   ALU.subtract, ALU.add).then_inc(dn["dec_t"], 1)

            def prep(d):
                dve.wait_ge(dn["erow"], d + 1)
                nc.vector.tensor_tensor(qd_all[:, d, :], q_st[:], e_row[:], ALU.mult).then_inc(dn["qd"], 1)
                nc.vector.tensor_copy(kn_all[:, d, :], k_st[:]).then_inc(dn["kcopy"], 1)
                dve.wait_ge(dn["dec"], d + 1)
                dve.wait_ge(dn["kk"], d + 1)
                nc.vector.tensor_tensor(at_1[:], bank[6][0:C, 0:TP], dec[:], ALU.mult).then_inc(dn["a1"], 1)
                nc.vector.tensor_tensor(qk_all[:, d, :], bank[7][0:C, 0:TP], dec[:], ALU.mult).then_inc(dn["qk"], 1)
                dve.wait_ge(dn["a2"], d + 1)
                dve.wait_ge(dn["beta"], d + 1)
                nc.vector.tensor_tensor(a_tr[:, d, :], at_2[:], bank[4][0:C, 0:TP], ALU.mult).then_inc(dn["at"], 1)

            def convs(d):
                conv(d, 0, q_y)
                conv(d, 1, k_y)
                if not (isinstance(d, int) and d == 0):
                    split_lo(dve, "w_dn", d, 3)
                conv(d, 2, v_y)

            def splits(d, qs):
                for q in qs:
                    split_lo(dve, *following("w_dn", d), q)

            convs(0)
            splits(0, (0, 1, 2))
            norms(0)
            dve.wait_ge(dn["bg"], 2)
            st.settle()
            st(nc.vector.tensor_copy(rows_d[0:64, 0, :], bg[0:64]))
            st.settle()
            nc.vector.tensor_tensor(bg[64:128], bg[0:64], rows_d[0:64, 0, :].bitcast(F32), ALU.subtract).then_inc(bg_split, 1)
            dve.wait_ge(bg_split, 1)
            dve.wait_ge(dn["bgt"], 1)
            st(nc.vector.tensor_copy(bg[0:64], rows_d[0:64, 0, :].bitcast(F32)))
            st.settle()
            nc.vector.tensor_tensor(rows_d[:], bg[:].unsqueeze(1).to_broadcast([P, DNH, TP]),
                                    tb("own_head").unsqueeze(2).to_broadcast([P, DNH, TP]), ALU.mult).then_inc(rows_ready, 1)
            dve.wait_ge(dn["eg"], 1)
            st(nc.vector.scalar_tensor_tensor(nbz[:], eg_t[:], -1.0, bg_t[:, :, 0:8], ALU.mult, ALU.mult))

            def step(d):
                convs(d)
                prep_decays(d - 1)
                splits(d, (0,))
                prep(d - 1)
                last = isinstance(d, int) and d == DNH - 1
                if not last:
                    splits(d, (1,))
                norms(d)
                splits(d, (1, 2, 3) if last else (2,))
            step(1)
            st.loop(2, DNH - 1, 8, step)
            step(DNH - 1)
            prep_decays(DNH - 1)
            prep(DNH - 1)

            dve.wait_ge(dn["kt_out"], NC * DNH)
            for n in range(DNH):
                dve.wait_ge(dn["pair"], n + 1)
                nc.vector.tensor_tensor(by_chunk(d_tr[:, n, :]), tb("ident_c").unsqueeze(1).to_broadcast([C, NC, C]),
                                        by_chunk(x_st[:, n % 4, :]), ALU.subtract).then_inc(dn["d"], 1)
            for n in range(DNH, LEVELS * DNH + 1):
                if n < LEVELS * DNH:
                    lv = n // DNH
                    dve.wait_ge(dn["clear"], lv)
                    wait(dve, dn["dd"], n - DNH - 1)
                    dve.wait_ge(dn["x"], n - DNH + 1)
                    masks = tb("levels")[:, (lv - 1) * C:lv * C].unsqueeze(1).to_broadcast([C, NC, C])
                    nc.vector.tensor_tensor(lower(by_chunk(x_slot(n)), lv), lower(by_chunk(bank[n % 2][0:C, 0:TP]), lv),
                                            lower(masks, lv), ALU.mult).then_inc(dn["x_out"], 1)
                if n > DNH:
                    k, lv = n - 1, (n - 1) // DNH
                    dve.wait_ge(dn["dd"], k - DNH + 1)
                    nc.vector.tensor_tensor(upper(by_chunk(d_tr[:, k % DNH, :]), lv), upper(by_chunk(d_tr[:, k % DNH, :]), lv),
                                            upper(by_chunk(bank[2 + k % 2][0:C, 0:TP]), lv), ALU.subtract).then_inc(dn["d"], 1)

            for c in range(NC):
                def residual(hd):
                    g = (c - 1) * DNH + hd
                    dve.wait_ge(dn["ks"], g + 1)
                    dve.wait_ge(dn["u"], c * DNH + hd - 1)
                    nc.vector.scalar_tensor_tensor(r_st[:, hd % 2, :], bank[hd % 2][0:C, 0:P], nbz[:, c, hd:hd + 1],
                                                   vb_all[:, hd, c, :], ALU.mult, ALU.add).then_inc(dn["r"], 1)

                def state(hd):
                    g = c * DNH + hd
                    dve.wait_ge(dn["s_up"], g + 1)
                    if c == 0:
                        nc.vector.tensor_copy(s_t[:, hd, :], bank[6 + hd % 2][:, 0:P]).then_inc(dn["s_new"], 1)
                    else:
                        nc.vector.scalar_tensor_tensor(s_t[:, hd, :], s_t[:, hd, :], g_last[:, hd, c:c + 1],
                                                       bank[6 + hd % 2][:, 0:P], ALU.mult, ALU.add).then_inc(dn["s_new"], 1)
                for hd in range(DNH + 2):
                    if hd < DNH and c:
                        residual(hd)
                    if hd >= 2 and c < NC - 1:
                        state(hd - 2)
            dve.wait_ge(dn["oroot"], 1)
            nc.vector.reciprocal(rstd[0:DNH], root[0:DNH]).then_inc(dn["oinv"], 1)
            for hd in range(DNH + 2):
                if hd < DNH:
                    dve.wait_ge(dn["ospread"], hd + 1)
                    nc.vector.scalar_tensor_tensor(o_raw[:, hd, PAD:TP], o_raw[:, hd, PAD:TP], pr("o_gain"),
                                                   bank[4 + hd % 2][:, 0:T], ALU.mult, ALU.mult).then_inc(dn["onorm"], 1)
                if 0 <= hd - 1 < DNH:
                    dve.wait_ge(dn["onorm"], hd)
                    nc.vector.tensor_tensor(o_gate[:, hd - 1, :], o_raw[:, hd - 1, PAD:TP], o_gate[:, hd - 1, :],
                                            ALU.mult).then_inc(dn["ot"], 1)
                if hd >= 2:
                    dve.wait_ge(dn["ohi"], hd - 1)
                    nc.vector.tensor_tensor(o_lo[:, hd - 2, :], o_gate[:, hd - 2, :], o_hi[:, hd - 2, :].bitcast(F32),
                                            ALU.subtract).then_inc(dn["olo"], 1)
            out_dve(dve, "w_dn_out")

        def by_chunk(ap):
            return ap.rearrange("p (c t) -> p c t", c=NC)

        def x_slot(n):
            return x_st[:, n // DNH % 2 * 2 + n % 2, :]

        def half_of(ap, lv, which):
            b = 1 << lv
            if C % (2 * b):
                return ap[:, :, 0:b] if which == 0 else ap[:, :, b:min(2 * b, C)]
            return ap.rearrange("p c (n a b) -> p c n a b", a=2, b=b)[:, :, :, which, :]

        def lower(ap, lv):
            return half_of(ap, lv, 0)

        def upper(ap, lv):
            return half_of(ap, lv, 1)

        def dn_pool(pool):
            def step(d):
                pool.wait_ge(dn["a1"], d + 1)
                wait(pool, dn["at"], d)
                nc.gpsimd.tensor_tensor(by_chunk(at_2[:]), by_chunk(at_1[:]), tb("strict").unsqueeze(1).to_broadcast([C, NC, C]),
                                        ALU.mult).then_inc(dn["a2"], 1)

            step(0)
            with pool.Fori(1, DNH) as d:
                step(d)
            pool.wait_ge(chunk_used, chunk("w_dn", DNH - 1, 3) + 1)
            for n in range(DNH):
                pool.wait_ge(dn["at"], n + 1)
                if n >= 4:
                    pool.wait_ge(dn["d"], n - 3)
                nc.gpsimd.tensor_tensor(by_chunk(x_st[:, n % 4, :]), by_chunk(a_tr[:, n, :]),
                                        tb("pairs").unsqueeze(1).to_broadcast([C, NC, C]), ALU.mult).then_inc(dn["pair"], 1)
            for lv in range(1, LEVELS):
                pool.wait_ge(dn["d"], DNH)
                if lv >= 3:
                    pool.wait_ge(dn["dd"], (lv - 2) * DNH)
                half = lv % 2 * 2
                nc.gpsimd.memset(x_st[:, half:half + 2, :], 0.0).then_inc(dn["clear"], 1)

        def latent_pe(pe):
            c0, c1 = META, T
            for j in range(KT):
                if j >= 2:
                    pe.wait_ge(sq_ready, sq0["lat_q"] + j - 1)
                weights_here(pe, "w_latent", j // 4, j % 4)
                for k in range(KT):
                    if j == 0:
                        pe.wait_ge(x_ready, X_BASE["post3"] + k + 1)
                    mm = product(bank[j % 2][:, c0:c1], j % 4, k * P, x_op, k, (c0, c1), k == 0, k == KT - 1)
                mm.then_inc(chunk_used, 1)
                if j:
                    lat_sum(pe, j - 1)
            lat_sum(pe, KT - 1)
            small_pe(pe, "w_k_rope", bank[5][:, c0:c1], 64)
            pe.wait_ge(kr_seen, 1)
            nc.tensor.matmul(bank[5][0:64, c0:c1], tb("rot32"), kr_raw[:], start=True, stop=True).then_inc(kr_rot, 1)

        def lat_sum(pe, j):
            if j < QL:
                sum_tile(pe, "lat_q", j, QL, (META, T), where=7)
            else:
                sum_tile(pe, "lat_kv", j - QL, KVL, (META, T), where=6)

        z_lat = sem("z_lat")

        def latent_act(act, st):
            c0, c1 = META, T
            x_split_act(act, h, (c0, c1), X_BASE["post3"], (h_ready, 3 * KT))
            split = out_splits(act, split_hi, "w_latent")

            def tile(j):
                act.wait_ge(chunk_used, out_tile_done("w_latent", j))
                nc.scalar.activation(m[:, j, c0:c1], bank[j % 2][:, c0:c1], ACT.Copy).then_inc(z_lat, 1)
                name, jj = ("lat_q", j) if j < QL else ("lat_kv", j - QL)
                square(act, bank[j % 2][:, c0:c1], name, jj, (c0, c1))
                split(j)

            def high(j):
                act.wait_ge(lat_t, j + 1)
                nc.scalar.activation(lat_op[0][:, j, c0:c1], m[:, j, c0:c1], ACT.Copy).then_inc(lat_hi_ready, 1)

            for j in range(QL + 1):
                if j == QL - 1:
                    prime(act, "lat_q")
                tile(j)
            rms_root(act, "lat_q", QL * P, (c0, c1), root)
            tile(KT - 1)
            for j in range(QL):
                high(j)
            rms_root(act, "lat_kv", KVL * P, (c0, c1), root2, where=6)
            act.wait_ge(chunk_used, chunk("w_k_rope", 0, 3) + 1)
            nc.scalar.activation(kr_raw[:], bank[5][0:64, c0:c1], ACT.Copy).then_inc(kr_seen, 1)
            small_splits(act, split_hi, "w_k_rope")
            for j in range(QL, KT):
                high(j)

        def latent_dve(dve, st):
            c0, c1 = META, T
            split = out_splits(dve, split_lo, "w_latent")

            def scaled(j):
                gain, r = (pr("q_lat")[:, j:j + 1], rstd) if j < QL else (pr("kv_lat")[:, j - QL:j - QL + 1], rstd2)
                nc.vector.scalar_tensor_tensor(m[:, j, c0:c1], m[:, j, c0:c1], gain, r[:, c0:c1], ALU.mult,
                                               ALU.mult).then_inc(lat_t, 1)

            def low(j):
                dve.wait_ge(lat_hi_ready, j + 1)
                nc.vector.tensor_tensor(lat_op[1][:, j, c0:c1], m[:, j, c0:c1], lat_op[0][:, j, c0:c1].bitcast(F32),
                                        ALU.subtract).then_inc(lat_ready, 1)

            for j in range(QL + 1):
                split(j)
            invert_root(dve, st, "lat_q", (c0, c1), root, rstd)
            dve.wait_ge(z_lat, QL)
            for j in range(QL):
                scaled(j)
            split(KT - 1)
            for j in range(QL):
                low(j)
            invert_root(dve, st, "lat_kv", (c0, c1), root2, rstd2)
            dve.wait_ge(z_lat, KT)
            for j in range(QL, KT):
                scaled(j)
            small_splits(dve, split_lo, "w_k_rope")
            for j in range(QL, KT):
                low(j)
            dve.wait_ge(kr_seen, 1)
            st(nc.vector.tensor_tensor(kr_cos[:], kr_raw[:], tb("cos32"), ALU.mult))
            dve.wait_ge(kr_rot, 1)
            st(nc.vector.tensor_tensor(kr_sin[:], bank[5][0:64, c0:c1], tb("sin32"), ALU.mult))
            st.settle()
            nc.vector.tensor_tensor(k_rp[:, 0:SEQ], kr_cos[:], kr_sin[:], ALU.add).then_inc(kr_ready, 1)

        gains = {"pre0": pr("mix_pre")[:, 0:KT], "post0": pr("mix_post")[:, 0:KT],
                 "pre1": pr("ffn_pre")[:, 0:KT], "post1": pr("ffn_post")[:, 0:KT],
                 "pre2": pr("mix_pre")[:, KT:], "post2": pr("mix_post")[:, KT:],
                 "pre3": pr("ffn_pre")[:, KT:], "post3": pr("ffn_post")[:, KT:]}
        FULL, TAIL, LAST = (0, T), (META - CONV_PAST, T), (META, T)

        @block.tensor
        def _(pe):
            pe.wait_ge(s_in, 32)
            sums_pe(pe, "pre0", KT, FULL)
            pe.wait_ge(ones_ready, 3)
            small_pe(pe, "w_forget", bank[7][:, 0:T], 16)
            attention_pe(pe, 0)
            out_pe(pe, "w_attn_out", "post0", o_op, KT, FULL, lambda e, k: e.wait_ge(o_ready, k + 1))
            sums_pe(pe, "pre1", KT, FULL)
            ffn_pe(pe, 0)
            sums_pe(pe, "pre2", KT, FULL)
            pe.wait_ge(tables_in, 16)
            dn_pe(pe)
            sums_pe(pe, "pre3", KT, TAIL)
            ffn_pe(pe, 1)
            latent_pe(pe)
            attention_pe(pe, 1)
            out_pe(pe, "w_mla_out", None, o_op, KT, LAST, lambda e, k: e.wait_ge(o_ready, 8 + k + 1), mean=True)
            sums_pe(pe, "var1", KT, LAST)
            attention_pe(pe, 2)
            out_pe(pe, "w_moba_out", None, o_op, KT, LAST, lambda e, k: e.wait_ge(o_ready, 16 + k + 1), mean=True)
            sums_pe(pe, "var2", KT, LAST)

        @block.scalar
        def _(act):
            st = Steps(act, act_step)

            def constants_and_first_weight():
                act.wait_ge(s_in, 32)
                nc.scalar.activation(ones_r[:], ones, ACT.Copy).then_inc(ones_ready, 1)
                nc.scalar.activation(sum_gc_r[:], tb("sum_gc"), ACT.Copy).then_inc(ones_ready, 1)
                nc.scalar.activation(sum_beta_r[:], tb("sum_beta"), ACT.Copy).then_inc(ones_ready, 1)
                prime(act, "pre0")
                for q in range(4):
                    split_hi(act, "w_forget", 0, q)

            pre_norm_act(act, "pre0", FULL, None, constants_and_first_weight)
            small_splits(act, split_hi, "w_forget")
            act.wait_ge(chunk_used, chunk("w_forget", 0, 3) + 1)
            nc.scalar.activation(sp_c[0:16], bank[7][0:16, 0:T], ACT.Identity, bias=pr("b_forget")[0:16]).then_inc(z_known, 1)
            act.wait_ge(z_known, 1)
            st(nc.scalar.activation(sp_a[0:16], sp_c[0:16], ACT.Abs))
            st.settle()
            st(nc.scalar.activation(sp_b[0:16], sp_a[0:16], ACT.Exp, scale=-1.0))
            st.settle()
            nc.scalar.activation(sp_a[0:16], sp_b[0:16], ACT.Ln, bias=ones[0:16, 0:1]).then_inc(ln_done, 1)
            attention_act(act, st, 0)
            out_act(act, "w_attn_out", "post0", FULL)
            pre_norm_act(act, "pre1", FULL, 0)
            ffn_act(act, st, 0)
            pre_norm_act(act, "pre2", FULL, 8)
            dn_act(act, st)
            pre_norm_act(act, "pre3", TAIL, 16)
            ffn_act(act, st, 1)
            latent_act(act, st)
            attention_act(act, st, 1)
            ln_act(act, "w_mla_out", 1)
            attention_act(act, st, 2)
            ln_act(act, "w_moba_out", 2)

        @block.vector
        def _(dve):
            st = Steps(dve, dve_step)
            st(nc.vector.memset(one_row[:], 1.0))
            st(nc.vector.memset(rs[:], 1.0))
            st(nc.vector.memset(mx[:], 0.0))
            st.settle()
            dve.wait_ge(s_in, 32)
            for q in range(4):
                split_lo(dve, "w_forget", 0, q)
            pre_norm_dve(dve, st, "pre0", gains["pre0"], FULL)
            small_splits(dve, split_lo, "w_forget")
            attention_dve(dve, st, 0)
            out_dve(dve, "w_attn_out")
            dve.wait_ge(m_ready, KT)
            post_norm_dve(dve, st, "post0", gains["post0"], FULL)
            dve.wait_ge(h_ready, 8)
            pre_norm_dve(dve, st, "pre1", gains["pre1"], FULL)
            ffn_dve(dve, st, 0)
            dve.wait_ge(m_ready, 2 * KT)
            post_norm_dve(dve, st, "post1", gains["post1"], FULL)
            dve.wait_ge(h_ready, 16)
            pre_norm_dve(dve, st, "pre2", gains["pre2"], FULL)
            dn_dve(dve, st)
            dve.wait_ge(m_ready, 3 * KT)
            post_norm_dve(dve, st, "post2", gains["post2"], TAIL)
            dve.wait_ge(h_ready, 24)
            pre_norm_dve(dve, st, "pre3", gains["pre3"], TAIL)
            ffn_dve(dve, st, 1)
            dve.wait_ge(m_ready, 4 * KT)
            post_norm_dve(dve, st, "post3", gains["post3"], LAST)
            latent_dve(dve, st)
            st(nc.vector.memset(rs[:], 1.0))
            st(nc.vector.memset(mx[:], 0.0))
            st.settle()
            attention_dve(dve, st, 1)
            ln_dve(dve, st, "w_mla_out", 1)
            attention_dve(dve, st, 2)
            ln_dve(dve, st, "w_moba_out", 2)

        @block.gpsimd
        def _(pool):
            pool.wait_ge(rows_ready, 1)
            nc.gpsimd.tensor_tensor(rows_a[:, 2:16, :], c_2[:].unsqueeze(1).to_broadcast([P, 14, T]),
                                    tb("own_head_a")[:, 2:16].unsqueeze(2).to_broadcast([P, 14, T]),
                                    ALU.mult).then_inc(rows_ready, 1)
            ffn_pool(pool, 0)
            pool.wait_ge(chunk_used, chunk("w_down0", KT - 1, 3) + 1)
            nc.gpsimd.memset(bg[:], 0.0)
            nc.gpsimd.memset(g_pad[:], 0.0)
            nc.gpsimd.memset(q_st[:], 0.0)
            nc.gpsimd.memset(k_st[:], 0.0)
            nc.gpsimd.memset(v_st[:], 0.0).then_inc(dn["zero"], 1)
            dn_pool(pool)
            ffn_pool(pool, 1)


def lay_out(inp):
    f32 = np.float32

    def cols(wm, c0, n):
        b = wm[:, c0:c0 + n]
        return b.reshape(b.shape[0] // P, P, n).transpose(1, 0, 2).reshape(P, -1)

    def units(lists):
        return np.ascontiguousarray(np.stack([np.concatenate(x, 1) for x in lists])).astype(f32, copy=False)

    def outs(wm):
        return units([[cols(wm, (4 * u + q) * P, P) for q in range(4)] for u in range(2)])

    w = {}
    wa = inp["attn_w_in"][0]
    w["w_attn"] = units([[cols(wa, s * D + p * P, P) for s in range(4)] for p in range(PAIRS)])
    w["w_attn_out"] = outs(inp["attn_w_out"][0])
    wd = inp["dn_w_in"][0]
    w["w_dn"] = units([[cols(wd, s * D + p * P, P) for s in range(4)] for p in range(DNH)])
    w["w_dn_out"] = outs(inp["dn_w_out"][0])
    for f in range(2):
        up, down = inp["ffn_w_up"][f], inp["ffn_w_down"][f]
        w[f"w_up{f}"] = units([[cols(up, half * FFN + (2 * u + r) * P, P) for r in range(2) for half in range(2)]
                               for u in range(FT // 2)])
        w[f"w_down{f}"] = units([[cols(down, j * P, P)] for j in range(KT)])
    wm = inp["mla_w_in_2"][0]
    w["w_latent"] = outs(wm[:, 0:D])
    uq, ukv = inp["mla_w_uq_2"][0], inp["mla_w_ukv_2"][0]

    def gather(wm_, parts):
        return cols(np.concatenate([wm_[:, c:c + n] for c, n in parts], 1), 0, sum(n for _, n in parts))

    w["w_mla"] = units([[
        gather(uq, [((2 * p + i) * 96, 64) for i in range(2)]),
        gather(uq, [((2 * p + i) * 96 + 64, 32) for i in range(2)]), np.zeros((P, 64), f32),
        gather(ukv, [((2 * p + i) * 128, 64) for i in range(2)]),
        gather(ukv, [((2 * p + i) * 128 + 64, 64) for i in range(2)]),
        cols(wm, D + 32 + p * P, P)] for p in range(PAIRS)])
    w["w_mla_out"] = outs(inp["mla_w_o_2"][0])
    kv, wi = inp["moba_w_kv_2"], inp["moba_w_in_2"][0]
    w["w_moba"] = units([[cols(wi, p * P, P), cols(kv, p * P, P), cols(kv, D + p * P, P), cols(wi, D + p * P, P)]
                         for p in range(PAIRS)])
    w["w_moba_out"] = outs(inp["moba_w_o_2"][0])

    where, width = param_columns()
    par = np.zeros((P, width), f32)

    def put(name, a, r0=0):
        at, n = where[name]
        a = a.reshape(a.shape[0], -1)
        assert a.shape[1] == n, (name, a.shape, n)
        par[r0:r0 + a.shape[0], at:at + n] = a

    for name, src in (("mix_pre", "norm_mix_pre"), ("mix_post", "norm_mix_post"), ("ffn_pre", "norm_ffn_pre"),
                      ("ffn_post", "norm_ffn_post"), ("ln_g", "ln_g_2"), ("ln_b", "ln_b_2")):
        put(name, inp[src].reshape(2, KT, P).transpose(2, 0, 1))
    put("q_gain", np.tile(inp["attn_q_norm"][0], 2)[:, None])
    put("k_gain", np.tile(inp["attn_k_norm"][0], 2)[:, None])
    put("b_forget", inp["attn_b_forget"][0][:, None])
    put("a_log", inp["dn_a_log"][0][:, None], 32)
    put("dt_bias", inp["dn_dt_bias"][0][:, None], 32)
    put("o_gain", inp["dn_o_norm"][0][:, None])
    put("q_lat", inp["mla_q_norm_2"][0].reshape(QL, P).T)
    put("kv_lat", inp["mla_kv_norm_2"][0].reshape(KVL, P).T)
    put("dn_conv", inp["dn_conv"][0].reshape(4, 3, DNH, P).transpose(3, 2, 1, 0))
    put("ffn_conv", inp["ffn_conv"].reshape(2, 3, 2, FT, P).transpose(4, 0, 3, 2, 1))

    def small(wm_, n):
        c_ = cols(wm_, 0, n).reshape(P, 4, 2 * n)
        return np.ascontiguousarray(np.concatenate([c_, np.zeros((P, 4, P - n), f32)], 2).reshape(1, P, -1))

    w["w_forget"] = small(wa[:, 4 * D:4 * D + 16], 16)
    ba = np.zeros((D, 64), f32)
    ba[:, 0:8] = wd[:, 4 * D:4 * D + 8]
    ba[:, 32:40] = wd[:, 4 * D + 8:4 * D + 16]
    w["w_beta_a"] = small(ba, 64)
    kr = wm[:, D:D + 32]
    w["w_k_rope"] = small(np.concatenate([kr, kr], 1), 64)
    return w, par


def kernel(**inputs):
    import concourse.bacc as bacc
    from concourse.bass_utils import run_bass_kernel_spmd

    inp = {k: np.asarray(v) for k, v in inputs.items()}
    w, par = lay_out(inp)
    tw = table_columns()[1]
    table = np.zeros((P, tw), np.float32)
    for name, a in tables().items():
        rows, at, n = table_columns()[0][name]
        table[0:rows, at:at + n] = a
    x = np.concatenate([inp["meta_tokens"], inp["x"][0]], 0)
    arrays = {"x": np.ascontiguousarray(x.reshape(T, KT, P).transpose(2, 1, 0)), "table": table, "params": par, **w}
    nc = bacc.Bacc("TRN2", target_bir_lowering=False, num_devices=1)
    aps = {k: nc.dram_tensor(k, v.shape, F32, kind="ExternalInput").ap() for k, v in arrays.items()}
    out = nc.dram_tensor("out", (P, KT, SEQ), F32, kind="ExternalOutput").ap()
    build(nc, aps["x"], aps["table"], aps["params"], {k: aps[k] for k in w}, out)
    r = run_bass_kernel_spmd(nc, [arrays], core_ids=[0])
    got = r.results[0]["out"]
    return np.ascontiguousarray(got.transpose(2, 1, 0)).reshape(1, SEQ, D)
```
